# Optimizing a Trainium2 kernel written in Bass

```python
import math
import jax
import jax.numpy as jnp
from jax import lax
import numpy as np
import jax, jax.numpy as jnp

D_MODEL = 1024
BATCH = 1
SEQ = 256
DEPTH = 1

HEAD_DIM = 64
ROPE_THETA = 10000.0
NORM_EPS = 1e-6
NEG_INF = -1e30
FORCE_SCORE = 1e9

DIFF_HEADS = 4
DIFF_VDIM = 2 * HEAD_DIM
DIFF_Q_BLOCK = 128

NSA_HEADS = 8
NSA_KV_GROUPS = 2
NSA_HPG = NSA_HEADS // NSA_KV_GROUPS
CMP_LEN = 32
CMP_STRIDE = 16
CMP_HIDDEN = 4 * HEAD_DIM
SEL_LEN = 64
SEL_TOPK = 16
WINDOW = 512
NSA_Q_BLOCK = 64

D_FF = int(math.ceil(8 * D_MODEL / 3 / 256)) * 256

DIFF_QK = DIFF_HEADS * 2 * HEAD_DIM
DIFF_V = DIFF_HEADS * DIFF_VDIM
NSA_Q = NSA_HEADS * HEAD_DIM
NSA_KV = NSA_KV_GROUPS * HEAD_DIM
NSA_GATES = 3 * NSA_HEADS
MERGE_GATES = 2 * D_MODEL
IN_SPLITS = (DIFF_QK, DIFF_QK, DIFF_V, NSA_Q, NSA_KV, NSA_KV, NSA_KV, NSA_KV, NSA_KV, NSA_KV, NSA_GATES, MERGE_GATES)
IN_DIM = sum(IN_SPLITS)
A_WIDTH = DIFF_V
B_WIDTH = NSA_HEADS * HEAD_DIM


def lambda_init(layer):
    return 0.8 - 0.6 * math.exp(-0.3 * layer)

def rms_norm(x, g):
    xf = x.astype(jnp.float32)
    y = xf * lax.rsqrt(jnp.mean(xf * xf, axis=-1, keepdims=True) + NORM_EPS)
    return (y * g.astype(jnp.float32)).astype(x.dtype)

def rope_tables(positions, dim):
    inv_freq = 1.0 / (ROPE_THETA ** (jnp.arange(0, dim, 2, dtype=jnp.float32) / dim))
    ang = positions.astype(jnp.float32)[..., None] * inv_freq
    return jnp.cos(ang), jnp.sin(ang)

def apply_rope(x, cos, sin):
    half = x.shape[-1] // 2
    xf = x.astype(jnp.float32)
    x1, x2 = xf[..., :half], xf[..., half:]
    return jnp.concatenate([x1 * cos - x2 * sin, x2 * cos + x1 * sin], axis=-1).astype(x.dtype)

def differential_attention(q, k, v, lam):
    B, S, H, _, dh = q.shape
    nblk = S // DIFF_Q_BLOCK
    scale = dh ** -0.5
    kpos = jnp.arange(S)

    def one_block(i):
        s0 = i * DIFF_Q_BLOCK
        qb = lax.dynamic_slice_in_dim(q, s0, DIFF_Q_BLOCK, axis=1)
        s = jnp.einsum('bqhcd,bkhcd->bhcqk', qb, k).astype(jnp.float32) * scale
        qpos = s0 + jnp.arange(DIFF_Q_BLOCK)
        causal = kpos[None, :] <= qpos[:, None]
        p = jax.nn.softmax(jnp.where(causal, s, NEG_INF), axis=-1)
        a = p[:, :, 0] - lam * p[:, :, 1]
        return jnp.einsum('bhqk,bkhe->bqhe', a.astype(v.dtype), v)

    o = lax.map(one_block, jnp.arange(nblk))
    return o.transpose(1, 0, 2, 3, 4).reshape(B, S, H, v.shape[-1])

def compress(x, pe, w1, w2):
    B, S, G, dh = x.shape
    nc = (S - CMP_LEN) // CMP_STRIDE + 1
    idx = np.arange(nc)[:, None] * CMP_STRIDE + np.arange(CMP_LEN)[None, :]
    blk = x[:, idx] + pe[None, None, :, None, :]
    blk = blk.transpose(0, 1, 3, 2, 4).reshape(B, nc, G, CMP_LEN * dh)
    return jax.nn.silu(blk @ w1) @ w2

def nsa_attention(q, kc, vc, ks, vs, kw, vw):
    B, S, G, hpg, dh = q.shape
    nc = kc.shape[1]
    nsb = S // SEL_LEN
    topk = min(SEL_TOPK, nsb)
    nblk = S // NSA_Q_BLOCK
    scale = dh ** -0.5
    cmp_end = np.arange(nc) * CMP_STRIDE + CMP_LEN - 1
    ci = np.arange(nc)[:, None] * CMP_STRIDE
    sj = np.arange(nsb)[None, :] * SEL_LEN
    overlap = jnp.asarray(((ci < sj + SEL_LEN) & (ci + CMP_LEN > sj)).astype(np.float32))
    kb = ks.reshape(B, nsb, SEL_LEN, G, dh).transpose(0, 3, 1, 2, 4)
    vb = vs.reshape(B, nsb, SEL_LEN, G, dh).transpose(0, 3, 1, 2, 4)
    kw_pad = jnp.pad(kw, ((0, 0), (WINDOW, 0), (0, 0), (0, 0)))
    vw_pad = jnp.pad(vw, ((0, 0), (WINDOW, 0), (0, 0), (0, 0)))
    b_idx = jnp.arange(B)[:, None, None, None]
    g_idx = jnp.arange(G)[None, None, :, None]
    blk_ids = jnp.arange(nsb)
    sel_off = jnp.arange(SEL_LEN)

    def one_block(i):
        s0 = i * NSA_Q_BLOCK
        qpos = s0 + jnp.arange(NSA_Q_BLOCK)
        qb = lax.dynamic_slice_in_dim(q, s0, NSA_Q_BLOCK, axis=1)
        sc = jnp.einsum('bqghd,bcgd->bqghc', qb, kc).astype(jnp.float32) * scale
        cm = (cmp_end[None, :] <= qpos[:, None])[None, :, None, None, :]
        pc = jax.nn.softmax(jnp.where(cm, sc, NEG_INF), axis=-1) * cm
        o_c = jnp.einsum('bqghc,bcgd->bqghd', pc.astype(vc.dtype), vc)
        imp = jnp.einsum('bqgc,cn->bqgn', pc.sum(axis=3), overlap)
        qblk = qpos // SEL_LEN
        forced = (blk_ids[None, :] == 0) | (blk_ids[None, :] == qblk[:, None]) | (blk_ids[None, :] == qblk[:, None] - 1)
        causal_blk = blk_ids[None, :] <= qblk[:, None]
        imp = jnp.where(forced[None, :, None, :], FORCE_SCORE, imp)
        imp = jnp.where(causal_blk[None, :, None, :], imp, NEG_INF)
        _, idx = lax.top_k(imp, topk)
        ksel = kb[b_idx, g_idx, idx]
        vsel = vb[b_idx, g_idx, idx]
        ss = jnp.einsum('bqghd,bqgnld->bqghnl', qb, ksel).astype(jnp.float32) * scale
        kp = idx[..., None] * SEL_LEN + sel_off
        smask = (kp <= qpos[None, :, None, None, None])[:, :, :, None]
        ss = jnp.where(smask, ss, NEG_INF).reshape(B, NSA_Q_BLOCK, G, hpg, topk * SEL_LEN)
        ps = jax.nn.softmax(ss, axis=-1).reshape(B, NSA_Q_BLOCK, G, hpg, topk, SEL_LEN)
        o_s = jnp.einsum('bqghnl,bqgnld->bqghd', ps.astype(vsel.dtype), vsel)
        kwb = lax.dynamic_slice_in_dim(kw_pad, s0, NSA_Q_BLOCK + WINDOW, axis=1)
        vwb = lax.dynamic_slice_in_dim(vw_pad, s0, NSA_Q_BLOCK + WINDOW, axis=1)
        kpos = s0 - WINDOW + jnp.arange(NSA_Q_BLOCK + WINDOW)
        dist = qpos[:, None] - kpos[None, :]
        wmask = ((dist >= 0) & (dist < WINDOW) & (kpos[None, :] >= 0))[None, :, None, None, :]
        sw = jnp.einsum('bqghd,bkgd->bqghk', qb, kwb).astype(jnp.float32) * scale
        pw = jax.nn.softmax(jnp.where(wmask, sw, NEG_INF), axis=-1)
        o_w = jnp.einsum('bqghk,bkgd->bqghd', pw.astype(vwb.dtype), vwb)
        return o_c, o_s, o_w

    o_c, o_s, o_w = lax.map(one_block, jnp.arange(nblk))

    def to_seq(o):
        return o.transpose(1, 0, 2, 3, 4, 5).reshape(B, S, G * hpg, dh)

    return to_seq(o_c), to_seq(o_s), to_seq(o_w)

def hybrid_mixer(u, cos, sin, layer, w_in, diff_lambda, diff_subln_g, cmp_pe_k, cmp_pe_v,
                 cmp_k_w1, cmp_k_w2, cmp_v_w1, cmp_v_w2, w_branch_a, w_branch_b, w_out):
    B, S, _ = u.shape
    G, dh = NSA_KV_GROUPS, HEAD_DIM
    split_at = np.cumsum(IN_SPLITS)[:-1].tolist()
    (dq, dk, dv, nq, kc_, vc_, ks_, vs_, kw_, vw_, ngate, mgate) = jnp.split(u @ w_in, split_at, axis=-1)
    c4, s4 = cos[:, :, None, None, :], sin[:, :, None, None, :]
    c3, s3 = cos[:, :, None, :], sin[:, :, None, :]
    dq = apply_rope(dq.reshape(B, S, DIFF_HEADS, 2, dh), c4, s4)
    dk = apply_rope(dk.reshape(B, S, DIFF_HEADS, 2, dh), c4, s4)
    dv = dv.reshape(B, S, DIFF_HEADS, DIFF_VDIM)
    lam_init = lambda_init(layer)
    lf = diff_lambda.astype(jnp.float32)
    lam = jnp.exp(jnp.sum(lf[0] * lf[1])) - jnp.exp(jnp.sum(lf[2] * lf[3])) + lam_init
    y_a = differential_attention(dq, dk, dv, lam)
    y_a = rms_norm(y_a, diff_subln_g) * (1.0 - lam_init)
    y_a = y_a.reshape(B, S, A_WIDTH) @ w_branch_a
    nq = apply_rope(nq.reshape(B, S, NSA_HEADS, dh), c3, s3).reshape(B, S, G, NSA_HPG, dh)

    def kv(t):
        return t.reshape(B, S, G, dh)

    k_cmp = compress(apply_rope(kv(kc_), c3, s3), cmp_pe_k, cmp_k_w1, cmp_k_w2)
    v_cmp = compress(kv(vc_), cmp_pe_v, cmp_v_w1, cmp_v_w2)
    k_sel = apply_rope(kv(ks_), c3, s3)
    k_win = apply_rope(kv(kw_), c3, s3)
    o_c, o_s, o_w = nsa_attention(nq, k_cmp, v_cmp, k_sel, kv(vs_), k_win, kv(vw_))
    g = jax.nn.sigmoid(ngate.astype(jnp.float32)).reshape(B, S, 3, NSA_HEADS, 1).astype(u.dtype)
    y_b = g[:, :, 0] * o_c + g[:, :, 1] * o_s + g[:, :, 2] * o_w
    y_b = y_b.reshape(B, S, B_WIDTH) @ w_branch_b
    mg = jax.nn.sigmoid(mgate.astype(jnp.float32)).reshape(B, S, 2, D_MODEL).astype(u.dtype)
    return (mg[:, :, 0] * y_a + mg[:, :, 1] * y_b) @ w_out

def swiglu(u, w_gate, w_up, w_down):
    return (jax.nn.silu(u @ w_gate) * (u @ w_up)) @ w_down

def first_inputs(seed: int = 0) -> dict:
    key = jax.random.key(seed)
    ks = jax.random.split(key, 22)

    def nrm(k, shape, scale):
        return jax.random.normal(k, shape, jnp.float32) * scale

    return {
        "x": nrm(ks[0], (BATCH, SEQ, D_MODEL), 1.0),
        "positions": jnp.tile(jnp.arange(SEQ, dtype=jnp.int32)[None, :], (BATCH, 1)),
        "attn_norm_g": 1.0 + nrm(ks[1], (DEPTH, D_MODEL), 0.02),
        "w_in": nrm(ks[2], (DEPTH, D_MODEL, IN_DIM), D_MODEL ** -0.5),
        "diff_lambda": nrm(ks[3], (DEPTH, 4, HEAD_DIM), 0.1),
        "diff_subln_g": 1.0 + nrm(ks[4], (DEPTH, DIFF_VDIM), 0.02),
        "cmp_pe_k": nrm(ks[5], (DEPTH, CMP_LEN, HEAD_DIM), 0.1),
        "cmp_pe_v": nrm(ks[6], (DEPTH, CMP_LEN, HEAD_DIM), 0.1),
        "cmp_k_w1": nrm(ks[7], (DEPTH, CMP_LEN * HEAD_DIM, CMP_HIDDEN), (CMP_LEN * HEAD_DIM) ** -0.5),
        "cmp_k_w2": nrm(ks[8], (DEPTH, CMP_HIDDEN, HEAD_DIM), CMP_HIDDEN ** -0.5),
        "cmp_v_w1": nrm(ks[9], (DEPTH, CMP_LEN * HEAD_DIM, CMP_HIDDEN), (CMP_LEN * HEAD_DIM) ** -0.5),
        "cmp_v_w2": nrm(ks[10], (DEPTH, CMP_HIDDEN, HEAD_DIM), CMP_HIDDEN ** -0.5),
        "w_branch_a": nrm(ks[11], (DEPTH, A_WIDTH, D_MODEL), A_WIDTH ** -0.5),
        "w_branch_b": nrm(ks[12], (DEPTH, B_WIDTH, D_MODEL), B_WIDTH ** -0.5),
        "w_out": nrm(ks[13], (DEPTH, D_MODEL, D_MODEL), D_MODEL ** -0.5),
        "ffn_norm_g": 1.0 + nrm(ks[14], (DEPTH, D_MODEL), 0.02),
        "w_gate": nrm(ks[15], (DEPTH, D_MODEL, D_FF), D_MODEL ** -0.5),
        "w_up": nrm(ks[16], (DEPTH, D_MODEL, D_FF), D_MODEL ** -0.5),
        "w_down": nrm(ks[17], (DEPTH, D_FF, D_MODEL), D_FF ** -0.5),
        "final_norm_g": 1.0 + nrm(ks[18], (D_MODEL,), 0.02),
    }

def first_block(x, positions, attn_norm_g, w_in, diff_lambda, diff_subln_g, cmp_pe_k, cmp_pe_v,
              cmp_k_w1, cmp_k_w2, cmp_v_w1, cmp_v_w2, w_branch_a, w_branch_b, w_out,
              ffn_norm_g, w_gate, w_up, w_down, final_norm_g):
    cos, sin = rope_tables(positions, HEAD_DIM)
    h = x
    for layer in range(DEPTH):
        u = rms_norm(h, attn_norm_g[layer])
        h = h + hybrid_mixer(u, cos, sin, layer, w_in[layer], diff_lambda[layer], diff_subln_g[layer],
                             cmp_pe_k[layer], cmp_pe_v[layer], cmp_k_w1[layer], cmp_k_w2[layer],
                             cmp_v_w1[layer], cmp_v_w2[layer], w_branch_a[layer], w_branch_b[layer],
                             w_out[layer])
        u = rms_norm(h, ffn_norm_g[layer])
        h = h + swiglu(u, w_gate[layer], w_up[layer], w_down[layer])
    return rms_norm(h, final_norm_g)


D_MIX = D_MODEL
D_MLSTM = D_MIX // 2
D_POOL = D_MIX - D_MLSTM
N_MLSTM_HEADS = 4
HEAD_DIM_2 = D_MLSTM // N_MLSTM_HEADS
POOL_WINDOWS = (2, 4, 8, 16)
N_POOL_GROUPS = len(POOL_WINDOWS)
POOL_GROUP_DIM = D_POOL // N_POOL_GROUPS
N_DIRS = 2
N_GATE_COLS = N_DIRS * 2 * N_MLSTM_HEADS
D_IN_PROJ = 4 * D_MLSTM + N_GATE_COLS + D_POOL
D_FF_2 = 4 * D_MODEL
CHUNK = 128
EPS = 1e-6


def _rmsnorm(x, g):
    xf = x.astype(jnp.float32)
    y = xf * lax.rsqrt(jnp.mean(xf * xf, axis=-1, keepdims=True) + EPS)
    return (y * g.astype(jnp.float32)).astype(x.dtype)

def _modulate(h, shift, scale):
    return h * (1 + scale[:, None, :]) + shift[:, None, :]

def _mlstm_scan(q, k, v, log_i, log_f):
    B, H, S, Dh = q.shape
    nc = S // CHUNK

    def to_chunks(a):
        a = a.reshape((B, H, nc, CHUNK) + a.shape[3:])
        return jnp.moveaxis(a, 2, 0)

    xs = (to_chunks(q), to_chunks(k), to_chunks(v), to_chunks(log_f), to_chunks(log_i))
    tril = jnp.tril(jnp.ones((CHUNK, CHUNK), dtype=bool))

    def step(carry, inp):
        C, n, m = carry
        q_c, k_c, v_c, lf, li = inp
        b = jnp.cumsum(lf, axis=-1)
        d = b[..., :, None] - b[..., None, :] + li[..., None, :]
        d = jnp.where(tril, d, -jnp.inf)
        inter = b + m[..., None]
        m_t = jnp.maximum(inter, jnp.max(d, axis=-1))
        w = jnp.exp(d - m_t[..., None])
        a = jnp.exp(inter - m_t)
        s = jnp.einsum('bhtd,bhsd->bhts', q_c, k_c) * w
        num = (jnp.einsum('bhts,bhse->bhte', s, v_c)
               + a[..., None] * jnp.einsum('bhtd,bhde->bhte', q_c, C))
        den = jnp.sum(s, axis=-1) + a * jnp.einsum('bhtd,bhd->bht', q_c, n)
        h = num / jnp.maximum(jnp.abs(den), jnp.exp(-m_t))[..., None]
        b_last = b[..., -1]
        g = b_last[..., None] - b + li
        m_new = jnp.maximum(b_last + m, jnp.max(g, axis=-1))
        decay = jnp.exp(b_last + m - m_new)
        wk = jnp.exp(g - m_new[..., None])
        C_new = decay[..., None, None] * C + jnp.einsum('bhs,bhsd,bhse->bhde', wk, k_c, v_c)
        n_new = decay[..., None] * n + jnp.einsum('bhs,bhsd->bhd', wk, k_c)
        return (C_new, n_new, m_new), h

    init = (jnp.zeros((B, H, Dh, Dh), jnp.float32),
            jnp.zeros((B, H, Dh), jnp.float32),
            jnp.zeros((B, H), jnp.float32))
    _, hs = lax.scan(step, init, xs)
    return jnp.moveaxis(hs, 0, 2).reshape(B, H, S, Dh)

def _multiscale_pool(u, w_pool, pool_scale):
    B, S, _ = u.shape
    uf = u.astype(jnp.float32).reshape(B, S, N_POOL_GROUPS, POOL_GROUP_DIM)
    prefix = jnp.concatenate([jnp.zeros_like(uf[:, :1]), jnp.cumsum(uf, axis=1)], axis=1)
    t = jnp.arange(S)
    means = []
    for gi, win in enumerate(POOL_WINDOWS):
        lo = jnp.clip(t - win // 2, 0, S)
        hi = jnp.clip(t + win // 2, 0, S)
        p = prefix[:, :, gi]
        cnt = (hi - lo).astype(jnp.float32)
        means.append((p[:, hi] - p[:, lo]) / cnt[None, :, None])
    pooled = jnp.stack(means, axis=2)
    mixed = (pooled - uf).astype(u.dtype)
    y = jnp.einsum('bsgc,gce->bsge', mixed, w_pool).reshape(B, S, D_POOL)
    return y * pool_scale

def _mixer(h, w_in, b_igate, b_fgate, g_head, w_pool, pool_scale, w_out):
    B, S, _ = h.shape
    H = N_MLSTM_HEADS
    proj = jnp.einsum('bsd,dp->bsp', h, w_in)
    cuts = [D_MLSTM, 2 * D_MLSTM, 3 * D_MLSTM, 4 * D_MLSTM, 4 * D_MLSTM + N_GATE_COLS]
    q, k, v, o, gates, u = jnp.split(proj, cuts, axis=-1)

    def heads(a):
        return a.reshape(B, S, H, HEAD_DIM_2).transpose(0, 2, 1, 3).astype(jnp.float32)

    qh = heads(q) * (HEAD_DIM_2 ** -0.5)
    kh = heads(k)
    vh = heads(v)
    gates = gates.astype(jnp.float32).reshape(B, S, N_DIRS, 2, H).transpose(2, 3, 0, 4, 1)
    log_i = gates[:, 0] + b_igate.astype(jnp.float32)[:, None, :, None]
    log_f = jax.nn.log_sigmoid(gates[:, 1] + b_fgate.astype(jnp.float32)[:, None, :, None])

    def flip(a):
        return jnp.flip(a, axis=2)

    h_fwd = _mlstm_scan(qh, kh, vh, log_i[0], log_f[0])
    h_bwd = flip(_mlstm_scan(flip(qh), flip(kh), flip(vh), flip(log_i[1]), flip(log_f[1])))
    hm = h_fwd + h_bwd
    hm = hm * lax.rsqrt(jnp.mean(hm * hm, axis=-1, keepdims=True) + EPS)
    hm = hm * g_head.astype(jnp.float32).reshape(H, 1, HEAD_DIM_2)
    hm = hm.transpose(0, 2, 1, 3).reshape(B, S, D_MLSTM)
    y_a = (jax.nn.sigmoid(o.astype(jnp.float32)) * hm).astype(h.dtype)

    y_b = _multiscale_pool(u, w_pool, pool_scale)
    y = jnp.concatenate([y_a, y_b], axis=-1)
    return jnp.einsum('bsm,md->bsd', y, w_out)

def second_inputs(seed: int = 0) -> dict:
    key = jax.random.key(seed)
    ks = jax.random.split(key, 17)
    f32 = jnp.float32
    H = N_MLSTM_HEADS

    def nrm(k, shape, scale):
        return jax.random.normal(k, shape, f32) * scale

    x = nrm(ks[0], (BATCH, SEQ, D_MODEL), 1.0)
    c = nrm(ks[1], (BATCH, D_MODEL), 1.0)
    w_ada = nrm(ks[2], (DEPTH, D_MODEL, 6 * D_MODEL), D_MODEL ** -0.5)
    b_ada = nrm(ks[3], (DEPTH, 6 * D_MODEL), 0.02)
    g_mix = 1.0 + nrm(ks[4], (DEPTH, D_MODEL), 0.05)
    w_in = nrm(ks[5], (DEPTH, D_MODEL, D_IN_PROJ), D_MODEL ** -0.5)
    b_igate = nrm(ks[6], (DEPTH, N_DIRS, H), 0.1)
    b_fgate = (jnp.broadcast_to(jnp.linspace(3.0, 6.0, H, dtype=f32), (DEPTH, N_DIRS, H))
               + nrm(ks[7], (DEPTH, N_DIRS, H), 0.1))
    g_head = 1.0 + nrm(ks[8], (DEPTH, D_MLSTM), 0.05)
    w_pool = nrm(ks[9], (DEPTH, N_POOL_GROUPS, POOL_GROUP_DIM, POOL_GROUP_DIM), POOL_GROUP_DIM ** -0.5)
    pool_scale = 1.0 + nrm(ks[10], (DEPTH, D_POOL), 0.1)
    w_out = nrm(ks[11], (DEPTH, D_MIX, D_MODEL), D_MIX ** -0.5)
    g_ffn = 1.0 + nrm(ks[12], (DEPTH, D_MODEL), 0.05)
    w_ff1 = nrm(ks[13], (DEPTH, D_MODEL, D_FF_2), D_MODEL ** -0.5)
    w_ff2 = nrm(ks[14], (DEPTH, D_FF_2, D_MODEL), D_FF_2 ** -0.5)
    g_final = 1.0 + nrm(ks[15], (D_MODEL,), 0.05)
    return {"x": x, "c": c, "w_ada": w_ada, "b_ada": b_ada, "g_mix": g_mix, "w_in": w_in,
            "b_igate": b_igate, "b_fgate": b_fgate, "g_head": g_head, "w_pool": w_pool,
            "pool_scale": pool_scale, "w_out": w_out, "g_ffn": g_ffn, "w_ff1": w_ff1,
            "w_ff2": w_ff2, "g_final": g_final}

def second_block(x, c, w_ada, b_ada, g_mix, w_in, b_igate, b_fgate, g_head, w_pool,
              pool_scale, w_out, g_ffn, w_ff1, w_ff2, g_final):
    c_act = jax.nn.silu(c)
    for l in range(DEPTH):
        mod = c_act @ w_ada[l] + b_ada[l]
        sh1, sc1, gt1, sh2, sc2, gt2 = jnp.split(mod, 6, axis=-1)
        h = _modulate(_rmsnorm(x, g_mix[l]), sh1, sc1)
        x = x + gt1[:, None, :] * _mixer(h, w_in[l], b_igate[l], b_fgate[l], g_head[l],
                                         w_pool[l], pool_scale[l], w_out[l])
        h = _modulate(_rmsnorm(x, g_ffn[l]), sh2, sc2)
        a = jnp.square(jax.nn.relu(jnp.einsum('bsd,df->bsf', h, w_ff1[l])))
        x = x + gt2[:, None, :] * jnp.einsum('bsf,fd->bsd', a, w_ff2[l])
    return _rmsnorm(x, g_final)


def setup_inputs(seed=0):
    out = dict(first_inputs(seed))
    for name, value in second_inputs(seed + 1).items():
        if name != "x":
            out[name + "_2"] = value
    return out


def reference(
    x, positions, attn_norm_g, w_in, diff_lambda, diff_subln_g, cmp_pe_k, cmp_pe_v, cmp_k_w1,
    cmp_k_w2, cmp_v_w1, cmp_v_w2, w_branch_a, w_branch_b, w_out, ffn_norm_g, w_gate, w_up,
    w_down, final_norm_g, c_2, w_ada_2, b_ada_2, g_mix_2, w_in_2, b_igate_2, b_fgate_2,
    g_head_2, w_pool_2, pool_scale_2, w_out_2, g_ffn_2, w_ff1_2, w_ff2_2, g_final_2,
):
    x = first_block(
        x, positions, attn_norm_g, w_in, diff_lambda, diff_subln_g, cmp_pe_k, cmp_pe_v,
        cmp_k_w1, cmp_k_w2, cmp_v_w1, cmp_v_w2, w_branch_a, w_branch_b, w_out, ffn_norm_g,
        w_gate, w_up, w_down, final_norm_g,
    )
    return second_block(
        x, c_2, w_ada_2, b_ada_2, g_mix_2, w_in_2, b_igate_2, b_fgate_2, g_head_2, w_pool_2,
        pool_scale_2, w_out_2, g_ffn_2, w_ff1_2, w_ff2_2, g_final_2,
    )


_drawn_inputs = setup_inputs


def setup_inputs(seed=0):
    import zlib

    import numpy as np

    out = dict(_drawn_inputs(seed))
    spreads = {}
    factors = {'attn_norm_g': 2.727,
     'diff_lambda': 8.0,
     'diff_subln_g': 4.702,
     'cmp_pe_k': 8.0,
     'cmp_pe_v': 2.91,
     'ffn_norm_g': 3.556,
     'b_igate_2': 8.0,
     'g_head_2': 5.094}
    for name, (base, spread) in spreads.items():
        noise = np.random.default_rng([zlib.crc32(name.encode()), seed]).standard_normal(out[name].shape)
        drawn = base * np.exp(spread * noise) if base else spread * noise
        out[name] = jnp.asarray(drawn.astype(out[name].dtype))
    for name, factor in factors.items():
        out[name] = (out[name] * factor).astype(out[name].dtype)
    return out
```

```python
from contextlib import ExitStack

import concourse.bass as bass
from concourse import mybir

F32 = mybir.dt.float32
F32R = mybir.dt.float32r
I32 = mybir.dt.int32
ACT = mybir.ActivationFunctionType
ALU = mybir.AluOpType
AX = mybir.AxisListType

P = 128
BANK = 512
SLAB = 2048
RAW_SLABS = 5
UNIT = 1024
SPLIT_UNITS = 4
AHEAD = 3
MASKED = -1e30
NORM_EPS = 1e-6
TWO_PI_PARTS = (6.28125, 0.0019350051879882812, 3.019916050e-07)
MAGIC = 12582912.0
PI_BELOW = 3.1415925


class Lane:

    def __init__(self, engine, semaphore):
        self.engine, self.semaphore = engine, semaphore
        self.count, self.reached = 0, {}

    def mark(self, instruction):
        self.count += 1
        instruction.then_inc(self.semaphore, 1)
        return (self.semaphore, self.count)

    def wait(self, *marks):
        for m in marks:
            if m is None:
                continue
            if isinstance(m, list):
                self.wait(*m)
            elif self.reached.get(id(m[0]), 0) < m[1]:
                self.engine.wait_ge(m[0], m[1])
                self.reached[id(m[0])] = m[1]


class Bank:

    def __init__(self, tensor):
        self.ap, self.readers = tensor, []


class Weights:

    def __init__(self, nc, sp, act, dve, raw, slot_sems, high, low):
        self.nc, self.sp, self.act, self.dve = nc, sp, act, dve
        self.raw, self.slot_sems, self.high, self.low = raw, slot_sems, high, low
        self.slabs, self.units, self.chunks = [], [], {}
        self.issued = self.prepared = 0

    def plan_slab(self, src, kn, n):
        i = len(self.slabs)
        self.slabs.append({"src": src, "kn": kn, "n": n, "released": None, "slot": i % RAW_SLABS,
                           "landed": (self.slot_sems[i % RAW_SLABS], 16 * (i // RAW_SLABS + 1))})
        return i

    def plan_split(self, name, w, c0, n):
        rows = w.shape[0] // P
        units = []
        for k0 in range(0, rows, 4):
            kn = min(4, rows - k0)
            src = w[k0 * P:(k0 + kn) * P, c0:c0 + n].rearrange("(k p) n -> p k n", p=P)
            i = self.plan_slab(src, kn, n)
            for k in range(0, kn, 2):
                units.append({"slab": i, "at": k, "kn": min(2, kn - k), "n": n, "k0": k0 + k,
                              "last": k + 2 >= kn, "used": None, "index": len(self.units)})
                self.units.append(units[-1])
        self.chunks[name] = units

    def plan_raw(self, name, sources):
        self.chunks[name] = [self.plan_slab(src, src.shape[1], src.shape[2]) for src in sources]

    def slab_view(self, i):
        s = self.slabs[i]
        return self.raw[:, s["slot"], 0:s["kn"] * s["n"]].rearrange("p (k n) -> p k n", k=s["kn"])

    def release(self, i, *marks):
        self.slabs[i]["released"] = list(marks)
        self.pump()

    def pump(self):
        while self.issued < len(self.slabs):
            s = self.slabs[self.issued]
            if self.issued >= RAW_SLABS:
                before = self.slabs[self.issued - RAW_SLABS]
                if before["released"] is None:
                    return
                self.sp.wait(before["released"])
            self.sp.engine.dma_start(self.slab_view(self.issued), s["src"]).then_inc(s["landed"][0], 16)
            self.issued += 1

    def prepare_through(self, last):
        while self.prepared <= min(last, len(self.units) - 1):
            u = self.units[self.prepared]
            slab = self.slabs[u["slab"]]
            if u["slab"] >= self.issued:
                return
            src = self.slab_view(u["slab"])[:, u["at"]:u["at"] + u["kn"], :]
            ring, size = self.prepared % SPLIT_UNITS, u["kn"] * u["n"]
            high = self.high[:, ring, 0:size].rearrange("p (k n) -> p k n", k=u["kn"])
            low = self.low[:, ring, 0:size].rearrange("p (k n) -> p k n", k=u["kn"])
            used = self.units[self.prepared - SPLIT_UNITS]["used"] if self.prepared >= SPLIT_UNITS else None
            self.act.wait(slab["landed"], used)
            u["high_ready"] = self.act.mark(self.act.engine.activation(high, src, ACT.Copy))
            self.dve.wait(slab["landed"], u["high_ready"], used)
            u["low_ready"] = self.dve.mark(
                self.dve.engine.tensor_tensor(low, src, high.bitcast(F32), ALU.subtract))
            u["high"], u["low"] = high, low
            self.prepared += 1
            if u["last"]:
                self.release(u["slab"], u["low_ready"])


def build(nc, io, out, debug=None):
    x_in = io["x"]
    T, D = x_in.shape[1], x_in.shape[2]
    NT = T // P
    KD = D // P
    w_in = io["w_in"][0]
    DH = io["diff_lambda"].shape[2]
    HALF = DH // 2
    DIFF_W = io["w_branch_a"].shape[1]
    DIFF_H = DIFF_W // (2 * DH)
    NSA_W = io["w_branch_b"].shape[1]
    NSA_H = NSA_W // DH
    G = 2
    HPG = NSA_H // G
    KV = G * DH
    N_GATES = 3 * NSA_H
    CMP_LEN, CMP_STRIDE = io["cmp_pe_k"].shape[1], 16
    NC = (T - CMP_LEN) // CMP_STRIDE + 1
    HID = io["cmp_k_w1"].shape[2]
    KH = HID // P
    CMP_J = CMP_LEN * DH // P
    CPAD = 32
    assert CPAD >= NC and CMP_LEN == 2 * CMP_STRIDE and HPG * CPAD == P and 2 * DH == P
    DFF = io["w_gate"].shape[2]
    DFF2 = io["w_ff1_2"].shape[2]
    KF, KF2 = DFF // P, DFF2 // P
    w_in2 = io["w_in_2"][0]
    H2 = io["b_igate_2"].shape[2]
    MW = io["g_head_2"].shape[1]
    E2 = MW // H2
    NG2 = 4 * H2
    PG = io["w_pool_2"].shape[1]
    LAM_INIT = 0.8 - 0.6
    assert NT == 2 and E2 == P and DIFF_H * P == DIFF_W

    O_DQ, O_DK, O_DV, O_NQ = 0, DIFF_W, 2 * DIFF_W, 3 * DIFF_W
    O_KC = O_NQ + NSA_W
    O_VC, O_KS, O_VS, O_KW, O_VW, O_NG = (O_KC + i * KV for i in range(1, 7))
    O_MG = O_NG + N_GATES

    with ExitStack() as ctx:
        def sb(name, shape, dtype=F32, stack=ctx):
            return stack.enter_context(nc.sbuf_tensor(name, shape, dtype))

        def sem(name):
            return ctx.enter_context(nc.semaphore(name))

        pe = Lane(nc.tensor, sem("tensor_done"))
        act = Lane(nc.scalar, sem("scalar_done"))
        dve = Lane(nc.vector, sem("vector_done"))
        pool = Lane(nc.gpsimd, sem("gpsimd_done"))
        sp = Lane(nc.sync, None)
        banks = [Bank(ctx.enter_context(nc.psum_tensor(f"bank{i}", [P, BANK], F32))) for i in range(8)]
        acc, tr_banks, aux_banks = banks[0:4], banks[4:6], banks[6:8]

        raw = sb("raw_weights", [P, RAW_SLABS, SLAB])
        high = sb("weights_high", [P, SPLIT_UNITS, UNIT], F32R)
        low = sb("weights_low", [P, SPLIT_UNITS, UNIT], F32R)
        x = sb("x", [P, NT, D])
        xn = sb("xn", [P, NT, D])
        uT_h = sb("uT_high", [P, KD, T], F32R)
        uT_l = sb("uT_low", [P, KD, T], F32R)
        row_a = sb("row_a", [P, D])
        row_b = sb("row_b", [P, D])
        row_c = sb("row_c", [P, D])
        row_d = sb("row_d", [P, D])
        consts = io["consts"]
        cst = sb("constants", [P, consts.shape[1]])
        ident = cst[:, 0:P]
        inv_freq = cst[:, 3 * P:3 * P + HALF]
        o_c = 3 * P + HALF
        cmp_add = cst[:, o_c:o_c + NT * NC].rearrange("p (t c) -> p t c", t=NT)
        cmp_keep = cst[:, o_c + NT * NC:o_c + 2 * NT * NC].rearrange("p (t c) -> p t c", t=NT)
        ident_r = sb("identity_r", [P, P], F32R)
        after_r = sb("mask_free_after_partition", [P, P], F32R)
        before_r = sb("mask_free_before_partition", [P, P], F32R)
        ones = sb("ones", [P, P])
        minus_half = sb("minus_half", [P, 4])
        b_ada = sb("b_ada", [12, BANK])
        ada_acc = sb("ada_acc", [P, BANK])
        vec_rows = sb("vector_rows", [64, P])
        vec_cols = sb("vector_columns", [P, 64])
        c_act = sb("c_act", [P, KD])
        stat = sb("stat", [P, 64])
        small = sb("small", [P, 64])

        slot_sems = [sem(f"raw_slot{i}_landed") for i in range(RAW_SLABS)]
        W = Weights(nc, sp, act, dve, raw, slot_sems, high, low)

        for name, c0, n in (("dq", O_DQ, DIFF_W), ("dk", O_DK, DIFF_W), ("dv", O_DV, DIFF_W),
                            ("nq", O_NQ, NSA_W), ("kva", O_KC, 3 * KV), ("kvb", O_VS, 3 * KV + N_GATES)):
            W.plan_split(name, w_in, c0, n)
        W.plan_split("mg0", w_in, O_MG, BANK)
        for name in ("k", "v"):
            w1 = io[f"cmp_{name}_w1"][0].rearrange("(j p) n -> p j n", p=P)
            W.plan_raw(f"cmp_{name}", [w1[:, 0:CMP_J // 2, :], w1[:, CMP_J // 2:CMP_J, :]])
        for i in range(1, 4):
            W.plan_split(f"mg{i}", w_in, O_MG + i * BANK, BANK)
        for i in range(2):
            W.plan_split(f"branch_a{i}", io["w_branch_a"][0], i * BANK, BANK)
            W.plan_split(f"branch_b{i}", io["w_branch_b"][0], i * BANK, BANK)
        for i in range(2):
            W.plan_split(f"w_out{i}", io["w_out"][0], i * BANK, BANK)

        def plan_ada(i):
            w = io["w_ada_2"][0][:, i * BANK:(i + 1) * BANK].rearrange("(k p) n -> p k n", p=P)
            W.plan_raw(f"ada{i}", [w[:, k:k + 4, :] for k in range(0, KD, 4)])

        ffn_chunks = [(c0, min(BANK, DFF - c0)) for c0 in range(0, DFF, BANK)]
        for i, (c0, n) in enumerate(ffn_chunks):
            W.plan_split(f"gate{i}", io["w_gate"][0], c0, n)
            W.plan_split(f"up{i}", io["w_up"][0], c0, n)
            plan_ada(i)
        for i in range(2):
            W.plan_split(f"down{i}", io["w_down"][0], i * BANK, BANK)
        GU = NG2 + MW
        in2 = [("q2", 0, BANK), ("k2", MW, BANK), ("v2", 2 * MW, BANK), ("o2", 3 * MW, BANK),
               ("gu0", 4 * MW, GU // 2), ("gu1", 4 * MW + GU // 2, GU // 2)]
        in2 = [in2[0], in2[1], in2[4], in2[5], in2[2], in2[3]]
        for i, (name, c0, n) in enumerate(in2):
            W.plan_split(name, w_in2, c0, n)
            if i == 3:
                W.plan_raw("pool_matrix", [io["pool_matrix"]])
            if 1 <= i <= 4:
                plan_ada(5 + i)
        for i in range(2):
            W.plan_split(f"w_out2_{i}", io["w_out_2"][0], i * BANK, BANK)
        for i in range(DFF2 // BANK):
            W.plan_split(f"ff1_{i}", io["w_ff1_2"][0], i * BANK, BANK)
            if i in (2, 4):
                plan_ada(10 if i == 2 else 11)
        for i in range(2):
            W.plan_split(f"ff2_{i}", io["w_ff2_2"][0], i * BANK, BANK)

        n_loads = [0]

        def load(dst, src, *marks, queue=None, scattered=False):
            lane = queue or pool
            n_loads[0] += 1
            s = sem(f"load{n_loads[0]}_landed")
            lane.wait(*marks)
            lane.engine.dma_start(dst, src, allow_slow_non_contiguous=scattered).then_inc(s, 16)
            return (s, 16)

        def dump(name, ap, *marks):
            if debug is not None and name in debug:
                s = sem(f"dump_{name}")
                sp.wait(*marks)
                nc.sync.dma_start(debug[name], ap).then_inc(s, 16)
                nc.sync.wait_ge(s, 16)
                for lane in (pe, act, dve, pool):
                    lane.wait((s, 16))

        turn = {"tr": 0, "aux": 0}

        def next_bank(kind):
            group = {"tr": tr_banks, "aux": aux_banks}[kind]
            turn[kind] += 1
            return group[turn[kind] % len(group)]

        def linear(name, in_h, in_l, ready, banks_by_tile, k_first=0):
            units = W.chunks[name]
            rows = units[-1]["k0"] + units[-1]["kn"]
            for u in units:
                W.prepare_through(u["index"] + AHEAD)
                assert W.prepared > u["index"]
                pe.wait(u["high_ready"], u["low_ready"])
                for j in range(u["kn"]):
                    k = u["k0"] + j
                    for t in range(NT):
                        bank = banks_by_tile[t]
                        if k == 0:
                            pe.wait(bank.readers)
                        pe.wait(ready[k // 4][t])
                        dst = bank.ap[:, 0:u["n"]]
                        ts = slice(t * P, (t + 1) * P)
                        xh, xl = in_h[:, k_first + k, ts], in_l[:, k_first + k, ts]
                        wh, wl = u["high"][:, j, :], u["low"][:, j, :]
                        pe.engine.matmul(dst, xh, wh, start=k == 0, stop=False)
                        pe.engine.matmul(dst, xl, wh, start=False, stop=False)
                        last = pe.engine.matmul(dst, xh, wl, start=False, stop=k == rows - 1)
                u["used"] = pe.mark(last)
                yield u["used"]

        later = []

        def run(chunk, hold=2):
            done = None
            for n, done in enumerate(chunk):
                if n == hold - 1:
                    run_later()
            return done

        def run_later():
            work, later[:] = list(later), []
            for f in work:
                f()

        def transpose_tiles(sources, marks, kind="tr"):
            bank = next_bank(kind)
            pe.wait(bank.readers)
            pe.wait(*marks)
            for i, s in enumerate(sources):
                last = pe.engine.transpose(bank.ap[0:s.shape[1], i * P:i * P + s.shape[0]], s,
                                           ident[0:s.shape[0], 0:s.shape[0]])
            return bank, pe.mark(last)

        def split_from(bank, mark, dst_h, dst_l, free, shape=None):
            n = dst_h.shape[1]
            src = bank.ap[:, 0:n * P].rearrange("p (k n) -> p k n", k=n)
            act.wait(mark, *free)
            h = act.mark(act.engine.activation(dst_h, src, ACT.Copy))
            dve.wait(mark, h, *free)
            l = dve.mark(dve.engine.tensor_tensor(dst_l, src, dst_h.bitcast(F32), ALU.subtract))
            bank.readers = [h, l]
            return [h, l]

        def to_features(tile, n, t, marks, in_h, in_l, k0, free):
            out_marks = []
            for g in range(0, n, 4):
                m = min(4, n - g)
                bank, mark = transpose_tiles([tile[:, (g + i) * P:(g + i + 1) * P] for i in range(m)], marks)
                dst = slice(k0 + g, k0 + g + m)
                out_marks.append(split_from(bank, mark, in_h[:, dst, t * P:(t + 1) * P],
                                            in_l[:, dst, t * P:(t + 1) * P], free))
            return out_marks

        stat_at = [0]

        def inverse_rms(sums, width, count, mark):
            pool.wait(mark)
            m = pool.mark(pool.engine.tensor_scalar(sums, sums, 1.0 / width, NORM_EPS, ALU.mult, ALU.add))
            pool.wait(m)
            return pool.mark(pool.engine.tensor_tensor(sums, sums, minus_half[:, 0:count], ALU.pow))

        def norm_scale(t, marks, xn_free):
            col = stat[:, stat_at[0]:stat_at[0] + 1]
            stat_at[0] += 1
            act.wait(*marks, *xn_free)
            m = act.mark(act.engine.activation(xn[:, t, :], x[:, t, :], ACT.Square, accum_out=col))
            return col, inverse_rms(col, D, 1, m)

        def norm_to(dst, t, row, row_mark, marks, xn_free):
            col, m = norm_scale(t, marks, xn_free)
            dve.wait(m, row_mark)
            return dve.mark(dve.engine.scalar_tensor_tensor(dst, x[:, t, :], col, row[:, :], ALU.mult, ALU.mult))

        def ready_of(marks_by_tile):
            return [[marks_by_tile[t][g] for t in range(NT)] for g in range(len(marks_by_tile[0]))]

        W.pump()
        x_landed = [load(x[:, t, :], x_in[0, t * P:(t + 1) * P, :], queue=act) for t in range(NT)]
        cst_landed = load(cst[:, :], consts, queue=act)
        row_a_full = load(row_a[:, :], io["attn_norm_g"].to_broadcast([P, D]), queue=act)
        ones_set = pool.mark(pool.engine.memset(ones[:, :], 1.0))
        half_set = pool.mark(pool.engine.memset(minus_half[:, :], -0.5))
        pool.wait(half_set)
        rows_zero = pool.mark(pool.engine.memset(vec_rows[:, :], 0.0))
        pool.wait(rows_zero)
        pos_i = sb("positions_int", [P, NT], I32)
        pos_landed = load(pos_i[:, :], io["positions"][0].rearrange("(t p) -> p t", p=P), scattered=True)
        lam_rows = sb("lambda_rows", [P, 4, DH])
        lam_landed = load(lam_rows[:, :, :], io["diff_lambda"][0].partition_broadcast(P))
        V_PEK, V_PEV, V_C, V_PS = 0, CMP_J, 2 * CMP_J, 2 * CMP_J + KD
        vecs = [load(vec_rows[V_PEK:V_PEK + CMP_J, :], io["cmp_pe_k"][0].rearrange("(j a) d -> j (a d)", a=2), rows_zero),
                load(vec_rows[V_PEV:V_PEV + CMP_J, :], io["cmp_pe_v"][0].rearrange("(j a) d -> j (a d)", a=2), rows_zero),
                load(vec_rows[V_C:V_C + KD, :], io["c_2"].rearrange("a (k p) -> (a k) p", p=P), rows_zero),
                load(vec_rows[V_PS:V_PS + PG, :], io["pool_scale_2"].rearrange("a (k p) -> (a k) p", p=P), rows_zero)]
        row_b_full = load(row_b[:, :], io["ffn_norm_g"].to_broadcast([P, D]))
        b_ada_landed = load(b_ada[:, :], io["b_ada_2"].rearrange("a (k n) -> (a k) n", n=BANK))

        mixer = ExitStack()
        ctx.enter_context(mixer)

        def mb(name, shape, dtype=F32):
            return sb(name, shape, dtype, stack=mixer)

        pj = mb("projected", [P, NT, O_MG])
        mg = mb("merge_gates", [P, NT, 2 * D])
        dqT = mb("diff_qT", [P, DIFF_H, 2, T])
        dkT = mb("diff_kT", [P, DIFF_H, T])
        nqT = mb("nsa_qT", [P, HPG, T])
        kswT = mb("nsa_kT", [P, 2, T])
        E = mb("exp_scores", [P, 2, BANK])
        PT = mb("probsT", [P, 2, BANK])
        g_sub = mb("subln_row", [P, P])
        w2k = mb("cmp_k_w2", [P, KH, DH])
        w2v = mb("cmp_v_w2", [P, KH, DH])
        cosT = mb("cos", [P, NT, 2, HALF])
        sinT = mb("sin", [P, NT, 2, HALF])
        g_sub_full = load(g_sub[:, :], io["diff_subln_g"].to_broadcast([P, P]))
        w2_full = [load(w2k[:, :, :], io["cmp_k_w2"][0].rearrange("(k p) n -> p k n", p=P)),
                   load(w2v[:, :, :], io["cmp_v_w2"][0].rearrange("(k p) n -> p k n", p=P))]
        x2T = mg[:, 0, D:2 * D].rearrange("p (g v t) -> p g v t", g=G, v=2)
        blk = mg[:, 1, D:D + 2 * CMP_J * G * NC].rearrange("p (v j c) -> p v j c", v=2, j=CMP_J)
        hv4 = mb("cmp_hidden_spread", [P, G, KH, HPG, CPAD])
        vbd = mb("cmp_v_blocks", [P, G, HPG, DH])
        cmp_f = mb("cmp_small", [P, 2, 2 * KH * G * NC])
        kcd = mb("cmp_kT", [P, NC])
        pc = mb("cmp_probs", [P, NT, NSA_H, CPAD])

        x_ready = []
        for t in range(NT):
            pool.wait(half_set)
            n_mark = norm_to(xn[:, t, :], t, row_a, row_a_full, [x_landed[t]], [])
            pe.wait(cst_landed)
            x_ready.append(to_features(xn[:, t, :], KD, t, [n_mark], uT_h, uT_l, 0, []))
            row_a_read = n_mark
        u_ready = ready_of(x_ready)
        row_a_full = load(row_a[:, :], io["final_norm_g"].unsqueeze(0).to_broadcast([P, D]), row_a_read)

        act.wait(cst_landed)
        act.engine.activation(ident_r[:, :], ident, ACT.Copy)
        act.engine.activation(after_r[:, :], cst[:, P:2 * P], ACT.Copy)
        masks_ready = act.mark(act.engine.activation(before_r[:, :], cst[:, 2 * P:3 * P], ACT.Copy))

        def chain(ins):
            m = dve.mark(ins)
            dve.wait(m)
            return m

        v = dve.engine
        dve.wait(pos_landed, cst_landed, lam_landed)
        chain(v.tensor_copy(small[:, 0:NT], pos_i[:, :]))
        ang = E[:, 0, 0:NT * 2 * HALF].rearrange("p (t s d) -> p t s d", t=NT, s=2)
        turns = E[:, 1, 0:NT * 2 * HALF].rearrange("p (t s d) -> p t s d", t=NT, s=2)
        for t in range(NT):
            for s in range(2):
                m = dve.mark(v.tensor_scalar(ang[:, t, s, :], inv_freq, small[:, t:t + 1], None, ALU.mult))
        dve.wait(m)
        for s, quarter in ((0, 0.25), (1, 0.0)):
            m = dve.mark(v.tensor_scalar(turns[:, :, s, :], ang[:, :, s, :], 0.15915494309189535, quarter,
                                         ALU.mult, ALU.add))
        dve.wait(m)
        chain(v.tensor_scalar(turns[:, :, :, :], turns[:, :, :, :], MAGIC, None, ALU.add))
        chain(v.tensor_scalar(turns[:, :, :, :], turns[:, :, :, :], MAGIC, None, ALU.subtract))
        for part in TWO_PI_PARTS:
            chain(v.scalar_tensor_tensor(ang[:, :, :, :], turns[:, :, :, :], -part, ang[:, :, :, :], ALU.mult, ALU.add))
        chain(v.tensor_scalar(ang[:, :, 0, :], ang[:, :, 0, :], 1.5707963267948966, None, ALU.add))
        ang_ready = chain(v.tensor_scalar(ang[:, :, :, :], ang[:, :, :, :], PI_BELOW, -PI_BELOW, ALU.min, ALU.max))
        act.wait(ang_ready)
        for h in range(2):
            act.engine.activation(cosT[:, :, h, :], ang[:, :, 0, :], ACT.Sin)
            rope_ready = act.mark(act.engine.activation(sinT[:, :, h, :], ang[:, :, 1, :], ACT.Sin))
        dve.wait(rope_ready)
        rope_ready = [rope_ready, chain(v.tensor_scalar(sinT[:, :, 0, :], sinT[:, :, 0, :], -1.0, None, ALU.mult))]

        lam_pair = lam_rows[:, :, :].rearrange("p (a b) d -> p a b d", a=2)
        chain(v.tensor_tensor(lam_rows[:, 0:2, :], lam_pair[:, :, 0, :], lam_pair[:, :, 1, :], ALU.mult))
        m = chain(v.tensor_reduce(small[:, 2:4], lam_rows[:, 0:2, :], AX.X, ALU.add))
        act.wait(m)
        m = act.mark(act.engine.activation(small[:, 4:6], small[:, 2:4], ACT.Exp))
        dve.wait(m)
        chain(v.tensor_tensor(small[:, 6:7], small[:, 5:6], small[:, 4:5], ALU.subtract))
        neg_lam = small[:, 6:7]
        lam_ready = chain(v.tensor_scalar(neg_lam, neg_lam, -LAM_INIT, None, ALU.add))

        bank, m = transpose_tiles([vec_rows[:, :]], [rows_zero] + vecs)
        dve.wait(m)
        vec_ready = chain(v.tensor_copy(vec_cols[:, :], bank.ap[:, 0:64]))
        bank.readers = [vec_ready]
        c_col = vec_cols[:, V_C:V_C + KD]
        act.wait(vec_ready)
        m = act.mark(act.engine.activation(small[:, 8:8 + KD], c_col, ACT.Exp, scale=-1.0))
        dve.wait(m)
        chain(v.tensor_scalar(small[:, 8:8 + KD], small[:, 8:8 + KD], 1.0, None, ALU.add))
        chain(v.reciprocal(small[:, 8:8 + KD], small[:, 8:8 + KD]))
        c_ready = chain(v.tensor_tensor(c_act[:, :], c_col, small[:, 8:8 + KD], ALU.mult))

        rope_free = [[], []]

        def rope(bank, mark, c0, n, t, dst):
            heads = n // DH
            src = bank.ap[:, c0:c0 + n].rearrange("p (h s d) -> p h s d", h=heads, s=2)
            straight = E[:, t, c0:c0 + n].rearrange("p (h s d) -> p h s d", h=heads, s=2)
            crossed = PT[:, t, c0:c0 + n].rearrange("p (h s d) -> p h s d", h=heads, s=2)
            cos = cosT[:, t, :, :].unsqueeze(1).to_broadcast([P, heads, 2, HALF])
            sin = sinT[:, t, :, :].unsqueeze(1).to_broadcast([P, heads, 2, HALF])
            dve.wait(mark, rope_ready, rope_free[t])
            v.tensor_tensor(straight, src, cos, ALU.mult)
            m = dve.mark(v.tensor_tensor(crossed, src[:, :, ::-1, :], sin, ALU.mult))
            pool.wait(m)
            a, b = E[:, t, c0:c0 + n], PT[:, t, c0:c0 + n]
            if len(dst.shape) == 4:
                a, b = (s.rearrange("p (g j d) -> p g j d", g=G, d=DH) for s in (a, b))
            done = pool.mark(pool.engine.tensor_tensor(dst, a, b, ALU.add))
            return m, done

        def copy_out(lane, dst, src, marks, scale=None):
            lane.wait(*marks)
            if lane is act:
                if scale is None:
                    return act.mark(act.engine.activation(dst, src, ACT.Copy))
                return act.mark(act.engine.activation(dst, src, ACT.Copy, scale=scale))
            if scale is None:
                return dve.mark(v.tensor_copy(dst, src))
            return dve.mark(v.tensor_scalar(dst, src, scale, None, ALU.mult))

        proj_done = {}
        dq_zero = pool.mark(pool.engine.memset(dqT[:, :, :, :], 0.0))

        def heads_T(name, c0, n_tiles, dst, scale, lane):
            def work():
                for t in range(NT):
                    tiles = [pj[:, t, c0 + i * P:c0 + (i + 1) * P] for i in range(n_tiles)]
                    bank, mark = transpose_tiles(tiles, [proj_done[name][t]])
                    src = bank.ap[:, 0:n_tiles * P].rearrange("p (k n) -> p k n", k=n_tiles)
                    if name == "dq":
                        for c in range(2):
                            rows = slice(c * DH, (c + 1) * DH)
                            m = copy_out(lane, dst[rows, :, c, t * P:(t + 1) * P], src[rows, :, :], [mark, dq_zero], scale)
                    else:
                        m = copy_out(lane, dst[:, :, t * P:(t + 1) * P], src, [mark], scale)
                    bank.readers = [m]
                    proj_done[name + "T"] = proj_done.get(name + "T", []) + [m]
            return work

        Q_SCALE = DH ** -0.5
        rotated = {"dq": (O_DQ, dqT, Q_SCALE, act), "dk": (O_DK, dkT, None, act), "nq": (O_NQ, nqT, Q_SCALE, act)}
        pairs = [acc[0:2], acc[2:4]]
        for i, name in enumerate(("dq", "dk", "dv", "nq")):
            pair = pairs[i % 2]
            done = run(linear(name, uT_h, uT_l, u_ready, pair))
            c0 = {"dq": O_DQ, "dk": O_DK, "dv": O_DV, "nq": O_NQ}[name]
            proj_done[name] = []
            for t in range(NT):
                if name == "dv":
                    m = copy_out(act, pj[:, t, c0:c0 + DIFF_W], pair[t].ap[:, :], [done])
                    pair[t].readers = [m]
                    proj_done[name].append(m)
                else:
                    dst = pj[:, t, c0:c0 + BANK]
                    if name == "nq":
                        dst = dst.rearrange("p (j g d) -> p g j d", g=G, d=DH)
                    read, m = rope(pair[t], done, 0, BANK, t, dst)
                    pair[t].readers = [read]
                    rope_free[t] = [m]
                    proj_done[name].append(m)
            if name != "dv":
                c0, dst, scale, lane = rotated[name]
                later.append(heads_T(name, c0, 4, dst, scale, lane))

        pair = pairs[0]
        done = run(linear("kva", uT_h, uT_l, u_ready, pair))
        kc_done, ks_done, vc_done = [], [], []
        for t in range(NT):
            m1, d1 = rope(pair[t], done, 0, KV, t, pj[:, t, O_KC:O_KC + KV])
            m2, d2 = rope(pair[t], done, 2 * KV, KV, t, pj[:, t, O_KS:O_KS + KV])
            m3 = copy_out(act, pj[:, t, O_VC:O_VC + KV], pair[t].ap[:, KV:2 * KV], [done, m2])
            pair[t].readers = [m2, m3]
            rope_free[t] = [d2]
            kc_done.append(d1), ks_done.append(d2), vc_done.append(m3)
        pair = pairs[1]
        done = run(linear("kvb", uT_h, uT_l, u_ready, pair))
        kw_done, vs_done = [], []
        for t in range(NT):
            m1, d1 = rope(pair[t], done, KV, KV, t, pj[:, t, O_KW:O_KW + KV])
            m2 = copy_out(act, pj[:, t, O_VS:O_VS + KV], pair[t].ap[:, 0:KV], [done, m1])
            m3 = copy_out(act, pj[:, t, O_VW:O_VW + KV + N_GATES], pair[t].ap[:, 2 * KV:3 * KV + N_GATES], [done])
            pair[t].readers = [m1, m3]
            rope_free[t] = [d1]
            kw_done.append(d1), vs_done.append(m3)

        gates = [pj[:, t, O_NG:O_NG + N_GATES] for t in range(NT)]
        gates_done = []
        for t in range(NT):
            act.wait(vs_done[t])
            m = act.mark(act.engine.activation(gates[t], gates[t], ACT.Exp, scale=-1.0))
            dve.wait(m)
            chain(v.tensor_scalar(gates[t], gates[t], 1.0, None, ALU.add))
            gates_done.append(chain(v.reciprocal(gates[t], gates[t])))

        x2_done = []

        def sources_T():
            tiles = [pj[:, t, c:c + KV] for c in (O_KC, O_VC) for t in range(NT)]
            bank, mark = transpose_tiles(tiles, kc_done + vc_done)
            src = bank.ap[:, :].rearrange("p (v t) -> p v t", v=2)
            marks = []
            for g in range(G):
                marks.append(copy_out(act, x2T[0:DH, g, :, :], src[g * DH:(g + 1) * DH, :, :], [mark]))
            for g in range(G):
                marks.append(copy_out(dve, x2T[DH:P, g, :, 0:T - 1], src[g * DH:(g + 1) * DH, :, 1:T], [mark, marks[1]]))
            bank.readers = marks
            x2_done.extend(marks)

        ksw_done = []

        def keys_T():
            tiles = [pj[:, t, c:c + KV] for c in (O_KS, O_KW) for t in range(NT)]
            bank, mark = transpose_tiles(tiles, ks_done + kw_done)
            src = bank.ap[:, :].rearrange("p (w t) -> p w t", w=2)
            marks = [copy_out(act, kswT[:, :, :], src, [mark])]
            bank.readers = marks
            ksw_done.extend(marks)

        later.append(sources_T)
        later.append(keys_T)

        mg_done = []

        def merge_gate_chunks():
            for i in range(4):
                pair = pairs[0]
                for mark in linear(f"mg{i}", uT_h, uT_l, u_ready, pair):
                    done = mark
                    yield mark
                for t in range(NT):
                    m = copy_out(act, mg[:, t, i * BANK:(i + 1) * BANK], pair[t].ap[:, :], [done] + (cmp_read if i >= 2 else []))
                    pair[t].readers = [m]
                    mg_done.append(m)
                gates_through[0] = done

        gates_through = [None]
        cmp_read = []
        filler = merge_gate_chunks()

        def fill(n=1):
            for _ in range(n):
                next(filler, None)

        fill(2)
        run_later()
        fill(2)

        blk_done = []
        for kv in range(2):
            for g in range(G):
                by = x2T[:, g, kv, :].rearrange("p (n j a) -> p j n a", j=CMP_J // 2, a=2)
                for half in range(2):
                    js = slice(half * (CMP_J // 2), (half + 1) * (CMP_J // 2))
                    pe_col = vec_cols[:, (V_PEK, V_PEV)[kv] + js.start:(V_PEK, V_PEV)[kv] + js.stop]
                    pool.wait(x2_done, vec_ready)
                    blk_done.append(pool.mark(pool.engine.tensor_tensor(
                        blk[:, kv, js, g * NC:(g + 1) * NC], by[:, :, half:half + NC, 0],
                        pe_col.unsqueeze(2).to_broadcast([P, CMP_J // 2, NC]), ALU.add)))
        m = pool.mark(pool.engine.memset(hv4[:, :, :, :, :], 0.0))
        m = pool.mark(pool.engine.memset(vbd[:, :, :, :], 0.0))
        cmp_zero = pool.mark(pool.engine.memset(pc[:, :, :, :], 0.0))

        hid_bank = next_bank("aux")
        hid = hid_bank.ap[:, 0:2 * KH * G * NC].rearrange("p (v m c) -> p v m c", v=2, m=KH)
        pe.wait(hid_bank.readers)
        for kv, name in enumerate("kv"):
            slabs = W.chunks[f"cmp_{name}"]
            pe.wait(blk_done[4 * kv + 3], *[W.slabs[s]["landed"] for s in slabs])
            for m_ in range(KH):
                for j in range(CMP_J):
                    w1 = W.slab_view(slabs[j // (CMP_J // 2)])[:, j % (CMP_J // 2), m_ * P:(m_ + 1) * P]
                    last = pe.engine.matmul(hid[:, kv, m_, :], w1, blk[:, kv, j, :], start=j == 0, stop=j == CMP_J - 1)
            done = pe.mark(last)
            for s in slabs:
                W.release(s, done)
        hid_n = 2 * KH * G * NC
        expo, hidden = cmp_f[:, 0, 0:hid_n], cmp_f[:, 1, 0:hid_n]
        act.wait(done)
        m = act.mark(act.engine.activation(expo, hid_bank.ap[:, 0:hid_n], ACT.Exp, scale=-1.0))
        dve.wait(m, done)
        chain(v.tensor_scalar(expo, expo, 1.0, None, ALU.add))
        chain(v.reciprocal(expo, expo))
        hid_done = chain(v.tensor_tensor(hidden, hid_bank.ap[:, 0:hid_n], expo, ALU.mult))
        hid_bank.readers = [hid_done]
        hT = hidden.rearrange("p (v m g c) -> p v m g c", v=2, m=KH, g=G)
        dve.wait(cmp_zero)
        for g in range(G):
            for m_ in range(KH):
                hv_done = dve.mark(v.tensor_copy(hv4[:, g, m_, :, 0:NC],
                                                 hT[:, 1, m_, g, :].unsqueeze(1).to_broadcast([P, HPG, NC])))
        fill(1)
        kc_bank = next_bank("aux")
        pe.wait(kc_bank.readers)
        pe.wait(hid_done, hv_done, w2_full)
        for g in range(G):
            for m_ in range(KH):
                pe.engine.matmul(kc_bank.ap[g * DH:(g + 1) * DH, 0:NC], w2k[:, m_, :],
                                 hT[:, 0, m_, g, :], start=m_ == 0, stop=m_ == KH - 1)
        for g in range(G):
            for m_ in range(KH):
                last = pe.engine.matmul(kc_bank.ap[:, 64 + g * DH:64 + (g + 1) * DH],
                                        hv4[:, g, m_, :, :], w2v[:, m_, :], start=m_ == 0, stop=m_ == KH - 1)
        done = pe.mark(last)
        kcd_done = copy_out(act, kcd[:, :], kc_bank.ap[:, 0:NC], [done])
        vals = kc_bank.ap[:, 64:64 + G * DH].rearrange("p (g d) -> p g d", g=G)
        dve.wait(done, kcd_done)
        for j in range(HPG):
            rows = slice(j * CPAD, (j + 1) * CPAD)
            vbd_done = dve.mark(v.tensor_copy(vbd[rows, :, j, :], vals[rows, :, :]))
        kc_bank.readers = [kcd_done, vbd_done]
        cmp_read += [blk_done[-1], hid_done]

        e_free, pt_free = [[], []], [[], []]
        e_free[0] = e_free[1] = rope_free[0] + rope_free[1]
        pt_free[0] = pt_free[1] = rope_free[0] + rope_free[1]
        sums = mb("score_sums", [P, 4, 2])
        nmax = mb("score_negmax", [P, 4, 2])
        inv = mb("score_scales", [P, 4, 2])
        turn_of = [0]

        def scores(matmuls, width, query_tile, marks):
            i = turn_of[0]
            turn_of[0] += 1
            bank = next_bank("aux")
            s = bank.ap[:, 0:2 * width].rearrange("p (c w) -> p c w", c=2)
            pe.wait(bank.readers)
            pe.wait(masks_ready, *marks)
            matmuls(s)
            done = pe.mark(pe.engine.matmul(s[:, :, width - P:width], ident_r[:, :],
                                            after_r[:, :].unsqueeze(1).to_broadcast([P, 2, P]),
                                            start=False, stop=True, skip_group_check=True))
            dve.wait(done)
            max_ready = dve.mark(v.tensor_reduce(nmax[:, i % 4, :], s, AX.X, ALU.max, negate=True))
            e = E[:, i % 2, 0:2 * width].rearrange("p (c w) -> p c w", c=2)
            act.wait(done, max_ready, e_free[i % 2])
            for c in range(2):
                m = act.mark(act.engine.activation(e[:, c, :], s[:, c, :], ACT.Exp, bias=nmax[:, i % 4, c:c + 1],
                                                   accum_out=sums[:, i % 4, c:c + 1]))
            bank.readers = [m]
            return i, e, m

        def probs_T(i, tiles, m, lane):
            bank, mark = transpose_tiles(tiles, [m])
            e_free[i % 2] = [mark]
            n = len(tiles)
            done = copy_out(lane, PT[:, i % 2, 0:n * P], bank.ap[:, 0:n * P], [mark] + pt_free[i % 2])
            bank.readers = [done]
            return PT[:, i % 2, 0:n * P].rearrange("p (b q) -> p b q", b=n), done

        def diff_scores(h, q):
            width = (q + 1) * P

            def matmuls(s):
                for c in range(2):
                    pe.engine.matmul(s[:, c, :], dqT[:, h, c, q * P:(q + 1) * P], dkT[:, h, 0:width],
                                     start=c == 0, stop=False, skip_group_check=True)
            return scores(matmuls, width, q, proj_done["dqT"] + proj_done["dkT"])

        o_banks = [acc[2], acc[3]]

        def diff_values(h, q, i, e, m):
            dve.wait(m, lam_ready)
            chain(v.reciprocal(inv[:, i % 4, :], sums[:, i % 4, :]))
            chain(v.tensor_tensor(inv[:, i % 4, 1:2], inv[:, i % 4, 1:2], neg_lam, ALU.mult))
            chain(v.tensor_scalar(e[:, 1, :], e[:, 1, :], inv[:, i % 4, 1:2], None, ALU.mult))
            m = chain(v.scalar_tensor_tensor(e[:, 0, :], e[:, 0, :], inv[:, i % 4, 0:1], e[:, 1, :], ALU.mult, ALU.add))
            pT, done = probs_T(i, [e[:, 0, b * P:(b + 1) * P] for b in range(q + 1)], m, act)
            pe.wait(done, proj_done["dv"])
            if h == 0:
                pe.wait(o_banks[q].readers)
            for b in range(q + 1):
                last = pe.engine.matmul(o_banks[q].ap[:, h * P:(h + 1) * P], pT[:, b, :],
                                        pj[:, b, O_DV + h * P:O_DV + (h + 1) * P], start=b == 0, stop=b == q)
            pt_free[i % 2] = [pe.mark(last)]
            return pt_free[i % 2][0]

        def pipeline(items, first, second, fills):
            waiting, last = [], {}
            for n, item in enumerate(items):
                waiting.append((item, first(*item)))
                if fills(n):
                    fill(1)
                if len(waiting) > 1:
                    it, got = waiting.pop(0)
                    last[it[1]] = second(*it, *got)
            for it, got in waiting:
                last[it[1]] = second(*it, *got)
            return last

        items = [(h, q) for h in range(DIFF_H) for q in range(NT)]
        diff_last = pipeline(items, diff_scores, diff_values, lambda n: n % 2 == 0)

        ya_done = []
        for t in range(NT):
            src = o_banks[t].ap[:, :]
            y = pj[:, t, O_DQ:O_DQ + DIFF_W]
            sq = pj[:, t, O_DK:O_DK + DIFF_W]
            s4 = stat[:, 40 + 4 * t:44 + 4 * t]
            act.wait(diff_last[t])
            m = act.mark(act.engine.activation(sq, src, ACT.Square))
            dve.wait(m, diff_last[t], g_sub_full)
            m = chain(v.tensor_reduce(s4, sq.rearrange("p (h e) -> p h e", h=DIFF_H), AX.X, ALU.add))
            r = inverse_rms(s4, 2 * DH, DIFF_H, m)
            g_all = g_sub[:, :].unsqueeze(1).to_broadcast([P, DIFF_H, P])
            m = dve.mark(v.scalar_tensor_tensor(sq.rearrange("p (h e) -> p h e", h=DIFF_H),
                                                src.rearrange("p (h e) -> p h e", h=DIFF_H), 1.0 - LAM_INIT, g_all,
                                                ALU.mult, ALU.mult))
            o_banks[t].readers = [m]
            dve.wait(m, r)
            ya_done.append(chain(v.tensor_tensor(y.rearrange("p (h e) -> p h e", h=DIFF_H),
                                                 sq.rearrange("p (h e) -> p h e", h=DIFF_H),
                                                 s4.unsqueeze(2).to_broadcast([P, DIFF_H, P]), ALU.mult)))

        o_open = [False, False]
        for q in range(NT):
            bank = next_bank("aux")
            pe.wait(bank.readers)
            pe.wait(kcd_done, proj_done["nqT"])
            for h in range(NSA_H):
                g = h // HPG
                rows = slice(g * DH, (g + 1) * DH)
                if h == HPG:
                    pe.wait(done)
                last = pe.engine.matmul(bank.ap[:, h * 16:h * 16 + NC], nqT[rows, h % HPG, q * P:(q + 1) * P],
                                        kcd[rows, :], start=True, stop=True)
                if h % HPG == HPG - 1:
                    done = pe.mark(last)
            sc = bank.ap[:, 0:NSA_H * 16].rearrange("p (h c) -> p h c", h=NSA_H)[:, :, 0:NC]
            p = pc[:, q, :, 0:NC]
            s8 = small[:, 16 + 16 * q:24 + 16 * q]
            wide = lambda a: a.unsqueeze(2).to_broadcast([P, NSA_H, NC])
            each = lambda a: a.unsqueeze(1).to_broadcast([P, NSA_H, NC])
            dve.wait(done, cmp_zero, cst_landed)
            m = chain(v.tensor_tensor(p, sc, each(cmp_add[:, q, :]), ALU.add))
            bank.readers = [m]
            chain(v.tensor_reduce(s8, p, AX.X, ALU.max))
            m = chain(v.tensor_tensor(p, p, wide(s8), ALU.subtract))
            act.wait(m)
            m = act.mark(act.engine.activation(p, p, ACT.Exp))
            dve.wait(m)
            chain(v.tensor_reduce(s8, p, AX.X, ALU.add))
            chain(v.reciprocal(s8, s8))
            dve.wait(gates_done[q])
            chain(v.tensor_tensor(s8, s8, gates[q][:, 0:NSA_H], ALU.mult))
            chain(v.tensor_tensor(p, p, each(cmp_keep[:, q, :]), ALU.mult))
            pc_done = chain(v.tensor_tensor(p, p, wide(s8), ALU.mult))
            fill(1)
            flat = pc[:, q, :, :].rearrange("p h c -> p (h c)")
            tb, mark = transpose_tiles([flat[:, g * P:(g + 1) * P] for g in range(G)], [pc_done])
            pcT = PT[:, q, 0:G * P]
            m = copy_out(act, pcT, tb.ap[:, 0:G * P], [mark] + pt_free[q])
            tb.readers = [m]
            pe.wait(m, vbd_done, o_banks[q].readers)
            for g in range(G):
                last = pe.engine.matmul(o_banks[q].ap[:, g * HPG * DH:(g + 1) * HPG * DH], pcT[:, g * P:(g + 1) * P],
                                        vbd[:, g, :, :], start=g == 0, stop=False, skip_group_check=True)
            pt_free[q] = [pe.mark(last)]

        def nsa_scores(h, q):
            width = (q + 1) * P
            g = h // HPG
            rows = slice(g * DH, (g + 1) * DH)

            def matmuls(s):
                pe.engine.matmul(s, nqT[rows, h % HPG, q * P:(q + 1) * P], kswT[rows, :, 0:width],
                                 start=True, stop=False, skip_group_check=True)
            return scores(matmuls, width, q, proj_done["nqT"] + ksw_done)

        def nsa_values(h, q, i, e, m):
            g = h // HPG
            gate = gates[q].rearrange("p (b h) -> p b h", b=3)[:, 1:3, h]
            dve.wait(m, gates_done[q])
            chain(v.reciprocal(inv[:, i % 4, :], sums[:, i % 4, :]))
            chain(v.tensor_tensor(inv[:, i % 4, :], inv[:, i % 4, :], gate, ALU.mult))
            for c in range(2):
                m = dve.mark(v.tensor_scalar(e[:, c, :], e[:, c, :], inv[:, i % 4, c:c + 1], None, ALU.mult))
            tiles = [(c, b) for c in range(2) for b in range(q + 1)]
            pT, done = probs_T(i, [e[:, c, b * P:(b + 1) * P] for c, b in tiles], m, act)
            pe.wait(done, vs_done)
            for n, (c, b) in enumerate(tiles):
                c0 = (O_VS, O_VW)[c] + g * DH
                last = pe.engine.matmul(o_banks[q].ap[:, h * DH:(h + 1) * DH], pT[:, n, :], pj[:, b, c0:c0 + DH],
                                        start=False, stop=n == len(tiles) - 1, skip_group_check=True)
            pt_free[i % 2] = [pe.mark(last)]
            return pt_free[i % 2][0]

        items = [(h, q) for h in range(NSA_H) for q in range(NT)]
        nsa_last = pipeline(items, nsa_scores, nsa_values, lambda n: n % 3 != 2)
        fill(16)
        gates_read = gates_through[0]

        yb_done = []
        for t in range(NT):
            yb = pj[:, t, O_NQ:O_NQ + NSA_W]
            m = copy_out(act, yb, o_banks[t].ap[:, :], [nsa_last[t]])
            o_banks[t].readers = [m]
            yb_done.append(m)
        free = [gates_read]
        ready_a = ready_of([to_features(pj[:, t, O_DQ:O_DQ + DIFF_W], 4, t, [ya_done[t]], uT_h, uT_l, 0, free)
                            for t in range(NT)])
        ready_b = ready_of([to_features(pj[:, t, O_NQ:O_NQ + NSA_W], 4, t, [yb_done[t]], uT_h, uT_l, 4, free)
                            for t in range(NT)])
        dump("ya", pj[:, :, O_DQ:O_DQ + DIFF_W], ya_done)
        dump("yb", pj[:, :, O_NQ:O_NQ + NSA_W], yb_done)

        W.prepare_through(W.chunks["branch_a0"][0]["index"] + AHEAD)
        sig_done = []
        for b in range(2):
            for t in range(NT):
                act.wait(mg_done)
                sig_done.append(act.mark(act.engine.activation(mg[:, t, b * D:(b + 1) * D], mg[:, t, b * D:(b + 1) * D], ACT.Sigmoid)))
        xn_free = []
        merged = [None, None]
        for i in range(2):
            cols = slice(i * BANK, (i + 1) * BANK)
            done = run(linear(f"branch_a{i}", uT_h, uT_l, ready_a, pairs[0]))
            for t in range(NT):
                dve.wait(done, sig_done)
                m = dve.mark(v.tensor_tensor(xn[:, t, cols], pairs[0][t].ap[:, :], mg[:, t, cols], ALU.mult))
                pairs[0][t].readers = [m]
            done = run(linear(f"branch_b{i}", uT_h, uT_l, ready_b, pairs[1], k_first=4))
            for t in range(NT):
                other = mg[:, t, D + i * BANK:D + (i + 1) * BANK]
                dve.wait(done)
                m = chain(v.tensor_tensor(other, pairs[1][t].ap[:, :], other, ALU.mult))
                pairs[1][t].readers = [m]
                merged[t] = chain(v.tensor_tensor(xn[:, t, cols], xn[:, t, cols], other, ALU.add))
        free = [done]
        ready = ready_of([to_features(xn[:, t, :], KD, t, [merged[t]], uT_h, uT_l, 0, free) for t in range(NT)])

        def residual(name, ready, in_h, in_l, after=None):
            marks = [[], []]
            for i in range(2):
                done = run(linear(f"{name}{i}", in_h, in_l, ready, pairs[i]))
                for t in range(NT):
                    cols = slice(i * BANK, (i + 1) * BANK)
                    dve.wait(done)
                    m = dve.mark(v.tensor_tensor(x[:, t, cols], pairs[i][t].ap[:, :], x[:, t, cols], ALU.add))
                    pairs[i][t].readers = [m]
                    marks[t].append(m)
            return marks, done

        x_marks, done = residual("w_out", ready, uT_h, uT_l)
        dump("x1", x[:, :, :], *x_marks)
        mixer.close()

        hidden_stack = ExitStack()
        ctx.enter_context(hidden_stack)
        hid_h = sb("hidden_high", [P, KF2, T], F32R, stack=hidden_stack)
        hid_l = sb("hidden_low", [P, KF2, T], F32R, stack=hidden_stack)

        def norm_and_turn(row, row_mark, marks, free):
            r, norms = [], []
            for t in range(NT):
                norms.append(norm_to(xn[:, t, :], t, row, row_mark, marks[t], []))
                r.append(to_features(xn[:, t, :], KD, t, [norms[t]], uT_h, uT_l, 0, free))
            return ready_of(r), norms

        ready, norms = norm_and_turn(row_b, row_b_full, x_marks, [done])
        row_b_full = load(row_b[:, :], io["g_mix_2"].to_broadcast([P, D]), *norms)

        ada_free = [[]]

        def ada(i, dst, dst_free, how):
            cols = None
            prev = None
            for n, s in enumerate(W.chunks[f"ada{i}"]):
                w = W.slab_view(s)
                for k in range(4):
                    dve.wait(W.slabs[s]["landed"], c_ready)
                    c = c_act[:, 4 * n + k:4 * n + k + 1]
                    if prev is None:
                        dve.wait(ada_free[0])
                        prev = chain(v.tensor_scalar(ada_acc[:, :], w[:, k, :], c, None, ALU.mult))
                    else:
                        prev = chain(v.scalar_tensor_tensor(ada_acc[:, :], w[:, k, :], c, ada_acc[:, :], ALU.mult, ALU.add))
                W.release(s, prev)

            def finish():
                bank = next_bank("aux")
                pe.wait(bank.readers)
                pe.wait(prev, ones_set, b_ada_landed)
                pe.engine.matmul(bank.ap[:, :], ones[:, :], ada_acc[:, :], start=True, stop=False)
                m = pe.mark(pe.engine.matmul(bank.ap[:, :], ident[0:12, i:i + 1].to_broadcast([12, P]), b_ada[:, :],
                                             start=False, stop=True))
                ada_free[0] = [m]
                dve.wait(m, *dst_free)
                if how == "scale":
                    r = dve.mark(v.scalar_tensor_tensor(dst, bank.ap[:, :], 1.0, dst, ALU.add, ALU.mult))
                else:
                    r = dve.mark(v.tensor_copy(dst, bank.ap[:, :]))
                bank.readers = [r]
                ada_done[i] = r
            later.append(finish)

        ada_done = {}
        halves = [slice(0, BANK), slice(BANK, D)]
        ada_plan = {0: (row_c, 0, "copy"), 1: (row_c, 1, "copy"), 2: (row_b, 0, "scale"), 3: (row_b, 1, "scale"),
                    4: (row_d, 0, "copy"), 5: (row_d, 1, "copy")}

        scratch_free = {}

        def hidden_T(tile, n, t, k0, mark, key):
            def work():
                m = to_features(tile, n, t, [mark], hid_h, hid_l, k0, [])
                scratch_free[key] = m[-1]
                hidden_ready[t].extend(m)
            return work

        hidden_ready = [[], []]
        for i, (c0, n) in enumerate(ffn_chunks):
            g_done = run(linear(f"gate{i}", uT_h, uT_l, ready, pairs[0]))
            sl = xn[:, :, (i % 2) * BANK:(i % 2) * BANK + n]
            silus = []
            for t in range(NT):
                act.wait(g_done)
                silus.append(copy := act.mark(act.engine.activation(sl[:, t, :], pairs[0][t].ap[:, 0:n], ACT.Silu)))
                pairs[0][t].readers = [copy]
            u_done = run(linear(f"up{i}", uT_h, uT_l, ready, pairs[1]))
            for t in range(NT):
                dve.wait(silus[t], u_done)
                m = dve.mark(v.tensor_tensor(sl[:, t, :], pairs[1][t].ap[:, 0:n], sl[:, t, :], ALU.mult))
                pairs[1][t].readers = [m]
                later.append(hidden_T(sl[:, t, :], n // P, t, c0 // P, m, (i % 2, t)))
            dst, half, how = ada_plan[i]
            ada(i, dst[:, halves[half]], [row_b_full] if how == "scale" else [], how)
        run_later()
        hidden_marks = ready_of(hidden_ready)
        x_marks, down_done = residual("down", hidden_marks, hid_h, hid_l)
        dump("x2", x[:, :, :], *x_marks)

        x_done = [[norm_to(x[:, t, :], t, row_a, row_a_full, x_marks[t], [])] for t in range(NT)]
        row_a_full = load(row_a[:, :], io["g_final_2"].unsqueeze(0).to_broadcast([P, D]), *[m[0] for m in x_done])
        hidden_stack.close()

        mix2 = ExitStack()
        ctx.enter_context(mix2)

        def m2(name, shape, dtype=F32):
            return sb(name, shape, dtype, stack=mix2)

        def norm_modulate(row, row_marks, shift, shift_marks, marks, free):
            r, adds = [], []
            for t in range(NT):
                m = norm_to(xn[:, t, :], t, row, row_marks, marks[t], [])
                dve.wait(m, *shift_marks)
                m = dve.mark(v.tensor_tensor(xn[:, t, :], xn[:, t, :], shift[:, :], ALU.add))
                adds.append(m)
                r.append(to_features(xn[:, t, :], KD, t, [m], uT_h, uT_l, 0, free))
            return ready_of(r), adds

        ready, adds = norm_modulate(row_b, [ada_done[2], ada_done[3]], row_c, [ada_done[0], ada_done[1]],
                                    x_done, [down_done])
        row_b_full = load(row_b[:, :], io["g_ffn_2"].to_broadcast([P, D]), *adds)

        vE = m2("v_and_one", [P, NT, H2, E2 + 1])
        so = m2("sigmoid_o", [P, NT, MW])
        u_pool = m2("pool_input", [P, NT, MW])
        qk = m2("q_k", [P, NT, 2 * MW])
        q2T = m2("q2T", [P, H2, T])
        k2T = m2("k2T", [P, H2, T])
        gt = m2("gate_values", [P, NT, 2, 2, H2])
        gb = m2("gate_bias", [P, 2, 2, H2])
        gp = m2("gate_padded", [P, NT, 2, 64])
        rows2 = m2("gate_rows", [64, 2, T])
        scans = m2("gate_scans", [64, 3, T])
        cols2 = m2("gate_columns", [P, NT, 3, 64])
        expm = m2("exp_minus_m", [P, NT, 64])
        gh = m2("head_gain_row", [P, MW])
        wT = m2("decay_T", [P, 2, 3 * P])
        sT = m2("scoresT_weighted", [P, 2, 3 * P])
        hm = m2("heads_out", [P, NT, MW])
        hsq = m2("heads_squared", [P, NT, MW])
        dn = m2("denominators", [P, 4, NT])
        wp = m2("w_pool", [P, PG, P])
        mixT = m2("pool_mixedT", [P, 2, T])
        ybT = m2("pool_outT", [P, PG, T])
        zeros = m2("zeros", [64, T])
        gb_full = [load(gb[:, :, j, :], io[n][0].partition_broadcast(P), down_done)
                   for j, n in ((0, "b_igate_2"), (1, "b_fgate_2"))]
        gh_full = load(gh[:, :], io["g_head_2"].to_broadcast([P, MW]), down_done)
        wp_full = load(wp[:, :, :], io["w_pool_2"][0].rearrange("g c e -> c g e"), down_done)
        pool.wait(down_done)
        m = pool.mark(pool.engine.memset(zeros[:, :], 0.0))
        pool.wait(m)
        m = pool.mark(pool.engine.memset(gp[:, :, :, :], 0.0))
        set2 = pool.mark(pool.engine.memset(vE[:, :, :, E2:E2 + 1], 1.0))
        dve.wait(down_done)
        act.wait(down_done)

        k_scale = {"q2": E2 ** -0.5, "k2": None}
        qk_T = {}

        def qk_work(name, col, dst, marks):
            def work():
                got = []
                for t in range(NT):
                    tiles = [qk[:, t, col + h * P:col + (h + 1) * P] for h in range(H2)]
                    bank, mark = transpose_tiles(tiles, [marks[t]])
                    src = bank.ap[:, :].rearrange("p (k n) -> p k n", k=H2)
                    m = copy_out(act, dst[:, :, t * P:(t + 1) * P], src, [mark], k_scale[name])
                    bank.readers = [m]
                    got.append(m)
                qk_T[name] = got
            return work

        def gates_work(t, marks):
            z = gt[:, t, :, :, :]
            zf = gt[:, t, :, 1, :]
            a, b = small[:, 40:40 + 2 * H2], small[:, 48:48 + 2 * H2]
            a3, b3 = (s.rearrange("p (d h) -> p d h", d=2) for s in (a, b))
            dve.wait(marks, gb_full, set2)
            m = chain(v.tensor_tensor(z.rearrange("p a b c -> p (a b c)"), z.rearrange("p a b c -> p (a b c)"),
                                  gb[:, :, :, :].rearrange("p a b c -> p (a b c)"), ALU.add))
            act.wait(m)
            m = act.mark(act.engine.activation(a3, zf, ACT.Abs))
            act.wait(m)
            m = act.mark(act.engine.activation(b, a, ACT.Exp, scale=-1.0))
            act.wait(m)
            m = act.mark(act.engine.activation(b, b, ACT.Ln, bias=1.0))
            dve.wait(m)
            for d in range(2):
                v.tensor_copy(gp[:, t, 0, 32 * d:32 * d + H2], gt[:, t, d, 0, :])
                m = dve.mark(v.scalar_tensor_tensor(gp[:, t, 1, 32 * d:32 * d + H2], zf[:, d, :], 0.0, b3[:, d, :],
                                                    ALU.min, ALU.subtract))
            dve.wait(m)
            return m

        gp_marks, og_marks, v2_marks, u_marks, so_marks = [], [], [], [[], []], []

        def gates_rows():
            bank = next_bank("aux")
            pe.wait(bank.readers)
            pe.wait(gp_marks)
            for q in range(2):
                for t in range(NT):
                    last = pe.engine.transpose(bank.ap[0:64, (q * NT + t) * P:(q * NT + t + 1) * P], gp[:, t, q, :], ident)
            done = pe.mark(last)
            m = copy_out(act, rows2[:, :, :], bank.ap[0:64, :].rearrange("p (q t) -> p q t", q=2), [done])
            bank.readers = [m]
            dve.wait(m, ones_set, set2)
            fw, bw = slice(0, 32), slice(32, 64)
            b_fw, b_bw = scans[fw, 2, :], scans[bw, 2, ::-1]
            one = ones[0:64, 0:1].to_broadcast([64, T])
            v.tensor_tensor_scan(b_fw, one[fw, :], rows2[fw, 1, :], 0.0, ALU.mult, ALU.add)
            chain(v.tensor_tensor_scan(b_bw, one[bw, :], rows2[bw, 1, ::-1], 0.0, ALU.mult, ALU.add))
            chain(v.tensor_tensor(scans[:, 0, :], rows2[:, 0, :], scans[:, 2, :], ALU.subtract))
            v.tensor_tensor_scan(scans[fw, 1, :], zeros[fw, :], scans[fw, 0, :], 0.0, ALU.max, ALU.max)
            chain(v.tensor_tensor_scan(scans[bw, 1, ::-1], zeros[bw, :], scans[bw, 0, ::-1], 0.0, ALU.max, ALU.max))
            m = chain(v.tensor_tensor(scans[:, 2, :], scans[:, 2, :], scans[:, 1, :], ALU.add))
            bank = next_bank("aux")
            pe.wait(bank.readers)
            pe.wait(m)
            for t in range(NT):
                for q in range(3):
                    last = pe.engine.transpose(bank.ap[:, (t * 3 + q) * 64:(t * 3 + q + 1) * 64],
                                               scans[:, q, t * P:(t + 1) * P], ident[0:64, 0:64])
            done = pe.mark(last)
            src = bank.ap[:, 0:NT * 3 * 64].rearrange("p (t q r) -> p t q r", t=NT, q=3)
            dve.wait(done)
            v.tensor_copy(cols2[:, :, 0, :], src[:, :, 0, :])
            m1 = dve.mark(v.tensor_scalar(cols2[:, :, 1, :], src[:, :, 1, :], -1.0, None, ALU.mult))
            act.wait(done, m1)
            m2_ = act.mark(act.engine.activation(expm[:, :, :], src[:, :, 2, :], ACT.Exp, scale=-1.0))
            bank.readers = [m1, m2_]
            cols_done.extend([m1, m2_])

        cols_done = []
        pool_out = []

        def pooling(g):
            slab = W.chunks["pool_matrix"][0]
            a = W.slab_view(slab).rearrange("p s (g t) -> p s g t", g=PG)
            bank = next_bank("aux")
            pe.wait(bank.readers)
            pe.wait(W.slabs[slab]["landed"], u_marks)
            for s in range(NT):
                last = pe.engine.matmul(bank.ap[:, 0:T], u_pool[:, s, g * P:(g + 1) * P], a[:, s, g, :],
                                        start=s == 0, stop=s == NT - 1)
            done = pe.mark(last)
            if g == PG - 1:
                W.release(slab, done)
            m = copy_out(act, mixT[:, g % 2, :], bank.ap[:, 0:T], [done] + pool_products[-2:-1])
            bank.readers = [m]
            bank = next_bank("aux")
            pe.wait(bank.readers)
            pe.wait(m, wp_full)
            done = pe.mark(pe.engine.matmul(bank.ap[:, 0:T], wp[:, g, :], mixT[:, g % 2, :], start=True, stop=True))
            pool_products.append(done)
            dve.wait(done, vec_ready)
            scaled = dve.mark(v.tensor_scalar(ybT[:, g, :], bank.ap[:, 0:T], vec_cols[:, V_PS + g:V_PS + g + 1], None, ALU.mult))
            bank.readers = [scaled]
            pool_out.append(scaled)

        pool_products = []
        ada_plan2 = {6: (row_c, 0, "copy"), 7: (row_c, 1, "copy"), 8: (row_b, 0, "scale"), 9: (row_b, 1, "scale")}
        for i, (name, c0, n) in enumerate(in2):
            pair = pairs[i % 2]
            done = run(linear(name, uT_h, uT_l, ready, pair))
            marks = []
            for t in range(NT):
                src = pair[t].ap[:, 0:n]
                if name in ("q2", "k2"):
                    col = 0 if name == "q2" else MW
                    m = copy_out(act, qk[:, t, col:col + MW], src, [done])
                elif name == "v2":
                    act.wait(done, set2)
                    m = act.mark(act.engine.activation(vE[:, t, :, 0:E2], src.rearrange("p (h e) -> p h e", h=H2), ACT.Copy))
                    v2_marks.append(m)
                elif name == "o2":
                    act.wait(done)
                    m = act.mark(act.engine.activation(so[:, t, :], src, ACT.Sigmoid))
                    so_marks.append(m)
                elif name == "gu0":
                    m1 = copy_out(dve, gt[:, t, :, :, :].rearrange("p a b c -> p (a b c)"), src[:, 0:NG2], [done])
                    m = copy_out(dve, u_pool[:, t, 0:n - NG2], src[:, NG2:n], [done])
                    u_marks[t].append(m)
                    pair[t].readers = [m]
                    gp_marks.append(gates_work(t, [m1]))
                else:
                    m = copy_out(act, u_pool[:, t, n - NG2:MW], src, [done])
                    u_marks[t].append(m)
                pair[t].readers = [m]
                marks.append(m)
            if name == "q2":
                later.append(qk_work(name, 0, q2T, marks))
            if name == "k2":
                later.append(qk_work(name, MW, k2T, marks))
            if name == "gu0":
                later.append(gates_rows)
            if 1 <= i <= 4:
                dst, half, how = ada_plan2[5 + i]
                ada(5 + i, dst[:, halves[half]], [row_b_full] if how == "scale" else adds, how)
            if name == "gu1":
                later.extend([lambda g=g: pooling(g) for g in range(PG)])
        run_later()
        pool_tail = [done]

        act.wait(pool_out, pool_tail)
        pooled = [act.mark(act.engine.activation(uT_h[:, H2:H2 + PG, :], ybT[:, :, :], ACT.Copy))]
        dve.wait(pooled, pool_tail)
        pooled.append(dve.mark(v.tensor_tensor(uT_l[:, H2:H2 + PG, :], ybT[:, :, :],
                                               uT_h[:, H2:H2 + PG, :].bitcast(F32), ALU.subtract)))

        st_bank = {}
        w_free, s_free = [[], []], [[], []]
        og_done = []
        for t in range(NT):
            dve.wait(so_marks[t], gh_full)
            og_done.append(dve.mark(v.tensor_tensor(so[:, t, :], so[:, t, :], gh[:, :], ALU.mult)))

        def scores2(h):
            bank = acc[h % 2]
            pe.wait(bank.readers)
            pe.wait(qk_T["q2"], qk_T["k2"])
            for s in range(NT):
                last = pe.engine.matmul(bank.ap[:, s * T:(s + 1) * T], k2T[:, h, s * P:(s + 1) * P], q2T[:, h, :],
                                        start=True, stop=True)
            bank.readers = []
            return bank, pe.mark(last)

        def decay(h, d):
            i = 2 * h + d
            r = 32 * d + h
            bank = tr_banks[i % 2]
            pe.wait(bank.readers)
            pe.wait(cols_done, masks_ready)
            for block, t in ((0, 0), (1, 1 - d), (2, 1)):
                pe.engine.matmul(bank.ap[:, block * P:(block + 1) * P], cols2[:, t, 1, r:r + 1].to_broadcast([P, P]), ident,
                                 start=block == 0, stop=False, skip_group_check=True)
            mask = (before_r, after_r)[d]
            diag = bank.ap[:, 0:3 * P].rearrange("p (b n) -> p b n", b=3)[:, ::2, :]
            done = pe.mark(pe.engine.matmul(diag, ident_r[:, :], mask[:, :].unsqueeze(1).to_broadcast([P, 2, P]),
                                            start=False, stop=True, skip_group_check=True))
            act.wait(done, w_free[i % 2])
            edges = ((0, 2 * P, 0), (2 * P, 3 * P, 1)) if d == 0 else ((0, P, 0), (P, 3 * P, 1))
            for a, b, s in edges:
                m = act.mark(act.engine.activation(wT[:, i % 2, a:b], bank.ap[:, a:b], ACT.Exp, bias=cols2[:, s, 0, r:r + 1]))
            bank.readers = [m]
            return m

        def weigh(h, d, sbank, s_mark, w_mark):
            i = 2 * h + d
            dve.wait(s_mark, w_mark, s_free[i % 2])
            st = sbank.ap[:, :].rearrange("p (s t) -> p s t", s=NT)
            parts = (((0, 2 * P), st[:, 0, 0:T]), ((2 * P, 3 * P), st[:, 1, P:T])) if d == 0 else \
                    (((0, P), st[:, 0, 0:P]), ((P, 3 * P), st[:, 1, 0:T]))
            for (a, b), src in parts:
                m = dve.mark(v.tensor_tensor(sT[:, i % 2, a:b], src, wT[:, i % 2, a:b], ALU.mult))
            w_free[i % 2] = [m]
            return m

        def numerators(h, d, mark):
            i = 2 * h + d
            r = 32 * d + h
            bank = aux_banks[i % 2]
            pe.wait(bank.readers)
            pe.wait(mark, v2_marks)
            blocks = {(0, 0): 0, (1, 1): 2, ((0, 1) if d == 0 else (1, 0)): 1}
            W1 = E2 + 1
            for t in range(NT):
                srcs = [s for s in range(NT) if (s, t) in blocks]
                for n, s in enumerate(srcs):
                    b = blocks[(s, t)]
                    last = pe.engine.matmul(bank.ap[:, t * W1:(t + 1) * W1], sT[:, i % 2, b * P:(b + 1) * P],
                                            vE[:, s, h, :], start=n == 0, stop=n == len(srcs) - 1)
            done = pe.mark(last)
            s_free[i % 2] = [done]
            num = bank.ap[:, 0:NT * W1].rearrange("p (t e) -> p t e", t=NT)
            den = dn[:, i % 4, :]
            dve.wait(done, cols_done)
            chain(v.tensor_reduce(den, num[:, :, E2:E2 + 1], AX.X, ALU.max, apply_absolute_value=True))
            chain(v.tensor_tensor(den, den, expm[:, :, r], ALU.max))
            chain(v.reciprocal(den, den))
            for t in range(NT):
                dst = hm[:, t, h * E2:(h + 1) * E2]
                if d == 0:
                    m = chain(v.tensor_scalar(dst, num[:, t, 0:E2], den[:, t:t + 1], None, ALU.mult))
                else:
                    m = chain(v.scalar_tensor_tensor(dst, num[:, t, 0:E2], den[:, t:t + 1], dst, ALU.mult, ALU.add))
            bank.readers = [m]
            return m

        queue = []
        for h in range(H2):
            sbank, s_mark = scores2(h)
            for d in range(2):
                w_mark = decay(h, d)
                m = weigh(h, d, sbank, s_mark, w_mark)
                if d == 1:
                    sbank.readers = [m]
                queue.append((h, d, m))
                if len(queue) > 1:
                    hm_mark = numerators(*queue.pop(0))
        hm_mark = numerators(*queue.pop(0))

        ready_a = []
        for t in range(NT):
            s4 = stat[:, 48 + 4 * t:52 + 4 * t]
            act.wait(hm_mark)
            m = act.mark(act.engine.activation(hsq[:, t, :], hm[:, t, :], ACT.Square))
            dve.wait(m)
            m = dve.mark(v.tensor_reduce(s4, hsq[:, t, :].rearrange("p (h e) -> p h e", h=H2), AX.X, ALU.add))
            r = inverse_rms(s4, E2, H2, m)
            dve.wait(og_done[t])
            m = dve.mark(v.tensor_tensor(hm[:, t, :], hm[:, t, :], so[:, t, :], ALU.mult))
            dve.wait(m, r)
            h3 = hm[:, t, :].rearrange("p (h e) -> p h e", h=H2)
            m = dve.mark(v.tensor_tensor(h3, h3, s4.unsqueeze(2).to_broadcast([P, H2, E2]), ALU.mult))
            ready_a.append(to_features(hm[:, t, :], H2, t, [m], uT_h, uT_l, 0, pool_tail))
        ready_y = ready_of(ready_a)
        ready_y.append([pooled, pooled])
        dump("hm", hm[:, :, :], *[a[0] for a in ready_a])

        def gated_residual(name, ready, in_h, in_l, gate, gate_marks):
            marks = [[], []]
            for i in range(2):
                done = run(linear(f"{name}{i}", in_h, in_l, ready, pairs[i]))
                cols = slice(i * BANK, (i + 1) * BANK)
                for t in range(NT):
                    dve.wait(done, gate_marks)
                    m = chain(v.tensor_tensor(xn[:, t, cols], pairs[i][t].ap[:, :], gate[:, cols], ALU.mult))
                    pairs[i][t].readers = [m]
                    marks[t].append(chain(v.tensor_tensor(x[:, t, cols], x[:, t, cols], xn[:, t, cols], ALU.add)))
            return marks, done

        x_marks, done = gated_residual("w_out2_", ready_y, uT_h, uT_l, row_d, [ada_done[4], ada_done[5]])
        dump("x3", x[:, :, :], *x_marks)
        mix2.close()

        hid2 = ExitStack()
        ctx.enter_context(hid2)
        hid_h = sb("hidden2_high", [P, KF2, T], F32R, stack=hid2)
        hid_l = sb("hidden2_low", [P, KF2, T], F32R, stack=hid2)
        ready, adds = norm_modulate(row_b, [ada_done[8], ada_done[9]], row_c, [ada_done[6], ada_done[7]], x_marks, [done])
        gt1_read = x_marks[0] + x_marks[1]
        hidden_ready = [[], []]
        sq_free = {}
        for i in range(DFF2 // BANK):
            pair = pairs[i % 2]
            f_done = run(linear(f"ff1_{i}", uT_h, uT_l, ready, pair))
            sl = xn[:, :, (i % 2) * BANK:(i % 2 + 1) * BANK]
            for t in range(NT):
                act.wait(f_done)
                m = act.mark(act.engine.activation(sl[:, t, :], pair[t].ap[:, :], ACT.Relu))
                pair[t].readers = [m]
                pool.wait(m)
                m = pool.mark(pool.engine.tensor_tensor(sl[:, t, :], sl[:, t, :], sl[:, t, :], ALU.mult))
                later.append(hidden_T(sl[:, t, :], 4, t, 4 * i, m, None))
            if i in (2, 4):
                j = 10 if i == 2 else 11
                ada(j, row_d[:, halves[j - 10]], gt1_read, "copy")
        run_later()
        hidden_marks = ready_of(hidden_ready)
        x_marks, done = gated_residual("ff2_", hidden_marks, hid_h, hid_l, row_d, [ada_done[10], ada_done[11]])

        stored = sem("result_stored")
        for t in range(NT):
            m = norm_to(xn[:, t, :], t, row_a, row_a_full, x_marks[t], [])
            sp.wait(m)
            nc.sync.dma_start(out[0, t * P:(t + 1) * P, :], xn[:, t, :]).then_inc(stored, 16)
        nc.sync.wait_ge(stored, 16 * NT)
        assert W.issued == len(W.slabs) and not later


_NAMES = ["x", "positions", "attn_norm_g", "w_in", "diff_lambda", "diff_subln_g", "cmp_pe_k", "cmp_pe_v", "cmp_k_w1",
          "cmp_k_w2", "cmp_v_w1", "cmp_v_w2", "w_branch_a", "w_branch_b", "w_out", "ffn_norm_g", "w_gate", "w_up",
          "w_down", "final_norm_g", "c_2", "w_ada_2", "b_ada_2", "g_mix_2", "w_in_2", "b_igate_2", "b_fgate_2",
          "g_head_2", "w_pool_2", "pool_scale_2", "w_out_2", "g_ffn_2", "w_ff1_2", "w_ff2_2", "g_final_2"]


def shape_constants(tokens, head_dim):
    import numpy as np
    tile, cmp_len, cmp_stride, theta, windows = 128, 32, 16, 10000.0, (2, 4, 8, 16)
    n_tiles, n_cmp = tokens // tile, (tokens - cmp_len) // cmp_stride + 1
    part, free = np.arange(tile)[:, None], np.arange(tile)[None, :]
    identity = (part == free).astype(np.float32)
    after = np.where(free > part, np.float32(-1e30), np.float32(0))
    before = np.where(free < part, np.float32(-1e30), np.float32(0))
    inv_freq = (1.0 / theta ** (np.arange(0, head_dim, 2, dtype=np.float32) / np.float32(head_dim))).astype(np.float32)
    inv_freq = np.broadcast_to(inv_freq, (tile, head_dim // 2))
    ends = np.arange(n_cmp) * cmp_stride + cmp_len - 1
    t = np.arange(tokens)
    seen = (ends[None, :] <= t[:, None]).reshape(n_tiles, tile, n_cmp).transpose(1, 0, 2).reshape(tile, -1)
    consts = np.concatenate([identity, after, before, inv_freq, np.where(seen, 0, np.float32(-1e30)), seen], 1)
    pool = np.zeros((tokens, len(windows), tokens), np.float32)
    for g, w in enumerate(windows):
        lo, hi = np.clip(t - w // 2, 0, tokens), np.clip(t + w // 2, 0, tokens)
        inside = (t[:, None] >= lo[None, :]) & (t[:, None] < hi[None, :])
        pool[:, g, :] = inside / (hi - lo)[None, :].astype(np.float32) - np.eye(tokens, dtype=np.float32)
    pool = pool.reshape(n_tiles, tile, -1).transpose(1, 0, 2)
    return np.ascontiguousarray(consts, np.float32), np.ascontiguousarray(pool, np.float32)


def kernel(_debug=None, **inputs):
    import numpy as _np
    import concourse.bacc as _bacc
    from concourse.bass_utils import run_bass_kernel_spmd as _run

    nc = _bacc.Bacc("TRN2", target_bir_lowering=False, num_devices=1)
    arrays = {name: _np.ascontiguousarray(inputs[name]) for name in _NAMES}
    arrays["consts"], arrays["pool_matrix"] = shape_constants(inputs["x"].shape[1], inputs["diff_lambda"].shape[2])
    io = {name: nc.dram_tensor(f"in_{name}", a.shape, mybir.dt.from_np(a.dtype), kind="ExternalInput").ap()
          for name, a in arrays.items()}
    shape = tuple(inputs["x"].shape)
    out = nc.dram_tensor("out", shape, F32, kind="ExternalOutput").ap()
    debug = {n: nc.dram_tensor(f"dbg_{n}", s, F32, kind="ExternalOutput").ap() for n, s in (_debug or {}).items()}
    build(nc, io, out, debug)
    result = _run(nc, [{f"in_{name}": a for name, a in arrays.items()}], core_ids=[0])
    return result.results[0]["out"]
```

```python
from contextlib import ExitStack

import concourse.bass as bass
from concourse import mybir

F32 = mybir.dt.float32
F32R = mybir.dt.float32r
I32 = mybir.dt.int32
ACT = mybir.ActivationFunctionType
ALU = mybir.AluOpType
AX = mybir.AxisListType

P = 128
BANK = 512
SLAB = 2048
RAW_SLABS = 5
UNIT = 1024
SPLIT_UNITS = 4
MASKED = -1e30
NORM_EPS = 1e-6
TWO_PI_PARTS = (6.28125, 0.0019350051879882812, 3.019916050e-07)
MAGIC = 12582912.0
PI_BELOW = 3.1415925


class Lane:

    def __init__(self, engine, semaphore):
        self.engine, self.semaphore = engine, semaphore
        self.count, self.reached = 0, {}

    def mark(self, instruction):
        self.count += 1
        instruction.then_inc(self.semaphore, 1)
        return (self.semaphore, self.count)

    def wait(self, *marks):
        for m in marks:
            if m is None:
                continue
            if isinstance(m, list):
                self.wait(*m)
            elif self.reached.get(id(m[0]), 0) < m[1]:
                self.engine.wait_ge(m[0], m[1])
                self.reached[id(m[0])] = m[1]


class Bank:

    def __init__(self, tensor):
        self.ap, self.readers = tensor, []


class InputReady:

    def __init__(self, marks_by_tile):
        self.marks = marks_by_tile

    def __getitem__(self, group):
        return [marks[group] if group < len(marks) else None for marks in self.marks]


class OutputReady:

    def __init__(self, heads, pooled):
        self.heads, self.pooled = heads, pooled

    def __getitem__(self, group):
        return self.heads if group == 0 else [self.pooled, self.pooled]


class Weights:

    def __init__(self, nc, sp, act, dve, raw, slot_sems, high, low):
        self.nc, self.sp, self.act, self.dve = nc, sp, act, dve
        self.raw, self.slot_sems, self.high, self.low = raw, slot_sems, high, low
        self.slabs, self.units, self.chunks = [], [], {}
        self.issued = self.prepared = 0

    def plan_slab(self, src, kn, n):
        i = len(self.slabs)
        self.slabs.append({"src": src, "kn": kn, "n": n, "released": None, "slot": i % RAW_SLABS,
                           "landed": (self.slot_sems[i % RAW_SLABS], 16 * (i // RAW_SLABS + 1))})
        return i

    def plan_split(self, name, w, c0, n, starts=None, before=None):
        rows = w.shape[0] // P
        units = []
        for k0 in starts or range(0, rows, 4):
            kn = min(4, rows - k0)
            if before and k0 in before:
                before[k0]()
            src = w[k0 * P:(k0 + kn) * P, c0:c0 + n].rearrange("(k p) n -> p k n", p=P)
            i = self.plan_slab(src, kn, n)
            for k in range(0, kn, 2):
                units.append({"slab": i, "at": k, "kn": min(2, kn - k), "n": n, "k0": k0 + k,
                              "last": k + 2 >= kn, "used": None, "index": len(self.units),
                              "opens": not units, "closes": False})
                self.units.append(units[-1])
        units[-1]["closes"] = True
        self.chunks[name] = units

    def plan_raw(self, name, sources):
        self.chunks[name] = [self.plan_slab(src, src.shape[1], src.shape[2]) for src in sources]

    def slab_view(self, i):
        s = self.slabs[i]
        return self.raw[:, s["slot"], 0:s["kn"] * s["n"]].rearrange("p (k n) -> p k n", k=s["kn"])

    def release(self, i, *marks):
        self.slabs[i]["released"] = list(marks)
        self.pump()

    def pump(self):
        while self.issued < len(self.slabs):
            s = self.slabs[self.issued]
            if self.issued >= RAW_SLABS:
                before = self.slabs[self.issued - RAW_SLABS]
                if before["released"] is None:
                    return
                self.sp.wait(before["released"])
            self.sp.engine.dma_start(self.slab_view(self.issued), s["src"]).then_inc(s["landed"][0], 16)
            self.issued += 1

    def prepare_through(self, last):
        while self.prepared <= min(last, len(self.units) - 1):
            u = self.units[self.prepared]
            slab = self.slabs[u["slab"]]
            if u["slab"] >= self.issued:
                return
            src = self.slab_view(u["slab"])[:, u["at"]:u["at"] + u["kn"], :]
            ring, size = self.prepared % SPLIT_UNITS, u["kn"] * u["n"]
            high = self.high[:, ring, 0:size].rearrange("p (k n) -> p k n", k=u["kn"])
            low = self.low[:, ring, 0:size].rearrange("p (k n) -> p k n", k=u["kn"])
            used = self.units[self.prepared - SPLIT_UNITS]["used"] if self.prepared >= SPLIT_UNITS else None
            self.act.wait(slab["landed"], used)
            u["high_ready"] = self.act.mark(self.act.engine.activation(high, src, ACT.Copy))
            self.dve.wait(slab["landed"], u["high_ready"], used)
            u["low_ready"] = self.dve.mark(
                self.dve.engine.tensor_tensor(low, src, high.bitcast(F32), ALU.subtract))
            u["high"], u["low"] = high, low
            self.prepared += 1
            if u["last"]:
                self.release(u["slab"], u["low_ready"])


def build(nc, io, out):
    x_in = io["x"]
    T, D = x_in.shape[1], x_in.shape[2]
    NT = T // P
    KD = D // P
    w_in = io["w_in"][0]
    DH = io["diff_lambda"].shape[2]
    HALF = DH // 2
    DIFF_W = io["w_branch_a"].shape[1]
    DIFF_H = DIFF_W // (2 * DH)
    NSA_W = io["w_branch_b"].shape[1]
    NSA_H = NSA_W // DH
    G = 2
    HPG = NSA_H // G
    KV = G * DH
    N_GATES = 3 * NSA_H
    CMP_LEN, CMP_STRIDE = io["cmp_pe_k"].shape[1], 16
    NC = (T - CMP_LEN) // CMP_STRIDE + 1
    HID = io["cmp_k_w1"].shape[2]
    KH = HID // P
    CMP_J = CMP_LEN * DH // P
    CPAD = 32
    assert CPAD >= NC and CMP_LEN == 2 * CMP_STRIDE and HPG * CPAD == P and 2 * DH == P
    DFF = io["w_gate"].shape[2]
    DFF2 = io["w_ff1_2"].shape[2]
    KF, KF2 = DFF // P, DFF2 // P
    w_in2 = io["w_in_2"][0]
    H2 = io["b_igate_2"].shape[2]
    MW = io["g_head_2"].shape[1]
    E2 = MW // H2
    NG2 = 4 * H2
    PG = io["w_pool_2"].shape[1]
    LAM_INIT = 0.8 - 0.6
    assert NT == 2 and E2 == P and DIFF_H * P == DIFF_W

    O_DQ, O_DK, O_DV, O_NQ = 0, DIFF_W, 2 * DIFF_W, 3 * DIFF_W
    O_KC = O_NQ + NSA_W
    O_VC, O_KS, O_VS, O_KW, O_VW, O_NG = (O_KC + i * KV for i in range(1, 7))
    O_MG = O_NG + N_GATES

    with ExitStack() as ctx:
        def sb(name, shape, dtype=F32, stack=ctx):
            return stack.enter_context(nc.sbuf_tensor(name, shape, dtype))

        def sem(name):
            return ctx.enter_context(nc.semaphore(name))

        pe = Lane(nc.tensor, sem("tensor_done"))
        act = Lane(nc.scalar, sem("scalar_done"))
        dve = Lane(nc.vector, sem("vector_done"))
        pool = Lane(nc.gpsimd, sem("gpsimd_done"))
        sp = Lane(nc.sync, None)
        banks = [Bank(ctx.enter_context(nc.psum_tensor(f"bank{i}", [P, BANK], F32))) for i in range(8)]
        acc, tr_banks, aux_banks = banks[0:4], banks[4:6], banks[6:8]

        raw = sb("raw_weights", [P, RAW_SLABS, SLAB])
        high = sb("weights_high", [P, SPLIT_UNITS, UNIT], F32R)
        low = sb("weights_low", [P, SPLIT_UNITS, UNIT], F32R)
        x = sb("x", [P, NT, D])
        xn = sb("xn", [P, NT, D])
        uT_h = sb("uT_high", [P, KD, T], F32R)
        uT_l = sb("uT_low", [P, KD, T], F32R)
        row_a = sb("row_a", [P, D])
        row_b = sb("row_b", [P, D])
        row_cd = sb("rows_c_d", [P, 2, D])
        row_c, row_d = row_cd[:, 0, :], row_cd[:, 1, :]
        consts = io["consts"]
        cst = sb("constants", [P, consts.shape[1]])
        ident = cst[:, 0:P]
        inv_freq = cst[:, 3 * P:3 * P + HALF]
        o_c = 3 * P + HALF
        cmp_add = cst[:, o_c:o_c + NT * NC].rearrange("p (t c) -> p t c", t=NT)
        cmp_keep = cst[:, o_c + NT * NC:o_c + 2 * NT * NC].rearrange("p (t c) -> p t c", t=NT)
        ident_r = sb("identity_r", [P, P], F32R)
        after_r = sb("mask_free_after_partition", [P, P], F32R)
        before_r = sb("mask_free_before_partition", [P, P], F32R)
        ones = sb("ones", [P, P])
        minus_half = sb("minus_half", [P, 8])
        b_ada = sb("b_ada", [12, BANK])
        ada_acc = sb("ada_acc", [P, 2, BANK])
        vec_rows = sb("vector_rows", [64, P])
        vec_cols = sb("vector_columns", [P, 64])
        c_act = sb("c_act", [P, KD])
        stat = sb("stat", [P, 112])
        small = sb("small", [P, 64])

        slot_sems = [sem(f"raw_slot{i}_landed") for i in range(RAW_SLABS)]
        W = Weights(nc, sp, act, dve, raw, slot_sems, high, low)

        projections = {"kva": (O_KC, 3 * KV), "dq": (O_DQ, DIFF_W), "kvb": (O_VS, 3 * KV + N_GATES),
                       "dk": (O_DK, DIFF_W), "nq": (O_NQ, NSA_W), "dv": (O_DV, DIFF_W)}
        for name, (c0, n) in projections.items():
            W.plan_split(name, w_in, c0, n)
            if name in ("dk", "nq"):
                which = "k" if name == "dk" else "v"
                w1 = io[f"cmp_{which}_w1"][0].rearrange("(j p) n -> p j n", p=P)
                W.plan_raw(f"cmp_{which}", [w1[:, 0:CMP_J // 2, :], w1[:, CMP_J // 2:CMP_J, :]])
        for i in range(4):
            W.plan_split(f"mg{i}", w_in, O_MG + i * BANK, BANK)
        for i in range(2):
            W.plan_split(f"branch_a{i}", io["w_branch_a"][0], i * BANK, BANK)
        for i in range(2):
            W.plan_split(f"branch_b{i}", io["w_branch_b"][0], i * BANK, BANK)
        for i in range(2):
            W.plan_split(f"w_out{i}", io["w_out"][0], i * BANK, BANK)

        def plan_ada(i, part):
            w = io["w_ada_2"][0][:, i * BANK:(i + 1) * BANK].rearrange("(k p) n -> p k n", p=P)
            W.plan_raw(f"ada{i}_{part}", [w[:, 4 * part:4 * part + 4, :]])

        ffn_chunks = [(c0, min(BANK, DFF - c0)) for c0 in range(0, DFF, BANK)]
        assert len(ffn_chunks) == 6 and KD == 8
        for i, (c0, n) in enumerate(ffn_chunks):
            W.plan_split(f"gate{i}", io["w_gate"][0], c0, n)
            plan_ada(i, 0)
            W.plan_split(f"up{i}", io["w_up"][0], c0, n)
            plan_ada(i, 1)
        W.plan_split("down0", io["w_down"][0], 0, BANK)
        plan_ada(6, 0), plan_ada(6, 1)
        W.plan_split("down1", io["w_down"][0], BANK, BANK, before={16: lambda: (plan_ada(7, 0), plan_ada(7, 1))})
        GU = NG2 + MW
        in2 = [("gu0", 4 * MW, GU // 2), ("gu1", 4 * MW + GU // 2, GU // 2), ("q2", 0, BANK), ("k2", MW, BANK),
               ("v2", 2 * MW, BANK), ("o2", 3 * MW, BANK)]
        in2_ada = {0: (8, 0), 1: (8, 1), 3: (9, 0), 4: (9, 1)}
        for i, (name, c0, n) in enumerate(in2):
            W.plan_split(name, w_in2, c0, n)
            if i == 2:
                W.plan_raw("pool_matrix", [io["pool_matrix"]])
            elif i in in2_ada:
                plan_ada(*in2_ada[i])
        for i in range(2):
            W.plan_split(f"w_out2_{i}", io["w_out_2"][0], i * BANK, BANK, starts=(4, 0))
        ff1_ada = {0: (10, 0), 1: (10, 1), 2: (11, 0), 3: (11, 1)}
        for i in range(DFF2 // BANK):
            W.plan_split(f"ff1_{i}", io["w_ff1_2"][0], i * BANK, BANK)
            if i in ff1_ada:
                plan_ada(*ff1_ada[i])
        for i in range(2):
            W.plan_split(f"ff2_{i}", io["w_ff2_2"][0], i * BANK, BANK)

        n_loads = [0]

        def load(dst, src, *marks, queue=None, scattered=False):
            lane = queue or pool
            n_loads[0] += 1
            s = sem(f"load{n_loads[0]}_landed")
            lane.wait(*marks)
            lane.engine.dma_start(dst, src, allow_slow_non_contiguous=scattered).then_inc(s, 16)
            return (s, 16)

        bank_turn = {"tr": 0, "aux": 0}

        def next_bank(kind):
            group = {"tr": tr_banks, "aux": aux_banks}[kind]
            bank_turn[kind] += 1
            return group[bank_turn[kind] % len(group)]

        later = []

        def put_off(steps, *works):
            later.extend([steps, w] for w in works)

        def tick():
            for entry in later:
                entry[0] -= 1
            due = [entry for entry in later if entry[0] <= 0]
            later[:] = [entry for entry in later if entry[0] > 0]
            for _, work in due:
                work()

        def run_later():
            while later:
                entry = min(later, key=lambda e: e[0])
                later.remove(entry)
                entry[1]()

        def linear(name, in_h, in_l, ready, banks_by_tile, evacuate, k_first=0):
            units = W.chunks[name]
            for first in range(0, len(units), SPLIT_UNITS):
                group = units[first:first + SPLIT_UNITS]
                for t in range(NT):
                    ts = slice(t * P, (t + 1) * P)
                    for u in group:
                        W.prepare_through(u["index"])
                        assert W.prepared > u["index"]
                        if u["opens"]:
                            pe.wait(banks_by_tile[t].readers)
                        pe.wait(u["high_ready"], u["low_ready"])
                        dst = banks_by_tile[t].ap[:, 0:u["n"]]
                        for j in range(u["kn"]):
                            k = u["k0"] + j
                            assert ready[k // 4][t] is not None
                            pe.wait(ready[k // 4][t])
                            xh, xl = in_h[:, k_first + k, ts], in_l[:, k_first + k, ts]
                            wh, wl = u["high"][:, j, :], u["low"][:, j, :]
                            start, stop = u["opens"] and j == 0, u["closes"] and j == u["kn"] - 1
                            pe.engine.matmul(dst, xh, wh, start=start, stop=False)
                            pe.engine.matmul(dst, xl, wh, start=False, stop=False)
                            last = pe.engine.matmul(dst, xh, wl, start=False, stop=stop)
                        mark = pe.mark(last)
                        if t == NT - 1:
                            u["used"] = mark
                            W.prepare_through(u["index"] + SPLIT_UNITS)
                        if u["closes"]:
                            evacuate(t, mark)
                        tick()
                        yield mark

        def run(chunk):
            done = None
            for done in chunk:
                pass
            return done

        def transpose_tiles(sources, marks, kind="tr"):
            bank = next_bank(kind)
            pe.wait(bank.readers)
            pe.wait(*marks)
            for i, s in enumerate(sources):
                last = pe.engine.transpose(bank.ap[0:s.shape[1], i * P:i * P + s.shape[0]], s,
                                           ident[0:s.shape[0], 0:s.shape[0]])
            return bank, pe.mark(last)

        def split_from(bank, mark, dst_h, dst_l, free, shape=None):
            n = dst_h.shape[1]
            src = bank.ap[:, 0:n * P].rearrange("p (k n) -> p k n", k=n)
            act.wait(mark, *free)
            h = act.mark(act.engine.activation(dst_h, src, ACT.Copy))
            dve.wait(mark, h, *free)
            l = dve.mark(dve.engine.tensor_tensor(dst_l, src, dst_h.bitcast(F32), ALU.subtract))
            bank.readers = [h, l]
            return [h, l]

        def to_features(tile, n, t, marks, in_h, in_l, k0, free):
            out_marks = []
            for g in range(0, n, 4):
                m = min(4, n - g)
                bank, mark = transpose_tiles([tile[:, (g + i) * P:(g + i + 1) * P] for i in range(m)], marks)
                dst = slice(k0 + g, k0 + g + m)
                out_marks.append(split_from(bank, mark, in_h[:, dst, t * P:(t + 1) * P],
                                            in_l[:, dst, t * P:(t + 1) * P], free))
            return out_marks

        stat_at = [0]

        def columns(n):
            stat_at[0] += n
            return stat[:, stat_at[0] - n:stat_at[0]]

        def inverse_rms(sums, width, count, mark):
            pool.wait(mark)
            m = pool.mark(pool.engine.tensor_scalar(sums, sums, 1.0 / width, NORM_EPS, ALU.mult, ALU.add))
            pool.wait(m)
            return pool.mark(pool.engine.tensor_tensor(sums, sums, minus_half[:, 0:count], ALU.pow))

        def half(h):
            return slice(h * BANK, (h + 1) * BANK)

        def square_half(t, h, sums, mark, unused, src=None):
            src = x[:, t, half(h)] if src is None else src
            act.wait(mark)
            return act.mark(act.engine.activation(unused, src, ACT.Square, scale=D ** -0.5,
                                                  accum_out=sums[:, h:h + 1]))

        def scale_from(sums, marks):
            col = columns(1)
            dve.wait(*marks)
            m = dve.mark(v.tensor_scalar(col, sums[:, 0:1], sums[:, 1:2], NORM_EPS, ALU.add, ALU.add))
            pool.wait(m, half_set)
            return col, pool.mark(pool.engine.tensor_tensor(col, col, minus_half[:, 0:1], ALU.pow))

        def norm_tile(t, stats, row, row_marks, out, read, free=(), shift=None, shift_marks=(), steps=2):
            sums, marks = stats
            col, ready = scale_from(sums, marks)
            for h in range(2):
                dve.wait(ready, *row_marks)
                m = dve.mark(v.scalar_tensor_tensor(xn[:, t, half(h)], x[:, t, half(h)], col, row[:, half(h)],
                                                    ALU.mult, ALU.mult))
                if shift is not None:
                    dve.wait(m, *shift_marks)
                    m = dve.mark(v.tensor_tensor(xn[:, t, half(h)], xn[:, t, half(h)], shift[:, half(h)], ALU.add))
                read.append(m)
                put_off(steps + h, turned(xn[:, t, half(h)], t, m, uT_h, uT_l, 4 * h, free, out))

        def turned(tile, t, mark, in_h, in_l, k0, free, out):
            def work():
                out[t].extend(to_features(tile, tile.shape[1] // P, t, [mark], in_h, in_l, k0, free))
            return work

        def ready_of(marks_by_tile):
            return [[marks_by_tile[t][g] for t in range(NT)] for g in range(len(marks_by_tile[0]))]

        v = dve.engine

        def chain(ins):
            m = dve.mark(ins)
            dve.wait(m)
            return m

        x_landed = [load(x[:, t, :], x_in[0, t * P:(t + 1) * P, :], queue=sp) for t in range(NT)]
        cst_landed = load(cst[:, :], consts, queue=sp)
        row_a_full = load(row_a[:, :], io["attn_norm_g"].to_broadcast([P, D]), queue=sp)
        W.pump()
        ones_set = pool.mark(pool.engine.memset(ones[:, :], 1.0))
        half_set = pool.mark(pool.engine.memset(minus_half[:, :], -0.5))
        pool.wait(half_set)
        rows_zero = pool.mark(pool.engine.memset(vec_rows[:, :], 0.0))
        pool.wait(rows_zero)
        pos_i = sb("positions_int", [P, NT], I32)
        pos_landed = load(pos_i[:, :], io["positions"][0].rearrange("(t p) -> p t", p=P), scattered=True)
        lam_rows = sb("lambda_rows", [P, 4, DH])
        lam_landed = load(lam_rows[:, :, :], io["diff_lambda"][0].partition_broadcast(P))
        V_PEK, V_PEV, V_C, V_PS = 0, CMP_J, 2 * CMP_J, 2 * CMP_J + KD
        vecs = [load(vec_rows[V_PEK:V_PEK + CMP_J, :], io["cmp_pe_k"][0].rearrange("(j a) d -> j (a d)", a=2), rows_zero),
                load(vec_rows[V_PEV:V_PEV + CMP_J, :], io["cmp_pe_v"][0].rearrange("(j a) d -> j (a d)", a=2), rows_zero),
                load(vec_rows[V_C:V_C + KD, :], io["c_2"].rearrange("a (k p) -> (a k) p", p=P), rows_zero),
                load(vec_rows[V_PS:V_PS + PG, :], io["pool_scale_2"].rearrange("a (k p) -> (a k) p", p=P), rows_zero)]
        row_b_full = load(row_b[:, :], io["ffn_norm_g"].to_broadcast([P, D]))
        b_ada_landed = load(b_ada[:, :], io["b_ada_2"].rearrange("a (k n) -> (a k) n", n=BANK))

        mixer = ExitStack()
        ctx.enter_context(mixer)

        def mb(name, shape, dtype=F32):
            return sb(name, shape, dtype, stack=mixer)

        pj = mb("projected", [P, NT, O_MG])
        mg = mb("merge_gates", [P, NT, 2 * D])
        dqT = mb("diff_qT", [P, DIFF_H, 2, T])
        dkT = mb("diff_kT", [P, DIFF_H, T])
        nqT = mb("nsa_qT", [P, HPG, T])
        kswT = mb("nsa_kT", [P, 2, T])
        E = row_cd[:, :, :].rearrange("p a (b n) -> p (a b) n", n=BANK)
        PT = mb("probsT", [P, 3, BANK])
        pcT = mb("cmp_probsT", [P, NT, G * P])
        g_sub = mb("subln_row", [P, P])
        w2k = mb("cmp_k_w2", [P, KH, DH])
        w2v = mb("cmp_v_w2", [P, KH, DH])
        cosT = mb("cos", [P, NT, 2, HALF])
        sinT = mb("sin", [P, NT, 2, HALF])
        g_sub_full = load(g_sub[:, :], io["diff_subln_g"].to_broadcast([P, P]))
        w2_full = [load(w2k[:, :, :], io["cmp_k_w2"][0].rearrange("(k p) n -> p k n", p=P)),
                   load(w2v[:, :, :], io["cmp_v_w2"][0].rearrange("(k p) n -> p k n", p=P))]
        x2T = mg[:, 0, D:2 * D].rearrange("p (g v t) -> p g v t", g=G, v=2)
        blk = mg[:, 1, D:D + 2 * CMP_J * G * NC].rearrange("p (v j c) -> p v j c", v=2, j=CMP_J)
        hv4 = mb("cmp_hidden_spread", [P, G, KH, HPG, CPAD])
        vbd = mb("cmp_v_blocks", [P, G, HPG, DH])
        cmp_f = mb("cmp_small", [P, 2, 2 * KH * G * NC])
        kcd = mb("cmp_kT", [P, NC])
        pc = mb("cmp_probs", [P, NT, NSA_H, CPAD])

        x_ready, row_a_read = [[], []], []
        pe.wait(cst_landed)
        for t in range(NT):
            sums = columns(2)
            marks = [square_half(t, h, sums, x_landed[t], xn[:, t, half(h)]) for h in range(2)]
            norm_tile(t, (sums, marks), row_a, [row_a_full], x_ready, row_a_read)
            run_later()
            W.prepare_through(2 * t + 1)
        u_ready = InputReady(x_ready)
        row_a_full = load(row_a[:, :], io["final_norm_g"].unsqueeze(0).to_broadcast([P, D]), *row_a_read)

        act.wait(cst_landed)
        act.engine.activation(ident_r[:, :], ident, ACT.Copy)
        act.engine.activation(after_r[:, :], cst[:, P:2 * P], ACT.Copy)
        masks_ready = act.mark(act.engine.activation(before_r[:, :], cst[:, 2 * P:3 * P], ACT.Copy))

        dve.wait(pos_landed, cst_landed)
        chain(v.tensor_copy(small[:, 0:NT], pos_i[:, :]))
        ang = E[:, 0, 0:NT * 2 * HALF].rearrange("p (t s d) -> p t s d", t=NT, s=2)
        turns = E[:, 1, 0:NT * 2 * HALF].rearrange("p (t s d) -> p t s d", t=NT, s=2)
        for t in range(NT):
            for s_ in range(2):
                m = dve.mark(v.tensor_scalar(ang[:, t, s_, :], inv_freq, small[:, t:t + 1], None, ALU.mult))
        dve.wait(m)
        for s_, quarter in ((0, 0.25), (1, 0.0)):
            m = dve.mark(v.tensor_scalar(turns[:, :, s_, :], ang[:, :, s_, :], 0.15915494309189535, quarter,
                                         ALU.mult, ALU.add))
        dve.wait(m)
        chain(v.tensor_scalar(turns[:, :, :, :], turns[:, :, :, :], MAGIC, None, ALU.add))
        chain(v.tensor_scalar(turns[:, :, :, :], turns[:, :, :, :], MAGIC, None, ALU.subtract))
        for part in TWO_PI_PARTS:
            chain(v.scalar_tensor_tensor(ang[:, :, :, :], turns[:, :, :, :], -part, ang[:, :, :, :], ALU.mult, ALU.add))
        chain(v.tensor_scalar(ang[:, :, 0, :], ang[:, :, 0, :], 1.5707963267948966, None, ALU.add))
        ang_ready = chain(v.tensor_scalar(ang[:, :, :, :], ang[:, :, :, :], PI_BELOW, -PI_BELOW, ALU.min, ALU.max))
        act.wait(ang_ready)
        for h in range(2):
            act.engine.activation(cosT[:, :, h, :], ang[:, :, 0, :], ACT.Sin)
            rope_ready = act.mark(act.engine.activation(sinT[:, :, h, :], ang[:, :, 1, :], ACT.Sin))
        dve.wait(rope_ready)
        rope_ready = [rope_ready, chain(v.tensor_scalar(sinT[:, :, 0, :], sinT[:, :, 0, :], -1.0, None, ALU.mult))]
        W.prepare_through(3)

        def lambda_and_vectors():
            dve.wait(lam_landed)
            lam_pair = lam_rows[:, :, :].rearrange("p (a b) d -> p a b d", a=2)
            chain(v.tensor_tensor(lam_rows[:, 0:2, :], lam_pair[:, :, 0, :], lam_pair[:, :, 1, :], ALU.mult))
            m = chain(v.tensor_reduce(small[:, 2:4], lam_rows[:, 0:2, :], AX.X, ALU.add))
            act.wait(m)
            m = act.mark(act.engine.activation(small[:, 4:6], small[:, 2:4], ACT.Exp))
            dve.wait(m)
            chain(v.tensor_tensor(small[:, 6:7], small[:, 5:6], small[:, 4:5], ALU.subtract))
            marks["lambda"] = chain(v.tensor_scalar(neg_lam, neg_lam, -LAM_INIT, None, ALU.add))

            bank, m = transpose_tiles([vec_rows[:, :]], [rows_zero] + vecs)
            dve.wait(m)
            marks["vectors"] = chain(v.tensor_copy(vec_cols[:, :], bank.ap[:, 0:64]))
            bank.readers = [marks["vectors"]]
            c_col = vec_cols[:, V_C:V_C + KD]
            act.wait(marks["vectors"])
            m = act.mark(act.engine.activation(small[:, 8:8 + KD], c_col, ACT.Exp, scale=-1.0))
            dve.wait(m)
            chain(v.tensor_scalar(small[:, 8:8 + KD], small[:, 8:8 + KD], 1.0, None, ALU.add))
            chain(v.reciprocal(small[:, 8:8 + KD], small[:, 8:8 + KD]))
            marks["c"] = chain(v.tensor_tensor(c_act[:, :], c_col, small[:, 8:8 + KD], ALU.mult))

        marks = {}
        neg_lam = small[:, 6:7]
        put_off(3, lambda_and_vectors)

        rope_free = [[], []]

        def rope(bank, mark, c0, n, t, dst):
            heads = n // DH
            src = bank.ap[:, c0:c0 + n].rearrange("p (h s d) -> p h s d", h=heads, s=2)
            straight = E[:, 2 * t, c0:c0 + n]
            crossed = E[:, 2 * t + 1, c0:c0 + n]
            pairs_of = lambda a: a.rearrange("p (h s d) -> p h s d", h=heads, s=2)
            cos = cosT[:, t, :, :].unsqueeze(1).to_broadcast([P, heads, 2, HALF])
            sin = sinT[:, t, :, :].unsqueeze(1).to_broadcast([P, heads, 2, HALF])
            dve.wait(mark, rope_ready, rope_free[t])
            v.tensor_tensor(pairs_of(straight), src, cos, ALU.mult)
            m = dve.mark(v.tensor_tensor(pairs_of(crossed), src[:, :, ::-1, :], sin, ALU.mult))
            pool.wait(m)
            if len(dst.shape) == 4:
                straight, crossed = (s.rearrange("p (g j d) -> p g j d", g=G, d=DH) for s in (straight, crossed))
            done = pool.mark(pool.engine.tensor_tensor(dst, straight, crossed, ALU.add))
            return m, done

        def copy_out(lane, dst, src, marks, scale=None):
            lane.wait(*marks)
            if lane is act:
                if scale is None:
                    return act.mark(act.engine.activation(dst, src, ACT.Copy))
                return act.mark(act.engine.activation(dst, src, ACT.Copy, scale=scale))
            if scale is None:
                return dve.mark(v.tensor_copy(dst, src))
            return dve.mark(v.tensor_scalar(dst, src, scale, None, ALU.mult))

        dq_zero = pool.mark(pool.engine.memset(dqT[:, :, :, :], 0.0))
        proj_done = {name: [None, None] for name in ("dq", "dk", "dv", "nq", "kc", "vc", "ks", "vs", "kw", "gates",
                                                     "dqT", "dkT", "nqT")}
        pairs = [acc[0:2], acc[2:4]]
        Q_SCALE = DH ** -0.5

        def heads_T(name, t, c0, n_tiles, dst, scale):
            def work():
                tiles = [pj[:, t, c0 + i * P:c0 + (i + 1) * P] for i in range(n_tiles)]
                bank, mark = transpose_tiles(tiles, [proj_done[name][t]])
                src = bank.ap[:, 0:n_tiles * P].rearrange("p (k n) -> p k n", k=n_tiles)
                ts = slice(t * P, (t + 1) * P)
                if name == "dq":
                    for c in range(2):
                        rows = slice(c * DH, (c + 1) * DH)
                        m = copy_out(act, dst[rows, :, c, ts], src[rows, :, :], [mark, dq_zero], scale)
                else:
                    m = copy_out(act, dst[:, :, ts], src, [mark], scale)
                bank.readers = [m]
                proj_done[name + "T"][t] = m
            return work

        rotated = {"dq": (O_DQ, dqT, Q_SCALE), "dk": (O_DK, dkT, None), "nq": (O_NQ, nqT, Q_SCALE)}

        def evacuate_heads(name, pair):
            c0, dst_T, scale = rotated[name]

            def work(t, done):
                dst = pj[:, t, c0:c0 + BANK]
                if name == "nq":
                    dst = dst.rearrange("p (j g d) -> p g j d", g=G, d=DH)
                read, proj_done[name][t] = rope(pair[t], done, 0, BANK, t, dst)
                pair[t].readers = [read]
                rope_free[t] = [proj_done[name][t]]
                put_off(3, heads_T(name, t, c0, 4, dst_T, scale))
            return work

        def evacuate_kva(pair):
            def work(t, done):
                m1, proj_done["kc"][t] = rope(pair[t], done, 0, KV, t, pj[:, t, O_KC:O_KC + KV])
                m2, proj_done["ks"][t] = rope(pair[t], done, 2 * KV, KV, t, pj[:, t, O_KS:O_KS + KV])
                m3 = copy_out(act, pj[:, t, O_VC:O_VC + KV], pair[t].ap[:, KV:2 * KV], [done, m2])
                pair[t].readers = [m2, m3]
                rope_free[t] = [proj_done["ks"][t]]
                proj_done["vc"][t] = m3
                if t == NT - 1:
                    put_off(3, sources_T)
                    put_off(7, compress_blocks)
            return work

        def evacuate_kvb(pair):
            def work(t, done):
                m1, proj_done["kw"][t] = rope(pair[t], done, KV, KV, t, pj[:, t, O_KW:O_KW + KV])
                m2 = copy_out(act, pj[:, t, O_VS:O_VS + KV], pair[t].ap[:, 0:KV], [done, m1])
                m3 = copy_out(act, pj[:, t, O_VW:O_VW + KV + N_GATES], pair[t].ap[:, 2 * KV:3 * KV + N_GATES], [done])
                pair[t].readers = [m1, m3]
                rope_free[t] = [proj_done["kw"][t]]
                proj_done["vs"][t] = m3
                act.wait(m3)
                m = act.mark(act.engine.activation(gates[t], gates[t], ACT.Exp, scale=-1.0))
                dve.wait(m)
                chain(v.tensor_scalar(gates[t], gates[t], 1.0, None, ALU.add))
                proj_done["gates"][t] = chain(v.reciprocal(gates[t], gates[t]))
                if t == NT - 1:
                    put_off(3, keys_T)
            return work

        def evacuate_dv(pair):
            def work(t, done):
                proj_done["dv"][t] = copy_out(act, pj[:, t, O_DV:O_DV + DIFF_W], pair[t].ap[:, :], [done])
                pair[t].readers = [proj_done["dv"][t]]
            return work

        gates = [pj[:, t, O_NG:O_NG + N_GATES] for t in range(NT)]
        ksw_done, x2_done, blk_done = [], [], []

        def sources_T():
            tiles = [pj[:, t, c:c + KV] for c in (O_KC, O_VC) for t in range(NT)]
            bank, mark = transpose_tiles(tiles, proj_done["kc"] + proj_done["vc"])
            src = bank.ap[:, :].rearrange("p (v t) -> p v t", v=2)
            got = []
            for g in range(G):
                got.append(copy_out(act, x2T[0:DH, g, :, :], src[g * DH:(g + 1) * DH, :, :], [mark]))
            for g in range(G):
                got.append(copy_out(dve, x2T[DH:P, g, :, 0:T - 1], src[g * DH:(g + 1) * DH, :, 1:T], [mark, got[1]]))
            bank.readers = got
            x2_done.extend(got)

        def keys_T():
            tiles = [pj[:, t, c:c + KV] for c in (O_KS, O_KW) for t in range(NT)]
            bank, mark = transpose_tiles(tiles, proj_done["ks"] + proj_done["kw"])
            m = copy_out(act, kswT[:, :, :], bank.ap[:, :].rearrange("p (w t) -> p w t", w=2), [mark])
            bank.readers = [m]
            ksw_done.append(m)

        def compress_blocks():
            pool.engine.memset(hv4[:, :, :, :, :], 0.0)
            pool.engine.memset(vbd[:, :, :, :], 0.0)
            marks["cmp_zero"] = pool.mark(pool.engine.memset(pc[:, :, :, :], 0.0))
            for kv in range(2):
                for g in range(G):
                    by = x2T[:, g, kv, :].rearrange("p (n j a) -> p j n a", j=CMP_J // 2, a=2)
                    for part in range(2):
                        js = slice(part * (CMP_J // 2), (part + 1) * (CMP_J // 2))
                        pe_col = vec_cols[:, (V_PEK, V_PEV)[kv] + js.start:(V_PEK, V_PEV)[kv] + js.stop]
                        pool.wait(x2_done, marks["vectors"])
                        blk_done.append(pool.mark(pool.engine.tensor_tensor(
                            blk[:, kv, js, g * NC:(g + 1) * NC], by[:, :, part:part + NC, 0],
                            pe_col.unsqueeze(2).to_broadcast([P, CMP_J // 2, NC]), ALU.add)))

        hid_n = KH * G * NC
        hT = {}

        def hidden_layer(kv):
            bank = next_bank("aux")
            pre = bank.ap[:, 0:hid_n]
            hid = pre.rearrange("p (m c) -> p m c", m=KH)
            pe.wait(bank.readers)
            slabs = W.chunks["cmp_" + "kv"[kv]]
            pe.wait(blk_done[4 * kv + 3], *[W.slabs[i]["landed"] for i in slabs])
            for m_ in range(KH):
                for j in range(CMP_J):
                    w1 = W.slab_view(slabs[j // (CMP_J // 2)])[:, j % (CMP_J // 2), m_ * P:(m_ + 1) * P]
                    last = pe.engine.matmul(hid[:, m_, :], w1, blk[:, kv, j, :], start=j == 0, stop=j == CMP_J - 1)
            done = pe.mark(last)
            for i in slabs:
                W.release(i, done)
            expo, hidden = cmp_f[:, 0, kv * hid_n:(kv + 1) * hid_n], cmp_f[:, 1, kv * hid_n:(kv + 1) * hid_n]
            act.wait(done)
            m = act.mark(act.engine.activation(expo, pre, ACT.Exp, scale=-1.0))
            dve.wait(m, done)
            chain(v.tensor_scalar(expo, expo, 1.0, None, ALU.add))
            chain(v.reciprocal(expo, expo))
            m = chain(v.tensor_tensor(hidden, pre, expo, ALU.mult))
            bank.readers = [m]
            hT[kv] = hidden.rearrange("p (m g c) -> p m g c", m=KH, g=G)
            marks[f"hid{kv}"] = m
            if kv == 1:
                dve.wait(marks["cmp_zero"])
                for g in range(G):
                    for m_ in range(KH):
                        marks["hv4"] = dve.mark(v.tensor_copy(hv4[:, g, m_, :, 0:NC],
                                                              hT[1][:, m_, g, :].unsqueeze(1).to_broadcast([P, HPG, NC])))

        def compressed_kv():
            bank = next_bank("aux")
            pe.wait(bank.readers)
            pe.wait(marks["hid0"], marks["hv4"], w2_full)
            for g in range(G):
                for m_ in range(KH):
                    pe.engine.matmul(bank.ap[g * DH:(g + 1) * DH, 0:NC], w2k[:, m_, :], hT[0][:, m_, g, :],
                                     start=m_ == 0, stop=m_ == KH - 1)
            for g in range(G):
                for m_ in range(KH):
                    last = pe.engine.matmul(bank.ap[:, 64 + g * DH:64 + (g + 1) * DH],
                                            hv4[:, g, m_, :, :], w2v[:, m_, :], start=m_ == 0, stop=m_ == KH - 1)
            done = pe.mark(last)
            marks["kcd"] = copy_out(act, kcd[:, :], bank.ap[:, 0:NC], [done])
            vals = bank.ap[:, 64:64 + G * DH].rearrange("p (g d) -> p g d", g=G)
            dve.wait(done, marks["kcd"])
            for j in range(HPG):
                rows = slice(j * CPAD, (j + 1) * CPAD)
                marks["vbd"] = dve.mark(v.tensor_copy(vbd[rows, :, j, :], vals[rows, :, :]))
            bank.readers = [marks["kcd"], marks["vbd"]]

        evacuate = {"kva": evacuate_kva, "kvb": evacuate_kvb, "dv": evacuate_dv}
        for i, name in enumerate(projections):
            pair = pairs[i % 2]
            empty = evacuate[name](pair) if name in evacuate else evacuate_heads(name, pair)
            if name in ("dk", "nq"):
                put_off(4, lambda kv=("dk", "nq").index(name): hidden_layer(kv))
            if name == "dv":
                put_off(4, compressed_kv)
            run(linear(name, uT_h, uT_l, u_ready, pair, empty))

        mg_done = {}
        xa_done = {}

        def filler_chunks():
            for i in range(4):
                pair = pairs[0]

                def empty(t, done, i=i, pair=pair):
                    mg_done[i, t] = copy_out(act, mg[:, t, half(i)], pair[t].ap[:, :],
                                             [done] + ([blk_done[-1], marks["hid1"]] if i >= 2 else []))
                    pair[t].readers = [mg_done[i, t]]
                for mark in linear(f"mg{i}", uT_h, uT_l, u_ready, pair, empty):
                    yield mark
            marks["gates_products"] = mark
            ready_a = ready_of([to_features(pj[:, t, O_DQ:O_DQ + DIFF_W], 4, t, [ya_done[t]], uT_h, uT_l, 0, [mark])
                                for t in range(NT)])
            yield mark
            for i in range(2):
                def empty(t, done, i=i, pair=pairs[0]):
                    xa_done[i, t] = copy_out(act, xn[:, t, half(i)], pair[t].ap[:, :], [done])
                    pair[t].readers = [xa_done[i, t]]
                for mark in linear(f"branch_a{i}", uT_h, uT_l, ready_a, pairs[0], empty):
                    yield mark
            marks["branch_a_products"] = mark

        filler = filler_chunks()

        def fill(n=1):
            for _ in range(n):
                next(filler, None)

        e_free, pt_free = [[] for _ in range(4)], [[] for _ in range(3)]
        e_free[0] = e_free[1] = rope_free[0]
        e_free[2] = e_free[3] = rope_free[1]
        sums4 = mb("score_sums", [P, 4, 2])
        nmax = mb("score_negmax", [P, 4, 2])
        inv = mb("score_scales", [P, 4, 2])
        o_banks = [acc[2], acc[3]]
        ya_done, yb_done = [None, None], [None, None]
        state = {}

        def item_scores(n, kind, h, q):
            width = (q + 1) * P
            bank = next_bank("aux")
            s = bank.ap[:, 0:2 * width].rearrange("p (c w) -> p c w", c=2)
            pe.wait(bank.readers)
            pe.wait(masks_ready)
            if kind == "diff":
                pe.wait(*proj_done["dqT"], *proj_done["dkT"])
                for c in range(2):
                    pe.engine.matmul(s[:, c, :], dqT[:, h, c, q * P:(q + 1) * P], dkT[:, h, 0:width],
                                     start=c == 0, stop=False, skip_group_check=True)
            else:
                pe.wait(*proj_done["nqT"], ksw_done)
                rows = slice((h // HPG) * DH, (h // HPG + 1) * DH)
                pe.engine.matmul(s, nqT[rows, h % HPG, q * P:(q + 1) * P], kswT[rows, :, 0:width],
                                 start=True, stop=False, skip_group_check=True)
            done = pe.mark(pe.engine.matmul(s[:, :, width - P:width], ident_r[:, :],
                                            after_r[:, :].unsqueeze(1).to_broadcast([P, 2, P]),
                                            start=False, stop=True, skip_group_check=True))
            dve.wait(done)
            max_ready = dve.mark(v.tensor_reduce(nmax[:, n % 4, :], s, AX.X, ALU.max, negate=True))
            e = E[:, n % 4, 0:2 * width].rearrange("p (c w) -> p c w", c=2)
            act.wait(done, max_ready, e_free[n % 4])
            for c in range(2):
                m = act.mark(act.engine.activation(e[:, c, :], s[:, c, :], ACT.Exp, bias=nmax[:, n % 4, c:c + 1],
                                                   accum_out=sums4[:, n % 4, c:c + 1]))
            bank.readers = [m]
            state[n] = {"e": e, "exp": m}

        def item_weights(n, kind, h, q):
            st = state[n]
            e, r = st["e"], inv[:, n % 4, :]
            dve.wait(st["exp"])
            chain(v.reciprocal(r, sums4[:, n % 4, :]))
            if kind == "diff":
                dve.wait(marks["lambda"])
                chain(v.tensor_scalar(e[:, 1, :], e[:, 1, :], r[:, 1:2], neg_lam, ALU.mult, ALU.mult))
                st["w"] = dve.mark(v.scalar_tensor_tensor(e[:, 0, :], e[:, 0, :], r[:, 0:1], e[:, 1, :], ALU.mult, ALU.add))
            else:
                dve.wait(proj_done["gates"][q])
                for c in range(2):
                    gate = gates[q][:, (1 + c) * NSA_H + h:(1 + c) * NSA_H + h + 1]
                    st["w"] = dve.mark(v.tensor_scalar(e[:, c, :], e[:, c, :], r[:, c:c + 1], gate, ALU.mult, ALU.mult))

        def item_transposes(n, kind, h, q):
            st = state[n]
            st["tiles"] = [(c, b) for c in range(1 if kind == "diff" else 2) for b in range(q + 1)]
            bank, mark = transpose_tiles([st["e"][:, c, b * P:(b + 1) * P] for c, b in st["tiles"]], [st["w"]])
            e_free[n % 4] = [mark]
            size = len(st["tiles"]) * P
            st["pT"] = copy_out(act, PT[:, n % 3, 0:size], bank.ap[:, 0:size], [mark] + pt_free[n % 3])
            bank.readers = [st["pT"]]

        def item_values(n, kind, h, q):
            st = state[n]
            pT = PT[:, n % 3, :].rearrange("p (b q) -> p b q", q=P)
            if kind == "nsa" and h == 0:
                open_values(q)
            pe.wait(st["pT"], *proj_done["dv"], *proj_done["vs"])
            if h == 0 and kind == "diff":
                pe.wait(o_banks[q].readers)
            for i, (c, b) in enumerate(st["tiles"]):
                if kind == "diff":
                    last = pe.engine.matmul(o_banks[q].ap[:, h * P:(h + 1) * P], pT[:, i, :],
                                            pj[:, b, O_DV + h * P:O_DV + (h + 1) * P], start=i == 0, stop=b == q)
                else:
                    c0 = (O_VS, O_VW)[c] + (h // HPG) * DH
                    last = pe.engine.matmul(o_banks[q].ap[:, h * DH:(h + 1) * DH], pT[:, i, :], pj[:, b, c0:c0 + DH],
                                            start=False, stop=i == len(st["tiles"]) - 1, skip_group_check=True)
            mark = pe.mark(last)
            pt_free[n % 3] = [mark]
            if kind == "diff" and h == DIFF_H - 1:
                sublayer_norm(q, mark)
            if kind == "nsa" and h == NSA_H - 1:
                yb_done[q] = copy_out(act, pj[:, q, O_NQ:O_NQ + NSA_W], o_banks[q].ap[:, :], [mark])
                o_banks[q].readers = [yb_done[q]]

        def sublayer_norm(t, mark):
            heads = lambda a: a.rearrange("p (h e) -> p h e", h=DIFF_H)
            src, y, sq = o_banks[t].ap[:, :], pj[:, t, O_DQ:O_DQ + DIFF_W], pj[:, t, O_DK:O_DK + DIFF_W]
            s4 = columns(4)
            act.wait(mark)
            m = act.mark(act.engine.activation(sq, src, ACT.Square))
            dve.wait(m, mark, g_sub_full)
            m = chain(v.tensor_reduce(s4, heads(sq), AX.X, ALU.add))
            r = inverse_rms(s4, 2 * DH, DIFF_H, m)
            g_all = g_sub[:, :].unsqueeze(1).to_broadcast([P, DIFF_H, P])
            m = dve.mark(v.scalar_tensor_tensor(heads(sq), heads(src), 1.0 - LAM_INIT, g_all, ALU.mult, ALU.mult))
            o_banks[t].readers = [m]
            dve.wait(m, r)
            ya_done[t] = chain(v.tensor_tensor(heads(y), heads(sq), s4.unsqueeze(2).to_broadcast([P, DIFF_H, P]), ALU.mult))

        wide = lambda a: a.unsqueeze(2).to_broadcast([P, NSA_H, NC])
        each = lambda a: a.unsqueeze(1).to_broadcast([P, NSA_H, NC])

        def cmp_scores(q):
            bank = next_bank("aux")
            pe.wait(bank.readers)
            pe.wait(marks["kcd"], *proj_done["nqT"])
            for h in range(NSA_H):
                rows = slice((h // HPG) * DH, (h // HPG + 1) * DH)
                if h == HPG:
                    pe.wait(done)
                last = pe.engine.matmul(bank.ap[:, h * 16:h * 16 + NC], nqT[rows, h % HPG, q * P:(q + 1) * P],
                                        kcd[rows, :], start=True, stop=True)
                if h % HPG == HPG - 1:
                    done = pe.mark(last)
            sc = bank.ap[:, 0:NSA_H * 16].rearrange("p (h c) -> p h c", h=NSA_H)[:, :, 0:NC]
            p_ = pc[:, q, :, 0:NC]
            s8 = small[:, 16 + 16 * q:24 + 16 * q]
            dve.wait(done, marks["cmp_zero"], cst_landed)
            m = chain(v.tensor_tensor(p_, sc, each(cmp_add[:, q, :]), ALU.add))
            bank.readers = [m]
            chain(v.tensor_reduce(s8, p_, AX.X, ALU.max))
            m = chain(v.tensor_tensor(p_, p_, wide(s8), ALU.subtract))
            act.wait(m)
            marks[f"cmp_exp{q}"] = act.mark(act.engine.activation(p_, p_, ACT.Exp))

        def cmp_weights(q):
            p_ = pc[:, q, :, 0:NC]
            s8 = small[:, 16 + 16 * q:24 + 16 * q]
            dve.wait(marks[f"cmp_exp{q}"])
            chain(v.tensor_reduce(s8, p_, AX.X, ALU.add))
            chain(v.reciprocal(s8, s8))
            dve.wait(proj_done["gates"][q])
            chain(v.tensor_tensor(s8, s8, gates[q][:, 0:NSA_H], ALU.mult))
            chain(v.tensor_tensor(p_, p_, each(cmp_keep[:, q, :]), ALU.mult))
            marks[f"pc{q}"] = chain(v.tensor_tensor(p_, p_, wide(s8), ALU.mult))

        def cmp_transposes(q):
            flat = pc[:, q, :, :].rearrange("p h c -> p (h c)")
            bank, mark = transpose_tiles([flat[:, g * P:(g + 1) * P] for g in range(G)], [marks[f"pc{q}"]])
            marks[f"pcT{q}"] = copy_out(act, pcT[:, q, :], bank.ap[:, 0:G * P], [mark])
            bank.readers = [marks[f"pcT{q}"]]

        def open_values(q):
            pe.wait(marks[f"pcT{q}"], marks["vbd"], o_banks[q].readers)
            for g in range(G):
                pe.engine.matmul(o_banks[q].ap[:, g * HPG * DH:(g + 1) * HPG * DH], pcT[:, q, g * P:(g + 1) * P],
                                 vbd[:, g, :, :], start=g == 0, stop=False, skip_group_check=True)

        items = [("diff", h, q) for h in range(DIFF_H) for q in range(NT)] + \
                [("nsa", h, q) for h in range(NSA_H) for q in range(NT)]
        n_items = len(items)
        extras = {3: lambda: cmp_scores(0), 4: lambda: cmp_scores(1), 5: lambda: cmp_weights(0),
                  6: lambda: cmp_weights(1), 7: lambda: cmp_transposes(0), 8: lambda: cmp_transposes(1)}
        n_fill = 4 * 8 + 2 * 4 + 1
        filled = 0
        for n in range(n_items + 3):
            if n < n_items:
                item_scores(n, *items[n])
            if n in extras:
                extras[n]()
            share = min(n_fill, (n + 1) * n_fill // n_items)
            fill(share - filled)
            filled = share
            if n == n_items:
                sigmoid_pieces = [(b, i, t) for i in range(2) for b in range(2) for t in range(NT)]
                sig_done = {}
                for b, i, t in sigmoid_pieces:
                    gate = mg[:, t, half(2 * b + i)]
                    act.wait(mg_done[2 * b + i, t])
                    sig_done[b, i, t] = act.mark(act.engine.activation(gate, gate, ACT.Sigmoid))
            for stage, work in ((1, item_weights), (2, item_transposes), (3, item_values)):
                if 0 <= n - stage < n_items:
                    work(n - stage, *items[n - stage])
        fill(n_fill)

        ready_b = ready_of([to_features(pj[:, t, O_NQ:O_NQ + NSA_W], 4, t, [yb_done[t]], uT_h, uT_l, 4,
                                        [marks["gates_products"]]) for t in range(NT)])
        w_out_ready = [[None, None], [None, None]]

        for i in range(2):
            for t in range(NT):
                pool.wait(sig_done[0, i, t], xa_done[i, t])
                xa_done[i, t] = pool.mark(pool.engine.tensor_tensor(xn[:, t, half(i)], xn[:, t, half(i)],
                                                                    mg[:, t, half(i)], ALU.mult))

        def merge(i, pair):
            def work(t, done):
                other = mg[:, t, half(2 + i)]
                dve.wait(done, sig_done[1, i, t])
                m = chain(v.tensor_tensor(other, pair[t].ap[:, :], other, ALU.mult))
                pair[t].readers = [m]
                dve.wait(xa_done[i, t])
                m = dve.mark(v.tensor_tensor(xn[:, t, half(i)], xn[:, t, half(i)], other, ALU.add))

                def turn():
                    free = [marks["branch_a_products"]] if i == 0 else [done]
                    w_out_ready[i][t], = to_features(xn[:, t, half(i)], 4, t, [m], uT_h, uT_l, 4 * i, free)
                put_off(3, turn)
            return work

        for i in range(2):
            run(linear(f"branch_b{i}", uT_h, uT_l, ready_b, pairs[i], merge(i, pairs[i]), k_first=4))

        def residual(name, ready, in_h, in_l, stats, after=None):
            got = [[], []]

            def empty_into(i):
                def work(t, done):
                    dve.wait(done)
                    m = dve.mark(v.tensor_tensor(x[:, t, half(i)], pairs[i][t].ap[:, :], x[:, t, half(i)], ALU.add))
                    pairs[i][t].readers = [m]
                    got[t].append(square_half(t, i, stats[t], m, pairs[i][t].ap[:, :]))
                    pairs[i][t].readers = [got[t][-1]]
                    if after:
                        after(t, i, m, got[t], done)
                return work
            for i in range(2):
                done = run(linear(f"{name}{i}", in_h, in_l, ready, pairs[i], empty_into(i)))
                if name == "down" and i == 0:
                    ada(6, 0), ada(6, 1, 4), ada(7, 0, 8), ada(7, 1, 12)
            return got, done

        stats = [columns(2) for _ in range(NT)]
        ffn_ready, row_b_read = [[], []], []

        def ffn_norm(t, i, mark, squares, closed):
            if i == 1:
                put_off(0 if t == 0 else 2, lambda: norm_tile(t, (stats[t], squares), row_b, [row_b_full], ffn_ready,
                                                              row_b_read, [closed]))
        x_squares, done = residual("w_out", w_out_ready, uT_h, uT_l, stats, ffn_norm)
        mixer.close()

        late = sb("late_rows", [P, 2, D])
        row_e, row_f = late[:, 0, :], late[:, 1, :]

        hidden_stack = ExitStack()
        ctx.enter_context(hidden_stack)
        hid_h = sb("hidden_high", [P, KF2, T], F32R, stack=hidden_stack)
        hid_l = sb("hidden_low", [P, KF2, T], F32R, stack=hidden_stack)

        ready = InputReady(ffn_ready)

        def next_row_b():
            marks["g_mix_2"] = load(row_b[:, :], io["g_mix_2"].to_broadcast([P, D]), *row_b_read)
        put_off(4, next_row_b)

        ada_free = [[], []]
        ada_done = {}

        ada_last = {}

        def ada(i, part, first=0):
            slab, = W.chunks[f"ada{i}_{part}"]
            acc_i = ada_acc[:, i % 2, :]

            def row(k):
                def work():
                    w, c = W.slab_view(slab)[:, k % 4, :], c_act[:, k:k + 1]
                    dve.wait(W.slabs[slab]["landed"], marks["c"], ada_last.get(i))
                    if k == 0:
                        dve.wait(ada_free[i % 2])
                        ada_last[i] = dve.mark(v.tensor_scalar(acc_i, w, c, None, ALU.mult))
                    else:
                        ada_last[i] = dve.mark(v.scalar_tensor_tensor(acc_i, w, c, acc_i, ALU.mult, ALU.add))
                    if k % 4 == 3:
                        W.release(slab, ada_last[i])
                return work

            def finish():
                dst, how, dst_marks = ada_plan[i]
                bank = next_bank("aux")
                pe.wait(bank.readers)
                pe.wait(ada_last[i], ones_set, b_ada_landed)
                pe.engine.matmul(bank.ap[:, :], ones[:, :], acc_i, start=True, stop=False)
                m = pe.mark(pe.engine.matmul(bank.ap[:, :], ident[0:12, i:i + 1].to_broadcast([12, P]), b_ada[:, :],
                                             start=False, stop=True))
                ada_free[i % 2] = [m]
                dve.wait(m, *[marks[name] for name in dst_marks])
                if how == "scale":
                    r = dve.mark(v.scalar_tensor_tensor(dst, bank.ap[:, :], 1.0, dst, ALU.add, ALU.mult))
                else:
                    r = dve.mark(v.tensor_copy(dst, bank.ap[:, :]))
                bank.readers = [r]
                ada_done[i] = r
            for k in range(4):
                put_off(first + k, row(4 * part + k))
            if part == 1:
                put_off(first + 7, finish)

        def shift_scale_gate(shift, scale, gain, gate, gate_read):
            return [(shift[:, half(h)], "copy", []) for h in range(2)] + \
                   [(scale[:, half(h)], "scale", [gain]) for h in range(2)] + \
                   [(gate[:, half(h)], "copy", gate_read) for h in range(2)]
        ada_plan = shift_scale_gate(row_c, row_b, "g_mix_2", row_d, []) + \
            shift_scale_gate(row_e, row_f, "g_ffn_2", row_d, ["row_d_read"])
        marks["g_ffn_2"] = load(row_f, io["g_ffn_2"].to_broadcast([P, D]), done)

        hidden_ready = [[], []]
        for i, (c0, n) in enumerate(ffn_chunks):
            sl = xn[:, :, (i % 2) * BANK:(i % 2) * BANK + n]
            silus = {}

            def empty_gate(t, done, sl=sl, n=n, silus=silus):
                act.wait(done)
                silus[t] = act.mark(act.engine.activation(sl[:, t, :], pairs[0][t].ap[:, 0:n], ACT.Silu))
                pairs[0][t].readers = [silus[t]]

            def empty_up(t, done, sl=sl, n=n, c0=c0, silus=silus):
                dve.wait(silus[t], done)
                m = dve.mark(v.tensor_tensor(sl[:, t, :], pairs[1][t].ap[:, 0:n], sl[:, t, :], ALU.mult))
                pairs[1][t].readers = [m]
                put_off(4, turned(sl[:, t, :], t, m, hid_h, hid_l, c0 // P, [], hidden_ready))
            run(linear(f"gate{i}", uT_h, uT_l, ready, pairs[0], empty_gate))
            ada(i, 0)
            run(linear(f"up{i}", uT_h, uT_l, ready, pairs[1], empty_up))
            ada(i, 1)
        hidden_marks = InputReady(hidden_ready)

        y_stats = [columns(2) for _ in range(NT)]
        stats = [columns(2) for _ in range(NT)]

        mix2_ready, adds = [[], []], []

        def final_gain(t, i, mark, got, closed):
            dve.wait(mark, row_a_full)
            m = dve.mark(v.tensor_tensor(xn[:, t, half(i)], x[:, t, half(i)], row_a[:, half(i)], ALU.mult))
            row_a_read.append(m)
            act.wait(got[-1])
            got.append(square_half(t, i, y_stats[t], m, pairs[i][t].ap[:, :], src=xn[:, t, half(i)]))
            pairs[i][t].readers = [got[-1]]
            if i == 1:
                put_off(0 if t == 0 else 2, lambda: two_norms(t, got, closed))

        def two_norms(t, squares, closed):
            r = columns(2)
            q = columns(2)
            dve.wait(*squares)
            v.tensor_scalar(r[:, 0:1], stats[t][:, 0:1], stats[t][:, 1:2], NORM_EPS, ALU.add, ALU.add)
            chain(v.tensor_scalar(q[:, 0:1], y_stats[t][:, 0:1], y_stats[t][:, 1:2], None, ALU.add))
            chain(v.reciprocal(q[:, 1:2], r[:, 0:1]))
            m = chain(v.tensor_scalar(r[:, 1:2], q[:, 0:1], q[:, 1:2], NORM_EPS, ALU.mult, ALU.add))
            pool.wait(m)
            m = pool.mark(pool.engine.tensor_tensor(r, r, minus_half[:, 0:2], ALU.pow))
            dve.wait(m)
            chain(v.tensor_tensor(q[:, 0:1], r[:, 0:1], r[:, 1:2], ALU.mult))
            dve.wait(*[ada_done[a] for a in range(4)])
            for h in range(2):
                y = xn[:, t, half(h)]
                chain(v.tensor_scalar(x[:, t, half(h)], y, r[:, 0:1], None, ALU.mult))
                chain(v.scalar_tensor_tensor(y, y, q[:, 0:1], row_b[:, half(h)], ALU.mult, ALU.mult))
                m = dve.mark(v.tensor_tensor(y, y, row_c[:, half(h)], ALU.add))
                adds.append(m)
                put_off(2 + h, turned(y, t, m, uT_h, uT_l, 4 * h, [closed], mix2_ready))

        row_a_read = []
        squares, down_done = residual("down", hidden_marks, hid_h, hid_l, stats, final_gain)
        row_a_full = load(row_a[:, :], io["g_final_2"].unsqueeze(0).to_broadcast([P, D]), *row_a_read)
        hidden_stack.close()

        mix2 = ExitStack()
        ctx.enter_context(mix2)

        def m2(name, shape, dtype=F32):
            return sb(name, shape, dtype, stack=mix2)

        ready = InputReady(mix2_ready)

        vE = m2("v_and_one", [P, NT, H2, E2 + 1])
        so = m2("sigmoid_o", [P, NT, MW])
        u_pool = m2("pool_input", [P, NT, MW])
        qk = m2("q_k", [P, NT, 2 * MW])
        q2T = m2("q2T", [P, H2, T])
        k2T = m2("k2T", [P, H2, T])
        gtmp = m2("gate_scratch", [P, NT, 2, 2 * H2])
        gt = m2("gate_values", [P, NT, 2, 2, H2])
        gb = m2("gate_bias", [P, 2, 2, H2])
        gp = m2("gate_padded", [P, NT, 2, 64])
        rows2 = m2("gate_rows", [64, 2, T])
        scans = m2("gate_scans", [64, 3, T])
        cols2 = m2("gate_columns", [P, NT, 3, 64])
        expm = m2("exp_minus_m", [P, NT, 64])
        gh = m2("head_gain_row", [P, MW])
        wT = m2("decay_T", [P, 2, 3 * P])
        sT = m2("scoresT_weighted", [P, 2, 3 * P])
        hm = m2("heads_out", [P, NT, MW])
        hsq = m2("heads_squared", [P, NT, MW])
        dn = m2("denominators", [P, 4, NT])
        wp = m2("w_pool", [P, PG, P])
        mixT = m2("pool_mixedT", [P, 2, T])
        ybT = m2("pool_outT", [P, PG, T])
        zeros = m2("zeros", [64, T])
        gb_full = [load(gb[:, :, j, :], io[n][0].partition_broadcast(P), down_done)
                   for j, n in ((0, "b_igate_2"), (1, "b_fgate_2"))]
        gh_full = load(gh[:, :], io["g_head_2"].to_broadcast([P, MW]), down_done)
        wp_full = load(wp[:, :, :], io["w_pool_2"][0].rearrange("g c e -> c g e"), down_done)
        pool.wait(down_done)
        m = pool.mark(pool.engine.memset(zeros[:, :], 0.0))
        pool.wait(m)
        m = pool.mark(pool.engine.memset(gp[:, :, :, :], 0.0))
        set2 = pool.mark(pool.engine.memset(vE[:, :, :, E2:E2 + 1], 1.0))
        dve.wait(down_done)
        act.wait(down_done)

        k_scale = {"q2": E2 ** -0.5, "k2": None}
        qk_T = {"q2": [None, None], "k2": [None, None]}

        def turn_heads(name, t, col, dst, mark):
            def work():
                bank, m = transpose_tiles([qk[:, t, col + h * P:col + (h + 1) * P] for h in range(H2)], [mark])
                src = bank.ap[:, :].rearrange("p (k n) -> p k n", k=H2)
                qk_T[name][t] = copy_out(act, dst[:, :, t * P:(t + 1) * P], src, [m], k_scale[name])
                bank.readers = [qk_T[name][t]]
            return work

        def gates_work(t, mark):
            flat = lambda a: a.rearrange("p a b c -> p (a b c)")
            z, zf = gt[:, t, :, :, :], gt[:, t, :, 1, :]
            a, b = gtmp[:, t, 0, :], gtmp[:, t, 1, :]
            a3, b3 = (s.rearrange("p (d h) -> p d h", d=2) for s in (a, b))
            dve.wait(mark, gb_full, set2)
            m = chain(v.tensor_tensor(flat(z), flat(z), flat(gb[:, :, :, :]), ALU.add))
            act.wait(m)
            m = act.mark(act.engine.activation(a3, zf, ACT.Abs))
            act.wait(m)
            m = act.mark(act.engine.activation(b, a, ACT.Exp, scale=-1.0))
            act.wait(m)
            m = act.mark(act.engine.activation(b, b, ACT.Ln, bias=1.0))
            dve.wait(m)
            for d in range(2):
                v.tensor_copy(gp[:, t, 0, 32 * d:32 * d + H2], gt[:, t, d, 0, :])
                m = dve.mark(v.scalar_tensor_tensor(gp[:, t, 1, 32 * d:32 * d + H2], zf[:, d, :], 0.0, b3[:, d, :],
                                                    ALU.min, ALU.subtract))
            return m

        gp_marks, og_marks, v2_marks, u_marks, so_marks = [], [], [], [[], []], []

        def gates_rows():
            bank = next_bank("aux")
            pe.wait(bank.readers)
            pe.wait(gp_marks)
            for q in range(2):
                for t in range(NT):
                    last = pe.engine.transpose(bank.ap[0:64, (q * NT + t) * P:(q * NT + t + 1) * P], gp[:, t, q, :], ident)
            done = pe.mark(last)
            m = copy_out(act, rows2[:, :, :], bank.ap[0:64, :].rearrange("p (q t) -> p q t", q=2), [done])
            bank.readers = [m]
            dve.wait(m, ones_set, set2)
            fw, bw = slice(0, 32), slice(32, 64)
            b_fw, b_bw = scans[fw, 2, :], scans[bw, 2, ::-1]
            one = ones[0:64, 0:1].to_broadcast([64, T])
            v.tensor_tensor_scan(b_fw, one[fw, :], rows2[fw, 1, :], 0.0, ALU.mult, ALU.add)
            chain(v.tensor_tensor_scan(b_bw, one[bw, :], rows2[bw, 1, ::-1], 0.0, ALU.mult, ALU.add))
            chain(v.tensor_tensor(scans[:, 0, :], rows2[:, 0, :], scans[:, 2, :], ALU.subtract))
            v.tensor_tensor_scan(scans[fw, 1, :], zeros[fw, :], scans[fw, 0, :], 0.0, ALU.max, ALU.max)
            chain(v.tensor_tensor_scan(scans[bw, 1, ::-1], zeros[bw, :], scans[bw, 0, ::-1], 0.0, ALU.max, ALU.max))
            marks["scans"] = chain(v.tensor_tensor(scans[:, 2, :], scans[:, 2, :], scans[:, 1, :], ALU.add))

        def gates_columns():
            bank = next_bank("aux")
            pe.wait(bank.readers)
            pe.wait(marks["scans"])
            for t in range(NT):
                for q in range(3):
                    last = pe.engine.transpose(bank.ap[:, (t * 3 + q) * 64:(t * 3 + q + 1) * 64],
                                               scans[:, q, t * P:(t + 1) * P], ident[0:64, 0:64])
            done = pe.mark(last)
            src = bank.ap[:, 0:NT * 3 * 64].rearrange("p (t q r) -> p t q r", t=NT, q=3)
            dve.wait(done)
            v.tensor_copy(cols2[:, :, 0, :], src[:, :, 0, :])
            m1 = dve.mark(v.tensor_scalar(cols2[:, :, 1, :], src[:, :, 1, :], -1.0, None, ALU.mult))
            act.wait(done, m1)
            m2_ = act.mark(act.engine.activation(expm[:, :, :], src[:, :, 2, :], ACT.Exp, scale=-1.0))
            bank.readers = [m1, m2_]
            cols_done.extend([m1, m2_])

        cols_done = []
        pool_out = []
        pool_products = []

        def pooling_window(g):
            slab = W.chunks["pool_matrix"][0]
            a = W.slab_view(slab).rearrange("p s (g t) -> p s g t", g=PG)
            bank = next_bank("aux")
            pe.wait(bank.readers)
            pe.wait(W.slabs[slab]["landed"], u_marks)
            for s in range(NT):
                last = pe.engine.matmul(bank.ap[:, 0:T], u_pool[:, s, g * P:(g + 1) * P], a[:, s, g, :],
                                        start=s == 0, stop=s == NT - 1)
            done = pe.mark(last)
            if g == PG - 1:
                W.release(slab, done)
            marks[f"mixed{g}"] = copy_out(act, mixT[:, g % 2, :], bank.ap[:, 0:T], [done] + pool_products[g - 2:g - 1])
            bank.readers = [marks[f"mixed{g}"]]

        def pooling_map(g):
            bank = next_bank("aux")
            pe.wait(bank.readers)
            pe.wait(marks[f"mixed{g}"], wp_full)
            done = pe.mark(pe.engine.matmul(bank.ap[:, 0:T], wp[:, g, :], mixT[:, g % 2, :], start=True, stop=True))
            pool_products.append(done)
            dve.wait(done, marks["vectors"])
            m = dve.mark(v.tensor_scalar(ybT[:, g, :], bank.ap[:, 0:T], vec_cols[:, V_PS + g:V_PS + g + 1], None, ALU.mult))
            bank.readers = [m]
            pool_out.append(m)

        def empty_in2(name, n, pair):
            def work(t, done):
                src = pair[t].ap[:, 0:n]
                if name in ("q2", "k2"):
                    col, dst = (0, q2T) if name == "q2" else (MW, k2T)
                    m = copy_out(act, qk[:, t, col:col + MW], src, [done])
                    put_off(2, turn_heads(name, t, col, dst, m))
                elif name == "v2":
                    act.wait(done, set2)
                    m = act.mark(act.engine.activation(vE[:, t, :, 0:E2], src.rearrange("p (h e) -> p h e", h=H2), ACT.Copy))
                    v2_marks.append(m)
                elif name == "o2":
                    m = copy_out(act, so[:, t, :], src, [done])
                    so_marks.append(m)
                elif name == "gu0":
                    m1 = copy_out(dve, gt[:, t, :, :, :].rearrange("p a b c -> p (a b c)"), src[:, 0:NG2], [done])
                    m = copy_out(dve, u_pool[:, t, 0:n - NG2], src[:, NG2:n], [done])
                    u_marks[t].append(m)
                    gp_marks.append(gates_work(t, m1))
                    if t == NT - 1:
                        put_off(4, gates_rows)
                        put_off(9, gates_columns)
                else:
                    m = copy_out(act, u_pool[:, t, n - NG2:MW], src, [done])
                    u_marks[t].append(m)
                pair[t].readers = [m]
            return work

        for i, (name, c0, n) in enumerate(in2[:-1]):
            pair = pairs[i % 2]
            run(linear(name, uT_h, uT_l, ready, pair, empty_in2(name, n, pair)))
            if i in in2_ada:
                ada(*in2_ada[i])
            if i == 2:
                for g in range(PG):
                    put_off(1 + g, lambda g=g: pooling_window(g))
                    put_off(2 + g, lambda g=g: pooling_map(g))

        w_free, s_free = [[], []], [[], []]

        def scores2(h):
            bank = acc[h % 2]
            pe.wait(bank.readers)
            pe.wait(qk_T["q2"], qk_T["k2"])
            for s in range(NT):
                last = pe.engine.matmul(bank.ap[:, s * T:(s + 1) * T], k2T[:, h, s * P:(s + 1) * P], q2T[:, h, :],
                                        start=True, stop=True)
            bank.readers = []
            return bank, pe.mark(last)

        def decay(h, d):
            i = 2 * h + d
            r = 32 * d + h
            bank = tr_banks[i % 2]
            pe.wait(bank.readers)
            pe.wait(cols_done, masks_ready)
            for block, t in ((0, 0), (1, 1 - d), (2, 1)):
                pe.engine.matmul(bank.ap[:, block * P:(block + 1) * P], cols2[:, t, 1, r:r + 1].to_broadcast([P, P]), ident,
                                 start=block == 0, stop=False, skip_group_check=True)
            mask = (before_r, after_r)[d]
            diag = bank.ap[:, 0:3 * P].rearrange("p (b n) -> p b n", b=3)[:, ::2, :]
            done = pe.mark(pe.engine.matmul(diag, ident_r[:, :], mask[:, :].unsqueeze(1).to_broadcast([P, 2, P]),
                                            start=False, stop=True, skip_group_check=True))
            act.wait(done, w_free[i % 2])
            edges = ((0, 2 * P, 0), (2 * P, 3 * P, 1)) if d == 0 else ((0, P, 0), (P, 3 * P, 1))
            for a, b, s in edges:
                m = act.mark(act.engine.activation(wT[:, i % 2, a:b], bank.ap[:, a:b], ACT.Exp, bias=cols2[:, s, 0, r:r + 1]))
            bank.readers = [m]
            return m

        def weigh(h, d, sbank, s_mark, w_mark):
            i = 2 * h + d
            dve.wait(s_mark, w_mark, s_free[i % 2])
            st = sbank.ap[:, :].rearrange("p (s t) -> p s t", s=NT)
            parts = (((0, 2 * P), st[:, 0, 0:T]), ((2 * P, 3 * P), st[:, 1, P:T])) if d == 0 else \
                    (((0, P), st[:, 0, 0:P]), ((P, 3 * P), st[:, 1, 0:T]))
            for (a, b), src in parts:
                m = dve.mark(v.tensor_tensor(sT[:, i % 2, a:b], src, wT[:, i % 2, a:b], ALU.mult))
            w_free[i % 2] = [m]
            return m

        def numerators(h, d, mark):
            i = 2 * h + d
            r = 32 * d + h
            bank = aux_banks[i % 2]
            pe.wait(bank.readers)
            pe.wait(mark, v2_marks)
            blocks = {(0, 0): 0, (1, 1): 2, ((0, 1) if d == 0 else (1, 0)): 1}
            W1 = E2 + 1
            for t in range(NT):
                srcs = [s for s in range(NT) if (s, t) in blocks]
                for n, s in enumerate(srcs):
                    b = blocks[(s, t)]
                    last = pe.engine.matmul(bank.ap[:, t * W1:(t + 1) * W1], sT[:, i % 2, b * P:(b + 1) * P],
                                            vE[:, s, h, :], start=n == 0, stop=n == len(srcs) - 1)
            done = pe.mark(last)
            s_free[i % 2] = [done]
            num = bank.ap[:, 0:NT * W1].rearrange("p (t e) -> p t e", t=NT)
            den = dn[:, i % 4, :]
            dve.wait(done, cols_done)
            chain(v.tensor_reduce(den, num[:, :, E2:E2 + 1], AX.X, ALU.max, apply_absolute_value=True))
            chain(v.tensor_tensor(den, den, expm[:, :, r], ALU.max))
            chain(v.reciprocal(den, den))
            for t in range(NT):
                dst = hm[:, t, h * E2:(h + 1) * E2]
                if d == 0:
                    m = chain(v.tensor_scalar(dst, num[:, t, 0:E2], den[:, t:t + 1], None, ALU.mult))
                else:
                    m = chain(v.scalar_tensor_tensor(dst, num[:, t, 0:E2], den[:, t:t + 1], dst, ALU.mult, ALU.add))
            bank.readers = [m]
            if d == 1:
                for t in range(NT):
                    act.wait(m)
                    squares2.append(act.mark(act.engine.activation(
                        hsq[:, t, h * E2:(h + 1) * E2], hm[:, t, h * E2:(h + 1) * E2], ACT.Square,
                        scale=E2 ** -0.5, accum_out=ms2[:, t * H2 + h:t * H2 + h + 1])))

        squares2, ms2 = [], columns(NT * H2)
        weighted, decayed, score_banks = {}, {}, {}

        def mlstm_steps():
            heads = [(h, d) for h in range(H2) for d in range(2)]
            for n in range(len(heads) + 2):
                if n < len(heads):
                    h, d = heads[n]
                    if d == 0:
                        score_banks[h] = scores2(h)
                    decayed[n] = decay(h, d)
                if 1 <= n <= len(heads):
                    h, d = heads[n - 1]
                    weighted[n - 1] = weigh(h, d, *score_banks[h], decayed[n - 1])
                    if d == 1:
                        score_banks[h][0].readers = [weighted[n - 1]]
                if n >= 2:
                    numerators(*heads[n - 2], weighted[n - 2])
                yield

        steps = mlstm_steps()
        name, c0, n = in2[-1]
        for i, done in enumerate(linear(name, uT_h, uT_l, ready, pairs[1], empty_in2(name, n, pairs[1]))):
            next(steps)
        pool_tail = [done]

        act.wait(pool_out, pool_tail)
        pooled = [act.mark(act.engine.activation(uT_h[:, H2:H2 + PG, :], ybT[:, :, :], ACT.Copy))]
        dve.wait(pooled, pool_tail)
        pooled.append(dve.mark(v.tensor_tensor(uT_l[:, H2:H2 + PG, :], ybT[:, :, :],
                                               uT_h[:, H2:H2 + PG, :].bitcast(F32), ALU.subtract)))
        for _ in steps:
            pass
        run_later()
        og_done = []
        for t in range(NT):
            act.wait(so_marks[t])
            m = act.mark(act.engine.activation(so[:, t, :], so[:, t, :], ACT.Sigmoid))
            dve.wait(m, gh_full)
            og_done.append(dve.mark(v.tensor_tensor(so[:, t, :], so[:, t, :], gh[:, :], ALU.mult)))

        dve.wait(*squares2)
        m = dve.mark(v.tensor_scalar(ms2, ms2, NORM_EPS, None, ALU.add))
        pool.wait(m)
        r = pool.mark(pool.engine.tensor_tensor(ms2, ms2, minus_half[:, 0:NT * H2], ALU.pow))
        ready_a = []
        for t in range(NT):
            h3 = hm[:, t, :].rearrange("p (h e) -> p h e", h=H2)
            dve.wait(og_done[t])
            m = dve.mark(v.tensor_tensor(hm[:, t, :], hm[:, t, :], so[:, t, :], ALU.mult))
            dve.wait(m, r)
            m = dve.mark(v.tensor_tensor(h3, h3, ms2[:, t * H2:(t + 1) * H2].unsqueeze(2).to_broadcast([P, H2, E2]), ALU.mult))

            def turn(t=t, m=m):
                ready_a.append(to_features(hm[:, t, :], H2, t, [m], uT_h, uT_l, 0, pool_tail)[0])
            put_off(1 + t, turn)
        ready_y = OutputReady(ready_a, pooled)

        def gated_residual(name, ready, in_h, in_l, gate, gate_marks, stats, after):
            got = [[], []]

            def empty_into(i):
                def work(t, done):
                    dve.wait(done, gate_marks[i]())
                    m = chain(v.tensor_tensor(xn[:, t, half(i)], pairs[i][t].ap[:, :], gate[:, half(i)], ALU.mult))
                    m = dve.mark(v.tensor_tensor(x[:, t, half(i)], x[:, t, half(i)], xn[:, t, half(i)], ALU.add))
                    got[t].append(square_half(t, i, stats[t], m, pairs[i][t].ap[:, :]))
                    pairs[i][t].readers = [got[t][-1]]
                    last_adds.append(m)
                    if i == 1:
                        after(t, got[t], done)
                return work
            for i in range(2):
                done = run(linear(f"{name}{i}", in_h, in_l, ready, pairs[i], empty_into(i)))
            return got, done

        last_adds = []
        stats = [columns(2) for _ in range(NT)]
        ffn2_ready = [[], []]

        def ffn2_norm(t, squares, closed):
            put_off(0 if t == 0 else 2, lambda: norm_tile(t, (stats[t], squares), row_f, [ada_done[8], ada_done[9]],
                                                          ffn2_ready, [], [closed], row_e, [ada_done[6], ada_done[7]]))
        squares, done = gated_residual("w_out2_", ready_y, uT_h, uT_l, row_d,
                                       [lambda: ada_done[4], lambda: ada_done[5]], stats, ffn2_norm)
        mix2.close()

        hid2 = ExitStack()
        ctx.enter_context(hid2)
        hid_h = sb("hidden2_high", [P, KF2, T], F32R, stack=hid2)
        hid_l = sb("hidden2_low", [P, KF2, T], F32R, stack=hid2)
        ready = InputReady(ffn2_ready)
        marks["row_d_read"] = last_adds[-1]
        hidden_ready = [[], []]
        for i in range(DFF2 // BANK):
            pair = pairs[i % 2]
            sl = xn[:, :, half(i % 2)]

            def empty_ff1(t, done, i=i, pair=pair, sl=sl):
                act.wait(done)
                m = act.mark(act.engine.activation(sl[:, t, :], pair[t].ap[:, :], ACT.Relu))
                pair[t].readers = [m]
                pool.wait(m)
                m = pool.mark(pool.engine.tensor_tensor(sl[:, t, :], sl[:, t, :], sl[:, t, :], ALU.mult))
                put_off(4, turned(sl[:, t, :], t, m, hid_h, hid_l, 4 * i, [], hidden_ready))
            run(linear(f"ff1_{i}", uT_h, uT_l, ready, pair, empty_ff1))
            if i in ff1_ada:
                ada(*ff1_ada[i])
        hidden_marks = InputReady(hidden_ready)
        stats = [columns(2) for _ in range(NT)]
        stored = sem("result_stored")

        def final_norm(t, squares, closed):
            col, m = scale_from(stats[t], squares)
            for h in range(2):
                dve.wait(m, row_a_full)
                done = dve.mark(v.scalar_tensor_tensor(xn[:, t, half(h)], x[:, t, half(h)], col, row_a[:, half(h)],
                                                       ALU.mult, ALU.mult))
                sp.wait(done)
                nc.sync.dma_start(out[0, t * P:(t + 1) * P, half(h)], xn[:, t, half(h)]).then_inc(stored, 16)

        gated_residual("ff2_", hidden_marks, hid_h, hid_l, row_d,
                       [lambda: ada_done[10], lambda: ada_done[11]], stats, final_norm)
        run_later()
        nc.sync.wait_ge(stored, 16 * NT * 2)
        assert W.issued == len(W.slabs) and not later


_NAMES = ["x", "positions", "attn_norm_g", "w_in", "diff_lambda", "diff_subln_g", "cmp_pe_k", "cmp_pe_v", "cmp_k_w1",
          "cmp_k_w2", "cmp_v_w1", "cmp_v_w2", "w_branch_a", "w_branch_b", "w_out", "ffn_norm_g", "w_gate", "w_up",
          "w_down", "final_norm_g", "c_2", "w_ada_2", "b_ada_2", "g_mix_2", "w_in_2", "b_igate_2", "b_fgate_2",
          "g_head_2", "w_pool_2", "pool_scale_2", "w_out_2", "g_ffn_2", "w_ff1_2", "w_ff2_2", "g_final_2"]


def shape_constants(tokens, head_dim):
    import numpy as np
    tile, cmp_len, cmp_stride, theta, windows = 128, 32, 16, 10000.0, (2, 4, 8, 16)
    n_tiles, n_cmp = tokens // tile, (tokens - cmp_len) // cmp_stride + 1
    part, free = np.arange(tile)[:, None], np.arange(tile)[None, :]
    identity = (part == free).astype(np.float32)
    after = np.where(free > part, np.float32(-1e30), np.float32(0))
    before = np.where(free < part, np.float32(-1e30), np.float32(0))
    inv_freq = (1.0 / theta ** (np.arange(0, head_dim, 2, dtype=np.float32) / np.float32(head_dim))).astype(np.float32)
    inv_freq = np.broadcast_to(inv_freq, (tile, head_dim // 2))
    ends = np.arange(n_cmp) * cmp_stride + cmp_len - 1
    t = np.arange(tokens)
    seen = (ends[None, :] <= t[:, None]).reshape(n_tiles, tile, n_cmp).transpose(1, 0, 2).reshape(tile, -1)
    consts = np.concatenate([identity, after, before, inv_freq, np.where(seen, 0, np.float32(-1e30)), seen], 1)
    pool = np.zeros((tokens, len(windows), tokens), np.float32)
    for g, w in enumerate(windows):
        lo, hi = np.clip(t - w // 2, 0, tokens), np.clip(t + w // 2, 0, tokens)
        inside = (t[:, None] >= lo[None, :]) & (t[:, None] < hi[None, :])
        pool[:, g, :] = inside / (hi - lo)[None, :].astype(np.float32) - np.eye(tokens, dtype=np.float32)
    pool = pool.reshape(n_tiles, tile, -1).transpose(1, 0, 2)
    return np.ascontiguousarray(consts, np.float32), np.ascontiguousarray(pool, np.float32)


def kernel(**inputs):
    import numpy as _np
    import concourse.bacc as _bacc
    from concourse.bass_utils import run_bass_kernel_spmd as _run

    nc = _bacc.Bacc("TRN2", target_bir_lowering=False, num_devices=1)
    arrays = {name: _np.ascontiguousarray(inputs[name]) for name in _NAMES}
    arrays["consts"], arrays["pool_matrix"] = shape_constants(inputs["x"].shape[1], inputs["diff_lambda"].shape[2])
    io = {name: nc.dram_tensor(f"in_{name}", a.shape, mybir.dt.from_np(a.dtype), kind="ExternalInput").ap()
          for name, a in arrays.items()}
    shape = tuple(inputs["x"].shape)
    out = nc.dram_tensor("out", shape, F32, kind="ExternalOutput").ap()
    build(nc, io, out)
    result = _run(nc, [{f"in_{name}": a for name, a in arrays.items()}], core_ids=[0])
    return result.results[0]["out"]
```

```python
from contextlib import ExitStack

import concourse.bass as bass
from concourse import mybir

F32 = mybir.dt.float32
F32R = mybir.dt.float32r
I32 = mybir.dt.int32
ACT = mybir.ActivationFunctionType
ALU = mybir.AluOpType
AX = mybir.AxisListType

P = 128
BANK = 512
SLAB = 2048
RAW_SLABS = 5
UNIT = 1024
SPLIT_UNITS = 4
NORM_EPS = 1e-6
TWO_PI_PARTS = (6.28125, 0.0019350051879882812, 3.019916050e-07)
MAGIC = 12582912.0
PI_BELOW = 3.1415925


class Lane:

    def __init__(self, engine, semaphore):
        self.engine, self.semaphore = engine, semaphore
        self.count, self.reached = 0, {}

    def mark(self, instruction):
        self.count += 1
        instruction.then_inc(self.semaphore, 1)
        return (self.semaphore, self.count)

    def wait(self, *marks):
        for m in marks:
            if m is None:
                continue
            if isinstance(m, list):
                self.wait(*m)
            elif self.reached.get(id(m[0]), 0) < m[1]:
                self.engine.wait_ge(m[0], m[1])
                self.reached[id(m[0])] = m[1]


class Bank:

    def __init__(self, tensor):
        self.ap, self.readers = tensor, []


class InputReady:

    def __init__(self, marks_by_tile):
        self.marks = marks_by_tile

    def __getitem__(self, group):
        return [marks[group] if group < len(marks) else None for marks in self.marks]


class OutputReady:

    def __init__(self, heads, pooled):
        self.heads, self.pooled = heads, pooled

    def __getitem__(self, group):
        return [marks[0] if marks else None for marks in self.heads] if group == 0 else self.pooled


class Weights:

    def __init__(self, nc, sp, act, dve, raw, slot_sems, high, low):
        self.nc, self.sp, self.act, self.dve = nc, sp, act, dve
        self.raw, self.slot_sems, self.high, self.low = raw, slot_sems, high, low
        self.slabs, self.units, self.chunks = [], [], {}
        self.issued = self.highs = self.prepared = 0

    def plan_slab(self, src, kn, n):
        i = len(self.slabs)
        self.slabs.append({"src": src, "kn": kn, "n": n, "released": None, "slot": i % RAW_SLABS,
                           "landed": (self.slot_sems[i % RAW_SLABS], 16 * (i // RAW_SLABS + 1))})
        return i

    def plan_split(self, name, w, c0, n, starts=None, before=None):
        rows = w.shape[0] // P
        units = []
        for k0 in starts or range(0, rows, 4):
            kn = min(4, rows - k0)
            if before and k0 in before:
                before[k0]()
            src = w[k0 * P:(k0 + kn) * P, c0:c0 + n].rearrange("(k p) n -> p k n", p=P)
            i = self.plan_slab(src, kn, n)
            for k in range(0, kn, 2):
                units.append({"slab": i, "at": k, "kn": min(2, kn - k), "n": n, "k0": k0 + k,
                              "last": k + 2 >= kn, "used": None, "index": len(self.units),
                              "opens": not units, "closes": False})
                self.units.append(units[-1])
        units[-1]["closes"] = True
        self.chunks[name] = units

    def plan_raw(self, name, sources):
        self.chunks[name] = [self.plan_slab(src, src.shape[1], src.shape[2]) for src in sources]

    def slab_view(self, i):
        s = self.slabs[i]
        return self.raw[:, s["slot"], 0:s["kn"] * s["n"]].rearrange("p (k n) -> p k n", k=s["kn"])

    def release(self, i, *marks):
        self.slabs[i]["released"] = list(marks)
        self.pump()

    def pump(self, most=None):
        while self.issued < (most or len(self.slabs)):
            s = self.slabs[self.issued]
            if self.issued >= RAW_SLABS:
                before = self.slabs[self.issued - RAW_SLABS]
                if before["released"] is None:
                    return
                self.sp.wait(before["released"])
            self.sp.engine.dma_start(self.slab_view(self.issued), s["src"]).then_inc(s["landed"][0], 16)
            self.issued += 1

    def split_high(self, last):
        while self.highs <= min(last, len(self.units) - 1):
            u = self.units[self.highs]
            slab = self.slabs[u["slab"]]
            if u["slab"] >= self.issued:
                return
            u["src"] = self.slab_view(u["slab"])[:, u["at"]:u["at"] + u["kn"], :]
            ring, size = self.highs % SPLIT_UNITS, u["kn"] * u["n"]
            u["high"], u["low"] = (part[:, ring, 0:size].rearrange("p (k n) -> p k n", k=u["kn"])
                                   for part in (self.high, self.low))
            used = self.units[self.highs - SPLIT_UNITS]["used"] if self.highs >= SPLIT_UNITS else None
            self.act.wait(slab["landed"], used)
            u["high_ready"] = self.act.mark(self.act.engine.activation(u["high"], u["src"], ACT.Copy))
            self.highs += 1

    def prepare_through(self, last):
        self.split_high(last)
        while self.prepared < min(last + 1, self.highs):
            u = self.units[self.prepared]
            self.dve.wait(self.slabs[u["slab"]]["landed"], u["high_ready"])
            u["low_ready"] = self.dve.mark(
                self.dve.engine.tensor_tensor(u["low"], u["src"], u["high"].bitcast(F32), ALU.subtract))
            self.prepared += 1
            if u["last"]:
                self.release(u["slab"], u["low_ready"])


def build(nc, io, out):
    x_in = io["x"]
    T, D = x_in.shape[1], x_in.shape[2]
    NT = T // P
    KD = D // P
    w_in = io["w_in"][0]
    DH = io["diff_lambda"].shape[2]
    HALF = DH // 2
    DIFF_W = io["w_branch_a"].shape[1]
    DIFF_H = DIFF_W // (2 * DH)
    NSA_W = io["w_branch_b"].shape[1]
    NSA_H = NSA_W // DH
    G = 2
    HPG = NSA_H // G
    KV = G * DH
    N_GATES = 3 * NSA_H
    CMP_LEN, CMP_STRIDE = io["cmp_pe_k"].shape[1], 16
    NC = (T - CMP_LEN) // CMP_STRIDE + 1
    HID = io["cmp_k_w1"].shape[2]
    KH = HID // P
    CMP_J = CMP_LEN * DH // P
    CPAD = 32
    assert CPAD >= NC and CMP_LEN == 2 * CMP_STRIDE and HPG * CPAD == P and 2 * DH == P
    DFF = io["w_gate"].shape[2]
    DFF2 = io["w_ff1_2"].shape[2]
    KF2 = DFF2 // P
    w_in2 = io["w_in_2"][0]
    H2 = io["b_igate_2"].shape[2]
    MW = io["g_head_2"].shape[1]
    E2 = MW // H2
    NG2 = 4 * H2
    PG = io["w_pool_2"].shape[1]
    LAM_INIT = 0.8 - 0.6
    assert NT == 2 and E2 == P and DIFF_H * P == DIFF_W

    O_DQ, O_DK, O_DV, O_NQ = 0, DIFF_W, 2 * DIFF_W, 3 * DIFF_W
    O_KC = O_NQ + NSA_W
    O_VC, O_KS, O_VS, O_KW, O_VW, O_NG = (O_KC + i * KV for i in range(1, 7))
    O_MG = O_NG + N_GATES

    with ExitStack() as ctx:
        def sb(name, shape, dtype=F32, stack=ctx):
            return stack.enter_context(nc.sbuf_tensor(name, shape, dtype))

        def sem(name):
            return ctx.enter_context(nc.semaphore(name))

        pe = Lane(nc.tensor, sem("tensor_done"))
        act = Lane(nc.scalar, sem("scalar_done"))
        dve = Lane(nc.vector, sem("vector_done"))
        pool = Lane(nc.gpsimd, sem("gpsimd_done"))
        sp = Lane(nc.sync, None)
        banks = [Bank(ctx.enter_context(nc.psum_tensor(f"bank{i}", [P, BANK], F32))) for i in range(8)]
        acc, tr_banks, aux_banks = banks[0:4], banks[4:6], banks[6:8]

        raw = sb("raw_weights", [P, RAW_SLABS, SLAB])
        high = sb("weights_high", [P, SPLIT_UNITS, UNIT], F32R)
        low = sb("weights_low", [P, SPLIT_UNITS, UNIT], F32R)
        x = sb("x", [P, NT, D])
        xn = sb("xn", [P, NT, D])
        uT_h = sb("uT_high", [P, KD, T], F32R)
        uT_l = sb("uT_low", [P, KD, T], F32R)
        row_a = sb("row_a", [P, D])
        row_b = sb("row_b", [P, D])
        row_cd = sb("rows_c_d", [P, 2, D])
        row_c, row_d = row_cd[:, 0, :], row_cd[:, 1, :]
        consts = io["consts"]
        cst = sb("constants", [P, consts.shape[1]])
        ident = cst[:, 0:P]
        inv_freq = cst[:, 3 * P:3 * P + HALF]
        o_c = 3 * P + HALF
        cmp_add = cst[:, o_c:o_c + NT * NC].rearrange("p (t c) -> p t c", t=NT)
        cmp_keep = cst[:, o_c + NT * NC:o_c + 2 * NT * NC].rearrange("p (t c) -> p t c", t=NT)
        ident_r = sb("identity_r", [P, P], F32R)
        after_r = sb("mask_free_after_partition", [P, P], F32R)
        before_r = sb("mask_free_before_partition", [P, P], F32R)
        ones = sb("ones", [P, P])
        minus_half = sb("minus_half", [P, 8])
        ada_acc = sb("ada_acc", [P, 2, BANK])
        vec_rows = sb("vector_rows", [64, P])
        vec_cols = sb("vector_columns", [P, 64])
        c_act = sb("c_act", [P, KD])
        stat = sb("stat", [P, 112])
        small = sb("small", [P, 64])

        slot_sems = [sem(f"raw_slot{i}_landed") for i in range(RAW_SLABS)]
        W = Weights(nc, sp, act, dve, raw, slot_sems, high, low)

        n_loads = [0]

        def load(dst, src, *marks, queue=None, scattered=False):
            lane = queue or pool
            n_loads[0] += 1
            s = sem(f"load{n_loads[0]}_landed")
            lane.wait(*marks)
            lane.engine.dma_start(dst, src, allow_slow_non_contiguous=scattered).then_inc(s, 16)
            return (s, 16)

        projections = {"kva": (O_KC, 3 * KV), "dq": (O_DQ, DIFF_W), "kvb": (O_VS, 3 * KV + N_GATES),
                       "dk": (O_DK, DIFF_W), "nq": (O_NQ, NSA_W), "dv": (O_DV, DIFF_W)}
        for name, (c0, n) in projections.items():
            W.plan_split(name, w_in, c0, n)
            if name in ("dk", "nq"):
                which = "k" if name == "dk" else "v"
                w1 = io[f"cmp_{which}_w1"][0].rearrange("(j p) n -> p j n", p=P)
                W.plan_raw(f"cmp_{which}", [w1[:, 0:CMP_J // 2, :], w1[:, CMP_J // 2:CMP_J, :]])
        def plan_ada(i, part):
            w = io["w_ada_2"][0][:, i * BANK:(i + 1) * BANK].rearrange("(k p) n -> p k n", p=P)
            W.plan_raw(f"ada{i}_{part}", [w[:, 4 * part:4 * part + 4, :]])

        def with_ada(i, part, k0=4):
            return {k0: lambda: plan_ada(i, part)}

        for i in range(4):
            W.plan_split(f"mg{i}", w_in, O_MG + i * BANK, BANK)
        for i in range(2):
            W.plan_split(f"branch_a{i}", io["w_branch_a"][0], i * BANK, BANK)
        for i in range(2):
            W.plan_split(f"branch_b{i}", io["w_branch_b"][0], i * BANK, BANK)
        for i in range(2):
            W.plan_split(f"w_out{i}", io["w_out"][0], i * BANK, BANK, before=with_ada(0, i))

        ffn_chunks = [(c0, min(BANK, DFF - c0)) for c0 in range(0, DFF, BANK)]
        assert len(ffn_chunks) == 6 and KD == 8
        for i, (c0, n) in enumerate(ffn_chunks):
            W.plan_split(f"gate{i}", io["w_gate"][0], c0, n, before=with_ada(i + 1, 0) if n == BANK else None)
            W.plan_split(f"up{i}", io["w_up"][0], c0, n, before=with_ada(i + 1, 1) if n == BANK else None)
        for i in range(2):
            W.plan_split(f"down{i}", io["w_down"][0], i * BANK, BANK,
                         before={**with_ada(6 + i, 0, 4), **with_ada(6 + i, 1, 12)})
        GU = NG2 + MW
        in2 = [("q2", 0, BANK), ("gu0", 4 * MW, GU // 2), ("k2", MW, BANK), ("v2", 2 * MW, BANK),
               ("gu1", 4 * MW + GU // 2, GU // 2), ("o2", 3 * MW, BANK)]
        in2_ada = {"q2": (8, 0), "k2": (8, 1), "v2": (9, 0), "o2": (9, 1)}
        for i, (name, c0, n) in enumerate(in2):
            W.plan_split(name, w_in2, c0, n, before=with_ada(*in2_ada[name]) if name in in2_ada else None)
        for i in range(2):
            W.plan_split(f"w_out2_{i}", io["w_out_2"][0], i * BANK, BANK, starts=(4, 0))
        ff1_ada = {0: (10, 0), 1: (10, 1), 2: (11, 0), 3: (11, 1)}
        for i in range(DFF2 // BANK):
            W.plan_split(f"ff1_{i}", io["w_ff1_2"][0], i * BANK, BANK,
                         before=with_ada(*ff1_ada[i]) if i in ff1_ada else None)
        for i in range(2):
            W.plan_split(f"ff2_{i}", io["w_ff2_2"][0], i * BANK, BANK)

        bank_turn = {"tr": 0, "aux": 0}

        def next_bank(kind):
            group = {"tr": tr_banks, "aux": aux_banks}[kind]
            bank_turn[kind] += 1
            return group[bank_turn[kind] % len(group)]

        later = []

        def put_off(steps, *works):
            later.extend([steps, w] for w in works)

        def tick():
            for entry in later:
                entry[0] -= 1
            due = [entry for entry in later if entry[0] <= 0]
            later[:] = [entry for entry in later if entry[0] > 0]
            for _, work in due:
                work()

        def run_later():
            while later:
                entry = min(later, key=lambda e: e[0])
                later.remove(entry)
                entry[1]()

        def linear(name, in_h, in_l, ready, banks_by_tile, evacuate, k_first=0, boundary=False):
            units = W.chunks[name]
            W.prepare_through(units[0]["index"] + SPLIT_UNITS - 1)
            rest = len(units) % SPLIT_UNITS
            groups = [units[:rest]] if rest else []
            groups += [units[i:i + SPLIT_UNITS] for i in range(rest, len(units), SPLIT_UNITS)]
            for group in groups:
                for t in range(NT):
                    ts = slice(t * P, (t + 1) * P)
                    for u in group:
                        W.prepare_through(u["index"])
                        assert W.prepared > u["index"]
                        if u["opens"]:
                            pe.wait(banks_by_tile[t].readers)
                        pe.wait(u["high_ready"], u["low_ready"])
                        dst = banks_by_tile[t].ap[:, 0:u["n"]]
                        for j in range(u["kn"]):
                            k = u["k0"] + j
                            assert ready[k // 4][t] is not None
                            pe.wait(ready[k // 4][t])
                            xh, xl = in_h[:, k_first + k, ts], in_l[:, k_first + k, ts]
                            wh, wl = u["high"][:, j, :], u["low"][:, j, :]
                            start, stop = u["opens"] and j == 0, u["closes"] and j == u["kn"] - 1
                            pe.engine.matmul(dst, xh, wh, start=start, stop=False)
                            pe.engine.matmul(dst, xl, wh, start=False, stop=False)
                            last = pe.engine.matmul(dst, xh, wl, start=False, stop=stop)
                        mark = pe.mark(last)
                        if t == NT - 1:
                            u["used"] = mark
                            if boundary and u in units[-3:]:
                                W.split_high(u["index"] + SPLIT_UNITS)
                            else:
                                W.prepare_through(u["index"] + SPLIT_UNITS)
                        tick()
                        if u["closes"]:
                            if boundary and t == NT - 1:
                                W.prepare_through(u["index"] + 2)
                            evacuate(t, mark)
                        yield mark

        def run(chunk):
            done = None
            for done in chunk:
                pass
            return done

        def transpose_tiles(sources, marks, kind="tr"):
            bank = next_bank(kind)
            pe.wait(bank.readers)
            pe.wait(*marks)
            for i, s in enumerate(sources):
                last = pe.engine.transpose(bank.ap[0:s.shape[1], i * P:i * P + s.shape[0]], s,
                                           ident[0:s.shape[0], 0:s.shape[0]])
            return bank, pe.mark(last)

        def split_from(bank, mark, dst_h, dst_l, free, shape=None):
            n = dst_h.shape[1]
            src = bank.ap[:, 0:n * P].rearrange("p (k n) -> p k n", k=n)
            act.wait(mark, *free)
            h = act.mark(act.engine.activation(dst_h, src, ACT.Copy))
            dve.wait(mark, h, *free)
            l = dve.mark(dve.engine.tensor_tensor(dst_l, src, dst_h.bitcast(F32), ALU.subtract))
            bank.readers = [h, l]
            return [h, l]

        def to_features(tile, n, t, marks, in_h, in_l, k0, free):
            out_marks = []
            for g in range(0, n, 4):
                m = min(4, n - g)
                bank, mark = transpose_tiles([tile[:, (g + i) * P:(g + i + 1) * P] for i in range(m)], marks)
                dst = slice(k0 + g, k0 + g + m)
                out_marks.append(split_from(bank, mark, in_h[:, dst, t * P:(t + 1) * P],
                                            in_l[:, dst, t * P:(t + 1) * P], free))
            return out_marks

        stat_at = [0]

        def columns(n):
            stat_at[0] += n
            return stat[:, stat_at[0] - n:stat_at[0]]

        def inverse_rms(sums, width, count, mark):
            pool.wait(mark)
            m = pool.mark(pool.engine.tensor_scalar(sums, sums, 1.0 / width, NORM_EPS, ALU.mult, ALU.add))
            pool.wait(m)
            return pool.mark(pool.engine.tensor_tensor(sums, sums, minus_half[:, 0:count], ALU.pow))

        def half(h):
            return slice(h * BANK, (h + 1) * BANK)

        def square_half(t, h, sums, mark, unused, src=None):
            src = x[:, t, half(h)] if src is None else src
            act.wait(mark)
            return act.mark(act.engine.activation(unused, src, ACT.Square, scale=D ** -0.5,
                                                  accum_out=sums[:, h:h + 1]))

        def scale_from(sums, marks):
            col = columns(1)
            dve.wait(*marks)
            m = dve.mark(v.tensor_scalar(col, sums[:, 0:1], sums[:, 1:2], NORM_EPS, ALU.add, ALU.add))
            pool.wait(m, half_set)
            return col, pool.mark(pool.engine.tensor_tensor(col, col, minus_half[:, 0:1], ALU.pow))

        def turned(tile, t, mark, in_h, in_l, k0, free, out):
            def work():
                out[t].extend(to_features(tile, tile.shape[1] // P, t, [mark], in_h, in_l, k0, free))
            return work

        v = dve.engine

        def chain(ins):
            m = dve.mark(ins)
            dve.wait(m)
            return m

        load_x = lambda t: load(x[:, t, :], x_in[0, t * P:(t + 1) * P, :], queue=sp)
        x_landed = [load_x(0)]
        angles_landed = load(cst[:, 3 * P:], consts[:, 3 * P:], queue=act)
        row_a_full = load(row_a[:, :], io["attn_norm_g"].to_broadcast([P, D]), queue=act)
        ident_landed = load(cst[:, 0:P], consts[:, 0:P], queue=sp)
        W.pump(1)
        x_landed.append(load_x(1))
        W.pump()
        masks_landed = load(cst[:, P:3 * P], consts[:, P:3 * P], queue=act)
        cst_landed = [ident_landed, angles_landed, masks_landed]
        ones_set = pool.mark(pool.engine.memset(ones[:, :], 1.0))
        half_set = pool.mark(pool.engine.memset(minus_half[:, :], -0.5))
        pool.wait(half_set)
        rows_zero = pool.mark(pool.engine.memset(vec_rows[:, :], 0.0))
        pool.wait(rows_zero)
        pos_i = sb("positions_int", [P, NT], I32)
        pos_landed = load(pos_i[:, :], io["positions"][0].rearrange("(t p) -> p t", p=P), scattered=True)
        lam_rows = sb("lambda_rows", [P, 4, DH])
        lam_landed = load(lam_rows[:, :, :], io["diff_lambda"][0].partition_broadcast(P))
        V_PEK, V_PEV, V_C, V_PS = 0, CMP_J, 2 * CMP_J, 2 * CMP_J + KD

        vecs = [load(vec_rows[V_PEK:V_PEK + CMP_J, :], io["cmp_pe_k"][0].rearrange("(j a) d -> j (a d)", a=2), rows_zero),
                load(vec_rows[V_PEV:V_PEV + CMP_J, :], io["cmp_pe_v"][0].rearrange("(j a) d -> j (a d)", a=2), rows_zero),
                load(vec_rows[V_C:V_C + KD, :], io["c_2"].rearrange("a (k p) -> (a k) p", p=P), rows_zero),
                load(vec_rows[V_PS:V_PS + PG, :], io["pool_scale_2"].rearrange("a (k p) -> (a k) p", p=P), rows_zero)]

        mixer = ExitStack()
        ctx.enter_context(mixer)

        def mb(name, shape, dtype=F32):
            return sb(name, shape, dtype, stack=mixer)

        pj = mb("projected", [P, NT, O_MG])
        mg = mb("merge_gates", [P, NT, 2 * D])
        dqT = mb("diff_qT", [P, DIFF_H, 2, T])
        dkT = mb("diff_kT", [P, DIFF_H, T])
        nqT = mb("nsa_qT", [P, HPG, T])
        kswT = mb("nsa_kT", [P, 2, T])
        E = row_cd[:, :, :].rearrange("p a (b n) -> p (a b) n", n=BANK)
        PT = mb("probsT", [P, 3, BANK])
        pcT = mb("cmp_probsT", [P, NT, G * P])
        g_sub = mb("subln_row", [P, P])
        w2k = mb("cmp_k_w2", [P, KH, DH])
        w2v = mb("cmp_v_w2", [P, KH, DH])
        cosT = mb("cos", [P, NT, 2, HALF])
        sinT = mb("sin", [P, NT, 2, HALF])
        x2T = mg[:, 0, D:2 * D].rearrange("p (g v t) -> p g v t", g=G, v=2)
        blk = mg[:, 1, D:D + 2 * CMP_J * G * NC].rearrange("p (v j c) -> p v j c", v=2, j=CMP_J)
        hv4 = mb("cmp_hidden_spread", [P, G, KH, HPG, CPAD])
        vbd = mb("cmp_v_blocks", [P, G, HPG, DH])
        cmp_f = mb("cmp_small", [P, 2, 2 * KH * G * NC])
        kcd = mb("cmp_kT", [P, NC])
        pc = mb("cmp_probs", [P, NT, NSA_H, CPAD])

        angles = E[:, 0, 0:NT * 2 * HALF].rearrange("p (t s d) -> p t s d", t=NT, s=2)
        turns = E[:, 1, 0:NT * 2 * HALF].rearrange("p (t s d) -> p t s d", t=NT, s=2)

        def count_turns():
            dve.wait(pos_landed, angles_landed)
            chain(v.tensor_copy(small[:, 0:NT], pos_i[:, :]))
            for t in range(NT):
                for s_ in range(2):
                    m = dve.mark(v.tensor_scalar(angles[:, t, s_, :], inv_freq, small[:, t:t + 1], None, ALU.mult))
            dve.wait(m)
            for s_, quarter in ((0, 0.25), (1, 0.0)):
                m = dve.mark(v.tensor_scalar(turns[:, :, s_, :], angles[:, :, s_, :], 0.15915494309189535, quarter,
                                             ALU.mult, ALU.add))
            dve.wait(m)
            chain(v.tensor_scalar(turns[:, :, :, :], turns[:, :, :, :], MAGIC, None, ALU.add))
            chain(v.tensor_scalar(turns[:, :, :, :], turns[:, :, :, :], MAGIC, None, ALU.subtract))

        def take_turns_off():
            for part in TWO_PI_PARTS:
                chain(v.scalar_tensor_tensor(angles[:, :, :, :], turns[:, :, :, :], -part, angles[:, :, :, :],
                                             ALU.mult, ALU.add))
            chain(v.tensor_scalar(angles[:, :, 0, :], angles[:, :, 0, :], 1.5707963267948966, None, ALU.add))
            return chain(v.tensor_scalar(angles[:, :, :, :], angles[:, :, :, :], PI_BELOW, -PI_BELOW, ALU.min, ALU.max))

        x_ready, row_a_read = [[], []], []
        rms_x, rope_ready = [None, None], [None, None]

        def gained(t):
            dve.wait(x_landed[t], row_a_full)
            for h in range(2):
                row_a_read.append(dve.mark(v.tensor_tensor(xn[:, t, half(h)], x[:, t, half(h)], row_a[:, half(h)],
                                                           ALU.mult)))
            for h in range(2):
                put_off(2 * t + h, turned(xn[:, t, half(h)], t, row_a_read[-1], uT_h, uT_l, 4 * h, (), x_ready))

        pe.wait(ident_landed)
        gained(0)
        count_turns()
        run_later()
        W.prepare_through(SPLIT_UNITS - 1)
        gained(1)
        angles_ready = take_turns_off()
        u_ready = InputReady(x_ready)

        act.wait(cst_landed)
        act.engine.activation(ident_r[:, :], ident, ACT.Copy)
        act.engine.activation(after_r[:, :], cst[:, P:2 * P], ACT.Copy)
        masks_ready = act.mark(act.engine.activation(before_r[:, :], cst[:, 2 * P:3 * P], ACT.Copy))

        for t in range(NT):
            sums = columns(2)
            rms_x[t] = scale_from(sums, [square_half(t, h, sums, x_landed[t], (PT[:, h, :], E[:, 2 + h, :])[t])
                                        for h in range(2)])
        dq_zero = pool.mark(pool.engine.memset(dqT[:, :, :, :], 0.0))

        def rotation_tables():
            act.wait(angles_ready)
            for h in range(2):
                act.engine.activation(cosT[:, :, h, :], angles[:, :, 0, :], ACT.Sin)
                sin_done = act.mark(act.engine.activation(sinT[:, :, h, :], angles[:, :, 1, :], ACT.Sin))
            dve.wait(sin_done)
            chain(v.tensor_scalar(sinT[:, :, 0, :], sinT[:, :, 0, :], -1.0, None, ALU.mult))
            for t in range(NT):
                col, m = rms_x[t]
                dve.wait(m)
                for table in (cosT, sinT):
                    rope_ready[t] = dve.mark(v.tensor_scalar(table[:, t, :, :], table[:, t, :, :], col, None, ALU.mult))

        put_off(4, rotation_tables)

        marks = {}

        row_b_full = load(row_b[:, :], io["ffn_norm_g"].to_broadcast([P, D]))
        g_sub_full = load(g_sub[:, :], io["diff_subln_g"].to_broadcast([P, P]))
        w2_full = [load(w2k[:, :, :], io["cmp_k_w2"][0].rearrange("(k p) n -> p k n", p=P)),
                   load(w2v[:, :, :], io["cmp_v_w2"][0].rearrange("(k p) n -> p k n", p=P))]
        row_a_full = load(row_a[:, :], io["final_norm_g"].unsqueeze(0).to_broadcast([P, D]), *row_a_read)

        def lambda_and_vectors():
            dve.wait(lam_landed)
            lam_pair = lam_rows[:, :, :].rearrange("p (a b) d -> p a b d", a=2)
            chain(v.tensor_tensor(lam_rows[:, 0:2, :], lam_pair[:, :, 0, :], lam_pair[:, :, 1, :], ALU.mult))
            m = chain(v.tensor_reduce(small[:, 2:4], lam_rows[:, 0:2, :], AX.X, ALU.add))
            act.wait(m)
            m = act.mark(act.engine.activation(small[:, 4:6], small[:, 2:4], ACT.Exp))
            dve.wait(m)
            chain(v.tensor_tensor(small[:, 6:7], small[:, 5:6], small[:, 4:5], ALU.subtract))
            marks["lambda"] = chain(v.tensor_scalar(neg_lam, neg_lam, -LAM_INIT, None, ALU.add))

            bank, m = transpose_tiles([vec_rows[:, :]], [rows_zero] + vecs)
            dve.wait(m)
            marks["vectors"] = chain(v.tensor_copy(vec_cols[:, :], bank.ap[:, 0:64]))
            bank.readers = [marks["vectors"]]
            c_col = vec_cols[:, V_C:V_C + KD]
            act.wait(marks["vectors"])
            m = act.mark(act.engine.activation(small[:, 8:8 + KD], c_col, ACT.Exp, scale=-1.0))
            dve.wait(m)
            chain(v.tensor_scalar(small[:, 8:8 + KD], small[:, 8:8 + KD], 1.0, None, ALU.add))
            chain(v.reciprocal(small[:, 8:8 + KD], small[:, 8:8 + KD]))
            marks["c"] = chain(v.tensor_tensor(c_act[:, :], c_col, small[:, 8:8 + KD], ALU.mult))

        neg_lam = small[:, 6:7]
        put_off(12, lambda_and_vectors)

        rope_free = [[], []]

        def rope(bank, mark, c0, n, t, dst):
            heads = n // DH
            src = bank.ap[:, c0:c0 + n].rearrange("p (h s d) -> p h s d", h=heads, s=2)
            straight = E[:, 2 * t, c0:c0 + n]
            crossed = E[:, 2 * t + 1, c0:c0 + n]
            pairs_of = lambda a: a.rearrange("p (h s d) -> p h s d", h=heads, s=2)
            cos = cosT[:, t, :, :].unsqueeze(1).to_broadcast([P, heads, 2, HALF])
            sin = sinT[:, t, :, :].unsqueeze(1).to_broadcast([P, heads, 2, HALF])
            dve.wait(mark, rope_ready[t], rope_free[t])
            v.tensor_tensor(pairs_of(straight), src, cos, ALU.mult)
            m = dve.mark(v.tensor_tensor(pairs_of(crossed), src[:, :, ::-1, :], sin, ALU.mult))
            pool.wait(m)
            if len(dst.shape) == 4:
                straight, crossed = (s.rearrange("p (g j d) -> p g j d", g=G, d=DH) for s in (straight, crossed))
            done = pool.mark(pool.engine.tensor_tensor(dst, straight, crossed, ALU.add))
            return m, done

        def copy_out(lane, dst, src, marks, scale=None):
            lane.wait(*marks)
            if lane is act:
                if scale is None:
                    return act.mark(act.engine.activation(dst, src, ACT.Copy))
                return act.mark(act.engine.activation(dst, src, ACT.Copy, scale=scale))
            if scale is None:
                return dve.mark(v.tensor_copy(dst, src))
            return dve.mark(v.tensor_scalar(dst, src, scale, None, ALU.mult))

        proj_done = {name: [None, None] for name in ("dq", "dk", "dv", "nq", "kc", "vc", "ks", "vs", "kw", "gates",
                                                     "dqT", "dkT", "nqT")}
        pairs = [acc[0:2], acc[2:4]]
        Q_SCALE = DH ** -0.5

        def heads_T(name, t, c0, n_tiles, dst, scale):
            def work():
                tiles = [pj[:, t, c0 + i * P:c0 + (i + 1) * P] for i in range(n_tiles)]
                bank, mark = transpose_tiles(tiles, [proj_done[name][t]])
                src = bank.ap[:, 0:n_tiles * P].rearrange("p (k n) -> p k n", k=n_tiles)
                ts = slice(t * P, (t + 1) * P)
                if name == "dq":
                    for c in range(2):
                        rows = slice(c * DH, (c + 1) * DH)
                        m = copy_out(act, dst[rows, :, c, ts], src[rows, :, :], [mark, dq_zero], scale)
                else:
                    m = copy_out(act, dst[:, :, ts], src, [mark], scale)
                bank.readers = [m]
                proj_done[name + "T"][t] = m
            return work

        rotated = {"dq": (O_DQ, dqT, Q_SCALE), "dk": (O_DK, dkT, None), "nq": (O_NQ, nqT, Q_SCALE)}

        def evacuate_heads(name, pair):
            c0, dst_T, scale = rotated[name]

            def work(t, done):
                dst = pj[:, t, c0:c0 + BANK]
                if name == "nq":
                    dst = dst.rearrange("p (j g d) -> p g j d", g=G, d=DH)
                read, proj_done[name][t] = rope(pair[t], done, 0, BANK, t, dst)
                pair[t].readers = [read]
                rope_free[t] = [proj_done[name][t]]
                put_off(5, heads_T(name, t, c0, 4, dst_T, scale))
            return work

        def evacuate_kva(pair):
            def work(t, done):
                m1, proj_done["kc"][t] = rope(pair[t], done, 0, KV, t, pj[:, t, O_KC:O_KC + KV])
                m2, proj_done["ks"][t] = rope(pair[t], done, 2 * KV, KV, t, pj[:, t, O_KS:O_KS + KV])
                r, r_done = rms_x[t]
                m3 = copy_out(act, pj[:, t, O_VC:O_VC + KV], pair[t].ap[:, KV:2 * KV], [done, m2, r_done], r)
                pair[t].readers = [m2, m3]
                rope_free[t] = [proj_done["ks"][t]]
                proj_done["vc"][t] = m3
                if t == NT - 1:
                    put_off(5, sources_T)
                    put_off(8, compress_blocks)
            return work

        def evacuate_kvb(pair):
            def work(t, done):
                m1, proj_done["kw"][t] = rope(pair[t], done, KV, KV, t, pj[:, t, O_KW:O_KW + KV])
                r, r_done = rms_x[t]
                m2 = copy_out(act, pj[:, t, O_VS:O_VS + KV], pair[t].ap[:, 0:KV], [done, m1, r_done], r)
                m3 = copy_out(act, pj[:, t, O_VW:O_VW + KV + N_GATES], pair[t].ap[:, 2 * KV:3 * KV + N_GATES], [done], r)
                pair[t].readers = [m1, m3]
                rope_free[t] = [proj_done["kw"][t]]
                proj_done["vs"][t] = m3
                act.wait(m3)
                m = act.mark(act.engine.activation(gates[t], gates[t], ACT.Exp, scale=-1.0))
                dve.wait(m)
                chain(v.tensor_scalar(gates[t], gates[t], 1.0, None, ALU.add))
                proj_done["gates"][t] = chain(v.reciprocal(gates[t], gates[t]))
                if t == NT - 1:
                    put_off(5, keys_T)
            return work

        def evacuate_dv(pair):
            def work(t, done):
                proj_done["dv"][t] = copy_out(act, pj[:, t, O_DV:O_DV + DIFF_W], pair[t].ap[:, :],
                                                 [done, rms_x[t][1]], rms_x[t][0])
                pair[t].readers = [proj_done["dv"][t]]
            return work

        gates = [pj[:, t, O_NG:O_NG + N_GATES] for t in range(NT)]
        ksw_done, x2_done, blk_done = [], [], []

        def sources_T():
            tiles = [pj[:, t, c:c + KV] for c in (O_KC, O_VC) for t in range(NT)]
            bank, mark = transpose_tiles(tiles, proj_done["kc"] + proj_done["vc"])
            src = bank.ap[:, :].rearrange("p (v t) -> p v t", v=2)
            got = []
            for g in range(G):
                got.append(copy_out(act, x2T[0:DH, g, :, :], src[g * DH:(g + 1) * DH, :, :], [mark]))
            for g in range(G):
                got.append(copy_out(dve, x2T[DH:P, g, :, 0:T - 1], src[g * DH:(g + 1) * DH, :, 1:T], [mark, got[1]]))
            bank.readers = got
            x2_done.extend(got)

        def keys_T():
            tiles = [pj[:, t, c:c + KV] for c in (O_KS, O_KW) for t in range(NT)]
            bank, mark = transpose_tiles(tiles, proj_done["ks"] + proj_done["kw"])
            m = copy_out(act, kswT[:, :, :], bank.ap[:, :].rearrange("p (w t) -> p w t", w=2), [mark])
            bank.readers = [m]
            ksw_done.append(m)

        def compress_blocks():
            pool.engine.memset(hv4[:, :, :, :, :], 0.0)
            pool.engine.memset(vbd[:, :, :, :], 0.0)
            marks["cmp_zero"] = pool.mark(pool.engine.memset(pc[:, :, :, :], 0.0))
            for kv in range(2):
                for g in range(G):
                    by = x2T[:, g, kv, :].rearrange("p (n j a) -> p j n a", j=CMP_J // 2, a=2)
                    for part in range(2):
                        js = slice(part * (CMP_J // 2), (part + 1) * (CMP_J // 2))
                        pe_col = vec_cols[:, (V_PEK, V_PEV)[kv] + js.start:(V_PEK, V_PEV)[kv] + js.stop]
                        pool.wait(x2_done, marks["vectors"])
                        blk_done.append(pool.mark(pool.engine.tensor_tensor(
                            blk[:, kv, js, g * NC:(g + 1) * NC], by[:, :, part:part + NC, 0],
                            pe_col.unsqueeze(2).to_broadcast([P, CMP_J // 2, NC]), ALU.add)))

        hid_n = KH * G * NC
        hT = {}

        def hidden_layer(kv):
            bank = next_bank("aux")
            pre = bank.ap[:, 0:hid_n]
            hid = pre.rearrange("p (m c) -> p m c", m=KH)
            pe.wait(bank.readers)
            slabs = W.chunks["cmp_" + "kv"[kv]]
            pe.wait(blk_done[4 * kv + 3], *[W.slabs[i]["landed"] for i in slabs])
            for m_ in range(KH):
                for j in range(CMP_J):
                    w1 = W.slab_view(slabs[j // (CMP_J // 2)])[:, j % (CMP_J // 2), m_ * P:(m_ + 1) * P]
                    last = pe.engine.matmul(hid[:, m_, :], w1, blk[:, kv, j, :], start=j == 0, stop=j == CMP_J - 1)
            done = pe.mark(last)
            for i in slabs:
                W.release(i, done)
            expo, hidden = cmp_f[:, 0, kv * hid_n:(kv + 1) * hid_n], cmp_f[:, 1, kv * hid_n:(kv + 1) * hid_n]
            act.wait(done)
            m = act.mark(act.engine.activation(expo, pre, ACT.Exp, scale=-1.0))
            dve.wait(m, done)
            chain(v.tensor_scalar(expo, expo, 1.0, None, ALU.add))
            chain(v.reciprocal(expo, expo))
            m = chain(v.tensor_tensor(hidden, pre, expo, ALU.mult))
            bank.readers = [m]
            hT[kv] = hidden.rearrange("p (m g c) -> p m g c", m=KH, g=G)
            marks[f"hid{kv}"] = m
            if kv == 1:
                dve.wait(marks["cmp_zero"])
                for g in range(G):
                    for m_ in range(KH):
                        marks["hv4"] = dve.mark(v.tensor_copy(hv4[:, g, m_, :, 0:NC],
                                                              hT[1][:, m_, g, :].unsqueeze(1).to_broadcast([P, HPG, NC])))

        def compressed_kv():
            bank = next_bank("aux")
            pe.wait(bank.readers)
            pe.wait(marks["hid0"], marks["hv4"], w2_full)
            for g in range(G):
                for m_ in range(KH):
                    pe.engine.matmul(bank.ap[g * DH:(g + 1) * DH, 0:NC], w2k[:, m_, :], hT[0][:, m_, g, :],
                                     start=m_ == 0, stop=m_ == KH - 1)
            for g in range(G):
                for m_ in range(KH):
                    last = pe.engine.matmul(bank.ap[:, 64 + g * DH:64 + (g + 1) * DH],
                                            hv4[:, g, m_, :, :], w2v[:, m_, :], start=m_ == 0, stop=m_ == KH - 1)
            done = pe.mark(last)
            marks["kcd"] = copy_out(act, kcd[:, :], bank.ap[:, 0:NC], [done])
            vals = bank.ap[:, 64:64 + G * DH].rearrange("p (g d) -> p g d", g=G)
            dve.wait(done, marks["kcd"])
            for j in range(HPG):
                rows = slice(j * CPAD, (j + 1) * CPAD)
                marks["vbd"] = dve.mark(v.tensor_copy(vbd[rows, :, j, :], vals[rows, :, :]))
            bank.readers = [marks["kcd"], marks["vbd"]]

        evacuate = {"kva": evacuate_kva, "kvb": evacuate_kvb, "dv": evacuate_dv}
        for i, name in enumerate(projections):
            pair = pairs[i % 2]
            empty = evacuate[name](pair) if name in evacuate else evacuate_heads(name, pair)
            if name in ("dk", "nq"):
                put_off(4, lambda kv=("dk", "nq").index(name): hidden_layer(kv))
            if name == "dv":
                put_off(4, compressed_kv)
            run(linear(name, uT_h, uT_l, u_ready, pair, empty))

        mg_done = {}
        xa_done = {}

        def filler_chunks():
            for i in range(4):
                pair = pairs[0]

                def empty(t, done, i=i, pair=pair):
                    mg_done[i, t] = copy_out(act, mg[:, t, half(i)], pair[t].ap[:, :],
                                             [done] + ([blk_done[-1], marks["hid1"]] if i >= 2 else []), rms_x[t][0])
                    pair[t].readers = [mg_done[i, t]]
                    if i == 3:
                        gates_products[t] = done
                        put_off(1 + t, turned(pj[:, t, O_DQ:O_DQ + DIFF_W], t, ya_done[t], uT_h, uT_l, 0, [done], ready_a))
                for mark in linear(f"mg{i}", uT_h, uT_l, u_ready, pair, empty):
                    yield mark
            for i in range(2):
                def empty(t, done, i=i, pair=pairs[0]):
                    xa_done[i, t] = copy_out(act, xn[:, t, half(i)], pair[t].ap[:, :], [done])
                    pair[t].readers = [xa_done[i, t]]
                for mark in linear(f"branch_a{i}", uT_h, uT_l, InputReady(ready_a), pairs[0], empty):
                    yield mark
            marks["branch_a_products"] = mark

        ready_a, ready_b, gates_products = [[], []], [[], []], {}
        filler = filler_chunks()

        def fill(n=1):
            for _ in range(n):
                next(filler, None)

        e_free, pt_free = [[] for _ in range(4)], [[] for _ in range(3)]
        e_free[0] = e_free[1] = rope_free[0]
        e_free[2] = e_free[3] = rope_free[1]
        sums4 = mb("score_sums", [P, 4, 2])
        nmax = mb("score_negmax", [P, 4, 2])
        inv = mb("score_scales", [P, 4, 2])
        o_banks = [acc[2], acc[3]]
        ya_done, yb_done = [None, None], [None, None]
        state = {}

        def item_scores(n, kind, h, q):
            width = (q + 1) * P
            bank = next_bank("aux")
            s = bank.ap[:, 0:2 * width].rearrange("p (c w) -> p c w", c=2)
            pe.wait(bank.readers)
            pe.wait(masks_ready)
            if kind == "diff":
                pe.wait(*proj_done["dqT"], *proj_done["dkT"])
                for c in range(2):
                    pe.engine.matmul(s[:, c, :], dqT[:, h, c, q * P:(q + 1) * P], dkT[:, h, 0:width],
                                     start=c == 0, stop=False, skip_group_check=True)
            else:
                pe.wait(*proj_done["nqT"], ksw_done)
                rows = slice((h // HPG) * DH, (h // HPG + 1) * DH)
                pe.engine.matmul(s, nqT[rows, h % HPG, q * P:(q + 1) * P], kswT[rows, :, 0:width],
                                 start=True, stop=False, skip_group_check=True)
            done = pe.mark(pe.engine.matmul(s[:, :, width - P:width], ident_r[:, :],
                                            after_r[:, :].unsqueeze(1).to_broadcast([P, 2, P]),
                                            start=False, stop=True, skip_group_check=True))
            dve.wait(done)
            max_ready = dve.mark(v.tensor_reduce(nmax[:, n % 4, :], s, AX.X, ALU.max, negate=True))
            e = E[:, n % 4, 0:2 * width].rearrange("p (c w) -> p c w", c=2)
            act.wait(done, max_ready, e_free[n % 4])
            for c in range(2):
                m = act.mark(act.engine.activation(e[:, c, :], s[:, c, :], ACT.Exp, bias=nmax[:, n % 4, c:c + 1],
                                                   accum_out=sums4[:, n % 4, c:c + 1]))
            bank.readers = [m]
            state[n] = {"e": e, "exp": m}

        def item_weights(n, kind, h, q):
            st = state[n]
            e, r = st["e"], inv[:, n % 4, :]
            dve.wait(st["exp"])
            chain(v.reciprocal(r, sums4[:, n % 4, :]))
            if kind == "diff":
                dve.wait(marks["lambda"])
                chain(v.tensor_scalar(e[:, 1, :], e[:, 1, :], r[:, 1:2], neg_lam, ALU.mult, ALU.mult))
                st["w"] = dve.mark(v.scalar_tensor_tensor(e[:, 0, :], e[:, 0, :], r[:, 0:1], e[:, 1, :], ALU.mult, ALU.add))
            else:
                dve.wait(proj_done["gates"][q])
                for c in range(2):
                    gate = gates[q][:, (1 + c) * NSA_H + h:(1 + c) * NSA_H + h + 1]
                    st["w"] = dve.mark(v.tensor_scalar(e[:, c, :], e[:, c, :], r[:, c:c + 1], gate, ALU.mult, ALU.mult))

        def item_transposes(n, kind, h, q):
            st = state[n]
            st["tiles"] = [(c, b) for c in range(1 if kind == "diff" else 2) for b in range(q + 1)]
            bank, mark = transpose_tiles([st["e"][:, c, b * P:(b + 1) * P] for c, b in st["tiles"]], [st["w"]])
            e_free[n % 4] = [mark]
            size = len(st["tiles"]) * P
            st["pT"] = copy_out(act, PT[:, n % 3, 0:size], bank.ap[:, 0:size], [mark] + pt_free[n % 3])
            bank.readers = [st["pT"]]

        def item_values(n, kind, h, q):
            st = state[n]
            pT = PT[:, n % 3, :].rearrange("p (b q) -> p b q", q=P)
            if kind == "nsa" and h == 0:
                open_values(q)
            pe.wait(st["pT"], *proj_done["dv"], *proj_done["vs"])
            if h == 0 and kind == "diff":
                pe.wait(o_banks[q].readers)
            for i, (c, b) in enumerate(st["tiles"]):
                if kind == "diff":
                    last = pe.engine.matmul(o_banks[q].ap[:, h * P:(h + 1) * P], pT[:, i, :],
                                            pj[:, b, O_DV + h * P:O_DV + (h + 1) * P], start=i == 0, stop=b == q)
                else:
                    c0 = (O_VS, O_VW)[c] + (h // HPG) * DH
                    last = pe.engine.matmul(o_banks[q].ap[:, h * DH:(h + 1) * DH], pT[:, i, :], pj[:, b, c0:c0 + DH],
                                            start=False, stop=i == len(st["tiles"]) - 1, skip_group_check=True)
            mark = pe.mark(last)
            pt_free[n % 3] = [mark]
            if kind == "diff" and h == DIFF_H - 1:
                sublayer_norm(q, mark)
            if kind == "nsa" and h == NSA_H - 1:
                yb_done[q] = copy_out(act, pj[:, q, O_NQ:O_NQ + NSA_W], o_banks[q].ap[:, :], [mark])
                o_banks[q].readers = [yb_done[q]]
                put_off(1, turned(pj[:, q, O_NQ:O_NQ + NSA_W], q, yb_done[q], uT_h, uT_l, 4, [gates_products[q]], ready_b))

        def sublayer_norm(t, mark):
            heads = lambda a: a.rearrange("p (h e) -> p h e", h=DIFF_H)
            src, y, sq = o_banks[t].ap[:, :], pj[:, t, O_DQ:O_DQ + DIFF_W], pj[:, t, O_DK:O_DK + DIFF_W]
            s4 = columns(4)
            act.wait(mark)
            squared = act.mark(act.engine.activation(sq, src, ACT.Square))

            def work():
                dve.wait(squared, mark, g_sub_full)
                rms = inverse_rms(s4, 2 * DH, DIFF_H, chain(v.tensor_reduce(s4, heads(sq), AX.X, ALU.add)))
                g_all = g_sub[:, :].unsqueeze(1).to_broadcast([P, DIFF_H, P])
                m = dve.mark(v.scalar_tensor_tensor(heads(sq), heads(src), 1.0 - LAM_INIT, g_all, ALU.mult, ALU.mult))
                o_banks[t].readers = [m]
                pool.wait(m, rms)
                ya_done[t] = pool.mark(pool.engine.tensor_tensor(heads(y), heads(sq),
                                                                 s4.unsqueeze(2).to_broadcast([P, DIFF_H, P]), ALU.mult))
            put_off(1, work)

        wide = lambda a: a.unsqueeze(2).to_broadcast([P, NSA_H, NC])
        each = lambda a: a.unsqueeze(1).to_broadcast([P, NSA_H, NC])

        def cmp_scores(q):
            bank = next_bank("aux")
            pe.wait(bank.readers)
            pe.wait(marks["kcd"], *proj_done["nqT"])
            for h in range(NSA_H):
                rows = slice((h // HPG) * DH, (h // HPG + 1) * DH)
                if h == HPG:
                    pe.wait(done)
                last = pe.engine.matmul(bank.ap[:, h * 16:h * 16 + NC], nqT[rows, h % HPG, q * P:(q + 1) * P],
                                        kcd[rows, :], start=True, stop=True)
                if h % HPG == HPG - 1:
                    done = pe.mark(last)
            sc = bank.ap[:, 0:NSA_H * 16].rearrange("p (h c) -> p h c", h=NSA_H)[:, :, 0:NC]
            p_ = pc[:, q, :, 0:NC]
            s8 = small[:, 16 + 16 * q:24 + 16 * q]
            dve.wait(done, marks["cmp_zero"], cst_landed)
            m = chain(v.tensor_tensor(p_, sc, each(cmp_add[:, q, :]), ALU.add))
            bank.readers = [m]
            chain(v.tensor_reduce(s8, p_, AX.X, ALU.max))
            m = chain(v.tensor_tensor(p_, p_, wide(s8), ALU.subtract))
            act.wait(m)
            marks[f"cmp_exp{q}"] = act.mark(act.engine.activation(p_, p_, ACT.Exp))

        def cmp_weights(q):
            p_ = pc[:, q, :, 0:NC]
            s8 = small[:, 16 + 16 * q:24 + 16 * q]
            dve.wait(marks[f"cmp_exp{q}"])
            chain(v.tensor_reduce(s8, p_, AX.X, ALU.add))
            chain(v.reciprocal(s8, s8))
            dve.wait(proj_done["gates"][q])
            chain(v.tensor_tensor(s8, s8, gates[q][:, 0:NSA_H], ALU.mult))
            chain(v.tensor_tensor(p_, p_, each(cmp_keep[:, q, :]), ALU.mult))
            marks[f"pc{q}"] = chain(v.tensor_tensor(p_, p_, wide(s8), ALU.mult))

        def cmp_transposes(q):
            flat = pc[:, q, :, :].rearrange("p h c -> p (h c)")
            bank, mark = transpose_tiles([flat[:, g * P:(g + 1) * P] for g in range(G)], [marks[f"pc{q}"]])
            marks[f"pcT{q}"] = copy_out(act, pcT[:, q, :], bank.ap[:, 0:G * P], [mark])
            bank.readers = [marks[f"pcT{q}"]]

        def open_values(q):
            pe.wait(marks[f"pcT{q}"], marks["vbd"], o_banks[q].readers)
            for g in range(G):
                pe.engine.matmul(o_banks[q].ap[:, g * HPG * DH:(g + 1) * HPG * DH], pcT[:, q, g * P:(g + 1) * P],
                                 vbd[:, g, :, :], start=g == 0, stop=False, skip_group_check=True)

        items = [("diff", h, q) for h in range(DIFF_H) for q in range(NT)] + \
                [("nsa", h, q) for h in range(NSA_H) for q in range(NT)]
        n_items = len(items)
        extras = {3: lambda: cmp_scores(0), 4: lambda: cmp_scores(1), 5: lambda: cmp_weights(0),
                  6: lambda: cmp_weights(1), 7: lambda: cmp_transposes(0), 8: lambda: cmp_transposes(1)}
        n_fill = 4 * 8 + 2 * 4
        TAIL = 6
        filled = 0
        for n in range(n_items + 3):
            if n < n_items:
                item_scores(n, *items[n])
            if 0 <= n - 1 < n_items:
                item_weights(n - 1, *items[n - 1])
            if n in extras:
                extras[n]()
            share = min(n_fill, (n + 1) * (n_fill - TAIL) // n_items)
            if n >= n_items:
                share = filled + 1
            fill(share - filled)
            filled = share
            for stage, work in ((2, item_transposes), (3, item_values)):
                if 0 <= n - stage < n_items:
                    work(n - stage, *items[n - stage])
        fill(n_fill)

        sig_done = {}

        def sigmoids(i, t):
            for b in range(2):
                gate = mg[:, t, half(2 * b + i)]
                act.wait(mg_done[2 * b + i, t])
                sig_done[b, i, t] = act.mark(act.engine.activation(gate, gate, ACT.Sigmoid))
            pool.wait(sig_done[0, i, t], xa_done[i, t])
            xa_done[i, t] = pool.mark(pool.engine.tensor_tensor(xn[:, t, half(i)], xn[:, t, half(i)],
                                                                mg[:, t, half(i)], ALU.mult))
        sigmoids(0, 0)
        sigmoids(0, 1)
        put_off(3, lambda: sigmoids(1, 0))
        put_off(4, lambda: sigmoids(1, 1))

        w_out_ready = [[None, None], [None, None]]

        def merge(i, pair):
            def work(t, done):
                other = mg[:, t, half(2 + i)]
                dve.wait(done, sig_done[1, i, t])
                m = chain(v.tensor_tensor(other, pair[t].ap[:, :], other, ALU.mult))
                pair[t].readers = [m]
                dve.wait(xa_done[i, t])
                m = dve.mark(v.tensor_tensor(xn[:, t, half(i)], xn[:, t, half(i)], other, ALU.add))

                def turn():
                    free = [marks["branch_a_products"]] if i == 0 else [done]
                    w_out_ready[i][t], = to_features(xn[:, t, half(i)], 4, t, [m], uT_h, uT_l, 4 * i, free)
                put_off(3, turn)
            return work

        for i in range(2):
            run(linear(f"branch_b{i}", uT_h, uT_l, InputReady(ready_b), pairs[i], merge(i, pairs[i]), k_first=4))

        ada_free = [[], []]
        ada_done = {}

        def ada_open(i):
            part = ada_acc[:, i % 2, :]
            pool.wait(ada_free[i % 2])
            zero = pool.mark(pool.engine.memset(part, 0.0))
            ada_last[i] = load(part[0:1, :], io["b_ada_2"][:, i * BANK:(i + 1) * BANK], zero)

        ada_last = {}

        def ada(i, part, first=0):
            slab, = W.chunks[f"ada{i}_{part}"]
            acc_i = ada_acc[:, i % 2, :]

            def row(k):
                def work():
                    w, c = W.slab_view(slab)[:, k % 4, :], c_act[:, k:k + 1]
                    dve.wait(W.slabs[slab]["landed"], marks["c"], ada_last[i])
                    ada_last[i] = dve.mark(v.scalar_tensor_tensor(acc_i, w, c, acc_i, ALU.mult, ALU.add))
                    if k % 4 == 3:
                        W.release(slab, ada_last[i])
                return work

            def finish():
                dst, how, dst_marks = ada_plan[i]
                bank = next_bank("aux")
                pe.wait(bank.readers)
                pe.wait(ada_last[i], ones_set)
                m = pe.mark(pe.engine.matmul(bank.ap[:, :], ones[:, :], acc_i, start=True, stop=True))
                ada_free[i % 2] = [m]
                before = [marks[name] for name in dst_marks]
                if how == "scale":
                    dve.wait(m, *before)
                    r = dve.mark(v.scalar_tensor_tensor(dst, bank.ap[:, :], 1.0, dst, ALU.add, ALU.mult))
                else:
                    r = copy_out(act, dst, bank.ap[:, :], [m] + before)
                bank.readers = [r]
                ada_done[i] = r
            if part == 1 and i + 1 < 12:
                ada_open(i + 1)
            for k in range(4):
                put_off(first + k, row(4 * part + k))
            if part == 1:
                put_off(first + 7, finish)

        def shift_scale_gate(shift, scale, gain, gate, gate_read):
            return [(shift[:, half(h)], "copy", []) for h in range(2)] + \
                   [(scale[:, half(h)], "scale", [gain]) for h in range(2)] + \
                   [(gate[:, half(h)], "copy", gate_read) for h in range(2)]
        ada_plan = shift_scale_gate(row_c, row_b, "g_mix_2", row_d, [])
        ada_open(0)

        turn_steps = ((SPLIT_UNITS, SPLIT_UNITS), (2, 3))

        def at_boundary(t, work):
            if t == 0:
                work()
            else:
                put_off(1, work)

        def residual(name, ready, in_h, in_l, stats, after=None):
            got = [[], []]

            def empty_into(i):
                def work(t, done):
                    dve.wait(done)
                    m = dve.mark(v.tensor_tensor(x[:, t, half(i)], pairs[i][t].ap[:, :], x[:, t, half(i)], ALU.add))
                    pairs[i][t].readers = [m]
                    got[t].append(square_half(t, i, stats[t], m, pairs[i][t].ap[:, :]))
                    pairs[i][t].readers = [got[t][-1]]
                    if after:
                        after(t, i, m, got[t], done)
                return work
            for i in range(2):
                if name == "down":
                    ada(6 + i, 0), ada(6 + i, 1, 8)
                else:
                    ada(0, i)
                done = run(linear(f"{name}{i}", in_h, in_l, ready, pairs[i], empty_into(i), boundary=i == 1))
            return got, done

        stats = [columns(2) for _ in range(NT)]
        ffn_ready, rms_ffn, row_b_read = [[], []], [None, None], []

        def ffn_norm(t, i, mark, squares, closed):
            dve.wait(mark, row_b_full)
            row_b_read.append(dve.mark(v.tensor_tensor(xn[:, t, half(i)], x[:, t, half(i)], row_b[:, half(i)], ALU.mult)))
            if i == 1:
                for h in range(2):
                    put_off((2, 3)[h] if t == 0 else (1, 2)[h],
                            turned(xn[:, t, half(h)], t, row_b_read[-1], uT_h, uT_l, 4 * h, [closed], ffn_ready))

                def scale():
                    rms_ffn[t] = scale_from(stats[t], squares)
                put_off(3, scale)
        _, done = residual("w_out", w_out_ready, uT_h, uT_l, stats, ffn_norm)
        mixer.close()

        late = sb("late_rows", [P, 2, D])
        row_e, row_f = late[:, 0, :], late[:, 1, :]

        ada_plan += shift_scale_gate(row_e, row_f, "g_ffn_2", row_d, ["row_d_read"])
        marks["g_ffn_2"] = load(row_f, io["g_ffn_2"].to_broadcast([P, D]), done)

        hidden_stack = ExitStack()
        ctx.enter_context(hidden_stack)
        hid_h = sb("hidden_high", [P, KF2, T], F32R, stack=hidden_stack)
        hid_l = sb("hidden_low", [P, KF2, T], F32R, stack=hidden_stack)

        ready = InputReady(ffn_ready)

        marks["g_mix_2"] = load(row_b[:, :], io["g_mix_2"].to_broadcast([P, D]), *row_b_read)

        hidden_ready = [[], []]
        for i, (c0, n) in enumerate(ffn_chunks):
            sl = xn[:, :, (i % 2) * BANK:(i % 2) * BANK + n]
            silus = {}

            def empty_gate(t, done, sl=sl, n=n, silus=silus):
                r, r_done = rms_ffn[t]
                act.wait(done, r_done)
                silus[t] = act.mark(act.engine.activation(sl[:, t, :], pairs[0][t].ap[:, 0:n], ACT.Silu, scale=r))
                pairs[0][t].readers = [silus[t]]

            def empty_up(t, done, sl=sl, n=n, c0=c0, silus=silus):
                dve.wait(silus[t], done)
                m = dve.mark(v.scalar_tensor_tensor(sl[:, t, :], pairs[1][t].ap[:, 0:n], rms_ffn[t][0], sl[:, t, :],
                                                    ALU.mult, ALU.mult))
                pairs[1][t].readers = [m]
                put_off(5, turned(sl[:, t, :], t, m, hid_h, hid_l, c0 // P, [], hidden_ready))
            if n == BANK:
                ada(i + 1, 0, 3 if i == 0 else 0)
            run(linear(f"gate{i}", uT_h, uT_l, ready, pairs[0], empty_gate))
            if n == BANK:
                ada(i + 1, 1)
            run(linear(f"up{i}", uT_h, uT_l, ready, pairs[1], empty_up))
        hidden_marks = InputReady(hidden_ready)

        y_stats = [columns(2) for _ in range(NT)]
        stats = [columns(2) for _ in range(NT)]

        mix2_ready, adds = [[], []], []

        def final_gain(t, i, mark, got, closed):
            dve.wait(mark, row_a_full)
            m = dve.mark(v.tensor_tensor(xn[:, t, half(i)], x[:, t, half(i)], row_a[:, half(i)], ALU.mult))
            row_a_read.append(m)
            act.wait(got[-1])
            got.append(square_half(t, i, y_stats[t], m, pairs[i][t].ap[:, :], src=xn[:, t, half(i)]))
            pairs[i][t].readers = [got[-1]]
            if i == 1:
                at_boundary(t, lambda: two_norms(t, got, closed))

        def two_norms(t, squares, closed):
            r = columns(2)
            q = columns(2)
            dve.wait(*squares)
            v.tensor_scalar(r[:, 0:1], stats[t][:, 0:1], stats[t][:, 1:2], NORM_EPS, ALU.add, ALU.add)
            chain(v.tensor_scalar(q[:, 0:1], y_stats[t][:, 0:1], y_stats[t][:, 1:2], None, ALU.add))
            chain(v.reciprocal(q[:, 1:2], r[:, 0:1]))
            m = chain(v.tensor_scalar(r[:, 1:2], q[:, 0:1], q[:, 1:2], NORM_EPS, ALU.mult, ALU.add))
            pool.wait(m)
            m = pool.mark(pool.engine.tensor_tensor(r, r, minus_half[:, 0:2], ALU.pow))
            dve.wait(m)
            chain(v.tensor_tensor(q[:, 0:1], r[:, 0:1], r[:, 1:2], ALU.mult))
            dve.wait(*[ada_done[a] for a in range(4)])
            for h in range(2):
                y = xn[:, t, half(h)]
                chain(v.scalar_tensor_tensor(y, y, q[:, 0:1], row_b[:, half(h)], ALU.mult, ALU.mult))
                m = dve.mark(v.tensor_tensor(y, y, row_c[:, half(h)], ALU.add))
                adds.append(m)
                put_off(turn_steps[t][h], turned(y, t, m, uT_h, uT_l, 4 * h, [closed], mix2_ready))

            def new_x():
                for h in range(2):
                    dve.wait(m, row_a_full)
                    row_a_read.append(dve.mark(v.scalar_tensor_tensor(x[:, t, half(h)], x[:, t, half(h)], r[:, 0:1],
                                                                      row_a[:, half(h)], ALU.mult, ALU.mult)))
                if t == NT - 1:
                    marks["g_final_2"] = load(row_a[:, :], io["g_final_2"].unsqueeze(0).to_broadcast([P, D]), *row_a_read)
            put_off(28 + 6 * t, new_x)

        row_a_read = []
        squares, down_done = residual("down", hidden_marks, hid_h, hid_l, stats, final_gain)
        hidden_stack.close()

        mix2 = ExitStack()
        ctx.enter_context(mix2)

        def m2(name, shape, dtype=F32):
            return sb(name, shape, dtype, stack=mix2)

        ready = InputReady(mix2_ready)

        vE = m2("v_and_one", [P, NT, H2, E2 + 1])
        so = m2("sigmoid_o", [P, NT, MW])
        u_pool = m2("pool_input", [P, NT, MW])
        qk = m2("q_k", [P, NT, 2 * MW])
        q2T = m2("q2T", [P, H2, T])
        k2T = m2("k2T", [P, H2, T])
        gtmp = m2("gate_scratch", [P, NT, 2, 2 * H2])
        gt = m2("gate_values", [P, NT, 2, 2, H2])
        gb = m2("gate_bias", [P, 2, 2, H2])
        gp = m2("gate_padded", [P, NT, 2, 64])
        rows2 = m2("gate_rows", [64, 2, T])
        scans = m2("gate_scans", [64, 3, T])
        cols2 = m2("gate_columns", [P, NT, 3, 64])
        expm = m2("exp_minus_m", [P, NT, 64])
        gh = m2("head_gain_row", [P, MW])
        wT = m2("decay_T", [P, 2, 3 * P])
        sT = m2("scoresT_weighted", [P, 2, 3 * P])
        hm = m2("heads_out", [P, NT, MW])
        hsq = m2("heads_squared", [P, NT, MW])
        dn = m2("denominators", [P, 4, NT])
        wp = m2("w_pool", [P, PG, P])
        window = m2("pool_matrix", [P, NT, PG, T])
        mixT = m2("pool_mixedT", [P, 2, T])
        ybT = m2("pool_outT", [P, PG, T])
        zeros = m2("zeros", [64, T])
        gb_full = [load(gb[:, :, j, :], io[n][0].partition_broadcast(P), down_done)
                   for j, n in ((0, "b_igate_2"), (1, "b_fgate_2"))]
        gh_full = load(gh[:, :], io["g_head_2"].to_broadcast([P, MW]), down_done)
        window_full = load(window[:, :, :, :], io["pool_matrix"].rearrange("p s (g t) -> p s g t", g=PG), down_done)
        wp_full = load(wp[:, :, :], io["w_pool_2"][0].rearrange("g c e -> c g e"), down_done)
        pool.wait(down_done)
        m = pool.mark(pool.engine.memset(zeros[:, :], 0.0))
        pool.wait(m)
        m = pool.mark(pool.engine.memset(gp[:, :, :, :], 0.0))
        set2 = pool.mark(pool.engine.memset(vE[:, :, :, E2:E2 + 1], 1.0))
        dve.wait(down_done)
        act.wait(down_done)

        k_scale = {"q2": E2 ** -0.5, "k2": None}
        qk_T = {"q2": [None, None], "k2": [None, None]}

        def turn_heads(name, t, col, dst, mark):
            def work():
                bank, m = transpose_tiles([qk[:, t, col + h * P:col + (h + 1) * P] for h in range(H2)], [mark])
                src = bank.ap[:, :].rearrange("p (k n) -> p k n", k=H2)
                qk_T[name][t] = copy_out(act, dst[:, :, t * P:(t + 1) * P], src, [m], k_scale[name])
                bank.readers = [qk_T[name][t]]
            return work

        zf = gt[:, :, :, 1, :]

        def gates_logs():
            a, b = (gtmp[:, :, q, :].rearrange("p t (d h) -> p t d h", d=2) for q in range(2))
            dve.wait(*g_marks, gb_full, set2)
            m = chain(v.tensor_tensor(gt[:, :, :, :, :], gt[:, :, :, :, :],
                                      gb[:, :, :, :].unsqueeze(1).to_broadcast([P, NT, 2, 2, H2]), ALU.add))
            act.wait(m)
            m = act.mark(act.engine.activation(a, zf, ACT.Abs))
            act.wait(m)
            m = act.mark(act.engine.activation(b, a, ACT.Exp, scale=-1.0))
            act.wait(m)
            marks["logs"] = act.mark(act.engine.activation(b, b, ACT.Ln, bias=1.0))
            for d in range(2):
                cols = slice(32 * d, 32 * d + H2)
                v.tensor_copy(gp[:, :, 0, cols], gt[:, :, d, 0, :])
            put_off(1, lambda: gates_padded(b))

        def gates_padded(b):
            dve.wait(marks["logs"])
            for d in range(2):
                cols = slice(32 * d, 32 * d + H2)
                m = dve.mark(v.scalar_tensor_tensor(gp[:, :, 1, cols], zf[:, :, d, :], 0.0, b[:, :, d, :],
                                                    ALU.min, ALU.subtract))
            gp_marks.append(m)
            put_off(2, gates_rows)
            put_off(6, gates_columns)

        g_marks, gp_marks, v2_marks, u_marks = [], [], [], [[], []]

        def gates_rows():
            bank = next_bank("aux")
            pe.wait(bank.readers)
            pe.wait(gp_marks)
            for q in range(2):
                for t in range(NT):
                    last = pe.engine.transpose(bank.ap[0:64, (q * NT + t) * P:(q * NT + t + 1) * P], gp[:, t, q, :], ident)
            done = pe.mark(last)
            m = copy_out(act, rows2[:, :, :], bank.ap[0:64, :].rearrange("p (q t) -> p q t", q=2), [done])
            bank.readers = [m]
            dve.wait(m, ones_set, set2)
            fw, bw = slice(0, 32), slice(32, 64)
            b_fw, b_bw = scans[fw, 2, :], scans[bw, 2, ::-1]
            one = ones[0:64, 0:1].to_broadcast([64, T])
            v.tensor_tensor_scan(b_fw, one[fw, :], rows2[fw, 1, :], 0.0, ALU.mult, ALU.add)
            chain(v.tensor_tensor_scan(b_bw, one[bw, :], rows2[bw, 1, ::-1], 0.0, ALU.mult, ALU.add))
            m = chain(v.tensor_tensor(scans[:, 0, :], rows2[:, 0, :], scans[:, 2, :], ALU.subtract))
            put_off(2, lambda: running_max(m))

        def running_max(c_ready):
            fw, bw = slice(0, 32), slice(32, 64)
            dve.wait(c_ready)
            v.tensor_tensor_scan(scans[fw, 1, :], zeros[fw, :], scans[fw, 0, :], 0.0, ALU.max, ALU.max)
            chain(v.tensor_tensor_scan(scans[bw, 1, ::-1], zeros[bw, :], scans[bw, 0, ::-1], 0.0, ALU.max, ALU.max))
            marks["scans"] = chain(v.tensor_tensor(scans[:, 2, :], scans[:, 2, :], scans[:, 1, :], ALU.add))

        def gates_columns():
            bank = next_bank("aux")
            pe.wait(bank.readers)
            pe.wait(marks["scans"])
            for t in range(NT):
                for q in range(3):
                    last = pe.engine.transpose(bank.ap[:, (t * 3 + q) * 64:(t * 3 + q + 1) * 64],
                                               scans[:, q, t * P:(t + 1) * P], ident[0:64, 0:64])
            done = pe.mark(last)
            src = bank.ap[:, 0:NT * 3 * 64].rearrange("p (t q r) -> p t q r", t=NT, q=3)
            dve.wait(done)
            v.tensor_copy(cols2[:, :, 0, :], src[:, :, 0, :])
            m1 = dve.mark(v.tensor_scalar(cols2[:, :, 1, :], src[:, :, 1, :], -1.0, None, ALU.mult))
            act.wait(done, m1)
            m2_ = act.mark(act.engine.activation(expm[:, :, :], src[:, :, 2, :], ACT.Exp, scale=-1.0))
            bank.readers = [m1, m2_]
            cols_done.extend([m1, m2_])

        cols_done = []
        pool_out = []
        pool_products = []

        def pooling_window(g):
            bank = next_bank("aux")
            pe.wait(bank.readers)
            pe.wait(window_full, u_marks)
            for s in range(NT):
                last = pe.engine.matmul(bank.ap[:, 0:T], u_pool[:, s, g * P:(g + 1) * P], window[:, s, g, :],
                                        start=s == 0, stop=s == NT - 1)
            done = pe.mark(last)
            marks[f"mixed{g}"] = copy_out(act, mixT[:, g % 2, :], bank.ap[:, 0:T], [done] + pool_products[g - 2:g - 1])
            bank.readers = [marks[f"mixed{g}"]]

        def pooling_map(g):
            bank = next_bank("aux")
            pe.wait(bank.readers)
            pe.wait(marks[f"mixed{g}"], wp_full)
            done = pe.mark(pe.engine.matmul(bank.ap[:, 0:T], wp[:, g, :], mixT[:, g % 2, :], start=True, stop=True))
            pool_products.append(done)
            dve.wait(done, marks["vectors"])
            m = dve.mark(v.tensor_scalar(ybT[:, g, :], bank.ap[:, 0:T], vec_cols[:, V_PS + g:V_PS + g + 1], None, ALU.mult))
            bank.readers = [m]
            pool_out.append(m)

        def empty_in2(name, n, pair):
            def work(t, done):
                src = pair[t].ap[:, 0:n]
                if name in ("q2", "k2"):
                    col, dst = (0, q2T) if name == "q2" else (MW, k2T)
                    m = copy_out(act, qk[:, t, col:col + MW], src, [done])
                    put_off(2, turn_heads(name, t, col, dst, m))
                elif name == "v2":
                    act.wait(done, set2)
                    m = act.mark(act.engine.activation(vE[:, t, :, 0:E2], src.rearrange("p (h e) -> p h e", h=H2), ACT.Copy))
                    v2_marks.append(m)
                elif name == "o2":
                    act.wait(done)
                    m = act.mark(act.engine.activation(so[:, t, :], src, ACT.Sigmoid))
                    pool_tail[t] = done

                    def gated():
                        dve.wait(m, marks["head_scales"], *gained)
                        for h in range(H2):
                            cols = slice(h * E2, (h + 1) * E2)
                            g = dve.mark(v.scalar_tensor_tensor(hm[:, t, cols], hm[:, t, cols],
                                                                ms2[:, t * H2 + h:t * H2 + h + 1], so[:, t, cols],
                                                                ALU.mult, ALU.mult))
                        put_off(1, turned(hm[:, t, :], t, g, uT_h, uT_l, 0, [done], heads_ready))
                    put_off(4 if t == 0 else 2, gated)
                elif name == "gu0":
                    m1 = copy_out(dve, gt[:, t, :, :, :].rearrange("p a b c -> p (a b c)"), src[:, 0:NG2], [done])
                    m = copy_out(dve, u_pool[:, t, 0:n - NG2], src[:, NG2:n], [done])
                    u_marks[t].append(m)
                    g_marks.append(m1)
                    if t == NT - 1:
                        put_off(2, gates_logs)
                else:
                    m = copy_out(act, u_pool[:, t, n - NG2:MW], src, [done])
                    u_marks[t].append(m)
                pair[t].readers = [m]
            return work

        w_free, s_free = [[], []], [[], []]

        def scores2(h):
            bank = acc[h % 2]
            pe.wait(bank.readers)
            pe.wait(qk_T["q2"], qk_T["k2"])
            for s in range(NT):
                last = pe.engine.matmul(bank.ap[:, s * T:(s + 1) * T], k2T[:, h, s * P:(s + 1) * P], q2T[:, h, :],
                                        start=True, stop=True)
            bank.readers = []
            return bank, pe.mark(last)

        def decay(h, d):
            i = 2 * h + d
            r = 32 * d + h
            bank = tr_banks[i % 2]
            pe.wait(bank.readers)
            pe.wait(cols_done, masks_ready)
            for block, t in ((0, 0), (1, 1 - d), (2, 1)):
                pe.engine.matmul(bank.ap[:, block * P:(block + 1) * P], cols2[:, t, 1, r:r + 1].to_broadcast([P, P]), ident,
                                 start=block == 0, stop=False, skip_group_check=True)
            mask = (before_r, after_r)[d]
            diag = bank.ap[:, 0:3 * P].rearrange("p (b n) -> p b n", b=3)[:, ::2, :]
            done = pe.mark(pe.engine.matmul(diag, ident_r[:, :], mask[:, :].unsqueeze(1).to_broadcast([P, 2, P]),
                                            start=False, stop=True, skip_group_check=True))
            act.wait(done, w_free[i % 2])
            edges = ((0, 2 * P, 0), (2 * P, 3 * P, 1)) if d == 0 else ((0, P, 0), (P, 3 * P, 1))
            for a, b, s in edges:
                m = act.mark(act.engine.activation(wT[:, i % 2, a:b], bank.ap[:, a:b], ACT.Exp, bias=cols2[:, s, 0, r:r + 1]))
            bank.readers = [m]
            return m

        def weigh(h, d, sbank, s_mark, w_mark):
            i = 2 * h + d
            dve.wait(s_mark, w_mark, s_free[i % 2])
            st = sbank.ap[:, :].rearrange("p (s t) -> p s t", s=NT)
            parts = (((0, 2 * P), st[:, 0, 0:T]), ((2 * P, 3 * P), st[:, 1, P:T])) if d == 0 else \
                    (((0, P), st[:, 0, 0:P]), ((P, 3 * P), st[:, 1, 0:T]))
            for (a, b), src in parts:
                m = dve.mark(v.tensor_tensor(sT[:, i % 2, a:b], src, wT[:, i % 2, a:b], ALU.mult))
            w_free[i % 2] = [m]
            return m

        def numerators(h, d, mark):
            i = 2 * h + d
            r = 32 * d + h
            bank = aux_banks[i % 2]
            pe.wait(bank.readers)
            pe.wait(mark, v2_marks)
            blocks = {(0, 0): 0, (1, 1): 2, ((0, 1) if d == 0 else (1, 0)): 1}
            W1 = E2 + 1
            for t in range(NT):
                srcs = [s for s in range(NT) if (s, t) in blocks]
                for n, s in enumerate(srcs):
                    b = blocks[(s, t)]
                    last = pe.engine.matmul(bank.ap[:, t * W1:(t + 1) * W1], sT[:, i % 2, b * P:(b + 1) * P],
                                            vE[:, s, h, :], start=n == 0, stop=n == len(srcs) - 1)
            done = pe.mark(last)
            s_free[i % 2] = [done]
            num = bank.ap[:, 0:NT * W1].rearrange("p (t e) -> p t e", t=NT)
            den = dn[:, i % 4, :]
            dve.wait(done, cols_done)
            chain(v.tensor_reduce(den, num[:, :, E2:E2 + 1], AX.X, ALU.max, apply_absolute_value=True))
            chain(v.tensor_tensor(den, den, expm[:, :, r], ALU.max))
            chain(v.reciprocal(den, den))
            dst = hm[:, :, h * E2:(h + 1) * E2]
            if d == 0:
                m = chain(v.tensor_tensor(dst, num[:, :, 0:E2], den.unsqueeze(2).to_broadcast([P, NT, E2]), ALU.mult))
            else:
                for t in range(NT):
                    m = dve.mark(v.scalar_tensor_tensor(dst[:, t, :], num[:, t, 0:E2], den[:, t:t + 1], dst[:, t, :],
                                                        ALU.mult, ALU.add))
            bank.readers = [m]
            if d == 1:
                for t in range(NT):
                    act.wait(m)
                    squares2.append(act.mark(act.engine.activation(
                        hsq[:, t, h * E2:(h + 1) * E2], hm[:, t, h * E2:(h + 1) * E2], ACT.Square,
                        scale=E2 ** -0.5, accum_out=ms2[:, t * H2 + h:t * H2 + h + 1])))
                pool.wait(squares2[-1], gh_full)
                cols = slice(h * E2, (h + 1) * E2)
                gained.append(pool.mark(pool.engine.tensor_tensor(
                    hm[:, :, cols], hm[:, :, cols], gh[:, cols].unsqueeze(1).to_broadcast([P, NT, E2]), ALU.mult)))

        squares2, gained, ms2 = [], [], columns(NT * H2)
        weighted, decayed, score_banks = {}, {}, {}

        def mlstm_steps():
            heads = [(h, d) for h in range(H2) for d in range(2)]
            for n in range(len(heads) + 2):
                if n < len(heads):
                    h, d = heads[n]
                    if d == 0:
                        score_banks[h] = scores2(h)
                    decayed[n] = decay(h, d)
                if 1 <= n <= len(heads):
                    h, d = heads[n - 1]
                    weighted[n - 1] = weigh(h, d, *score_banks[h], decayed[n - 1])
                    if d == 1:
                        score_banks[h][0].readers = [weighted[n - 1]]
                if n >= 2:
                    numerators(*heads[n - 2], weighted[n - 2])
                yield

        def head_scales():
            dve.wait(*squares2)
            m = dve.mark(v.tensor_scalar(ms2, ms2, NORM_EPS, None, ALU.add))
            pool.wait(m)
            marks["head_scales"] = pool.mark(pool.engine.tensor_tensor(ms2, ms2, minus_half[:, 0:NT * H2], ALU.pow))

        heads_ready, pooled, pool_tail = [[], []], [None, None], {}

        def pooled_half(t):
            ts = slice(t * P, (t + 1) * P)
            act.wait(pool_out, pool_tail[t])
            m = act.mark(act.engine.activation(uT_h[:, H2:H2 + PG, ts], ybT[:, :, ts], ACT.Copy))
            dve.wait(pool_out, m)
            pooled[t] = [m, dve.mark(v.tensor_tensor(uT_l[:, H2:H2 + PG, ts], ybT[:, :, ts],
                                                     uT_h[:, H2:H2 + PG, ts].bitcast(F32), ALU.subtract))]

        steps = mlstm_steps()
        one_step = lambda: next(steps, None)
        for i, (name, c0, n) in enumerate(in2):
            pair = pairs[i % 2] if i < 3 else pairs[1]
            if name == "v2":
                for at in (5, 7):
                    put_off(at, one_step)
            if name == "gu1":
                for at in (1, 3, 5, 7):
                    put_off(at, one_step)
            if name == "o2":
                for at in (1, 2, 4, 6):
                    put_off(at, one_step)
                put_off(7, head_scales)
                for g in range(PG):
                    put_off(1 + g, lambda g=g: pooling_window(g))
                    put_off(3 + g, lambda g=g: pooling_map(g))
                put_off(7, lambda: pooled_half(0))
                put_off(9, lambda: pooled_half(1))
            if name in in2_ada:
                ada(*in2_ada[name], 2 if i == 0 else 0)
            done = run(linear(name, uT_h, uT_l, ready, pair, empty_in2(name, n, pair)))
        ready_y = OutputReady(heads_ready, pooled)

        def gated_residual(name, ready, in_h, in_l, gate, gate_marks, stats, after):
            got = [[], []]

            def empty_into(i):
                def work(t, done):
                    dve.wait(done, gate_marks[i]())
                    m = chain(v.tensor_tensor(xn[:, t, half(i)], pairs[i][t].ap[:, :], gate[:, half(i)], ALU.mult))
                    m = dve.mark(v.tensor_tensor(x[:, t, half(i)], x[:, t, half(i)], xn[:, t, half(i)], ALU.add))
                    got[t].append(square_half(t, i, stats[t], m, pairs[i][t].ap[:, :]))
                    pairs[i][t].readers = [got[t][-1]]
                    last_adds.append(m)
                    if i == 1:
                        after(t, got[t], done)
                return work
            for i in range(2):
                done = run(linear(f"{name}{i}", in_h, in_l, ready, pairs[i], empty_into(i), boundary=i == 1))
            return got, done

        last_adds = []
        stats = [columns(2) for _ in range(NT)]
        ffn2_ready = [[], []]

        def ffn2_norm(t, squares, closed):
            def modulated():
                col, scale_ready = scale_from(stats[t], squares)
                dve.wait(scale_ready, *[ada_done[a] for a in range(6, 10)])
                for h in range(2):
                    y = xn[:, t, half(h)]
                    chain(v.scalar_tensor_tensor(y, x[:, t, half(h)], col, row_f[:, half(h)], ALU.mult, ALU.mult))
                    m = dve.mark(v.tensor_tensor(y, y, row_e[:, half(h)], ALU.add))
                    put_off(turn_steps[t][h], turned(y, t, m, uT_h, uT_l, 4 * h, [closed], ffn2_ready))
            at_boundary(t, modulated)
        squares, done = gated_residual("w_out2_", ready_y, uT_h, uT_l, row_d,
                                       [lambda: ada_done[4], lambda: ada_done[5]], stats, ffn2_norm)
        mix2.close()

        hid2 = ExitStack()
        ctx.enter_context(hid2)
        hid_h = sb("hidden2_high", [P, KF2, T], F32R, stack=hid2)
        hid_l = sb("hidden2_low", [P, KF2, T], F32R, stack=hid2)
        ready = InputReady(ffn2_ready)
        marks["row_d_read"] = last_adds[-1]
        hidden_ready = [[], []]
        for i in range(DFF2 // BANK):
            pair = pairs[i % 2]
            sl = xn[:, :, half(i % 2)]

            def empty_ff1(t, done, i=i, pair=pair, sl=sl):
                act.wait(done)
                m = act.mark(act.engine.activation(sl[:, t, :], pair[t].ap[:, :], ACT.Relu))
                pair[t].readers = [m]
                pool.wait(m)
                m = pool.mark(pool.engine.tensor_tensor(sl[:, t, :], sl[:, t, :], sl[:, t, :], ALU.mult))
                put_off(5, turned(sl[:, t, :], t, m, hid_h, hid_l, 4 * i, [], hidden_ready))
            if i in ff1_ada:
                ada(*ff1_ada[i], 3 if i == 0 else 0)
            run(linear(f"ff1_{i}", uT_h, uT_l, ready, pair, empty_ff1))
        hidden_marks = InputReady(hidden_ready)
        stats = [columns(2) for _ in range(NT)]
        stored = sem("result_stored")

        def final_norm(t, squares, closed):
            col, m = scale_from(stats[t], squares)
            for h in range(2):
                dve.wait(m, marks["g_final_2"])
                done = dve.mark(v.scalar_tensor_tensor(xn[:, t, half(h)], x[:, t, half(h)], col, row_a[:, half(h)],
                                                       ALU.mult, ALU.mult))
                sp.wait(done)
                nc.sync.dma_start(out[0, t * P:(t + 1) * P, half(h)], xn[:, t, half(h)]).then_inc(stored, 16)

        gated_residual("ff2_", hidden_marks, hid_h, hid_l, row_d,
                       [lambda: ada_done[10], lambda: ada_done[11]], stats, final_norm)
        run_later()
        nc.sync.wait_ge(stored, 16 * NT * 2)
        assert W.issued == len(W.slabs) and not later


_NAMES = ["x", "positions", "attn_norm_g", "w_in", "diff_lambda", "diff_subln_g", "cmp_pe_k", "cmp_pe_v", "cmp_k_w1",
          "cmp_k_w2", "cmp_v_w1", "cmp_v_w2", "w_branch_a", "w_branch_b", "w_out", "ffn_norm_g", "w_gate", "w_up",
          "w_down", "final_norm_g", "c_2", "w_ada_2", "b_ada_2", "g_mix_2", "w_in_2", "b_igate_2", "b_fgate_2",
          "g_head_2", "w_pool_2", "pool_scale_2", "w_out_2", "g_ffn_2", "w_ff1_2", "w_ff2_2", "g_final_2"]


def shape_constants(tokens, head_dim):
    import numpy as np
    tile, cmp_len, cmp_stride, theta, windows = 128, 32, 16, 10000.0, (2, 4, 8, 16)
    n_tiles, n_cmp = tokens // tile, (tokens - cmp_len) // cmp_stride + 1
    part, free = np.arange(tile)[:, None], np.arange(tile)[None, :]
    identity = (part == free).astype(np.float32)
    after = np.where(free > part, np.float32(-1e30), np.float32(0))
    before = np.where(free < part, np.float32(-1e30), np.float32(0))
    inv_freq = (1.0 / theta ** (np.arange(0, head_dim, 2, dtype=np.float32) / np.float32(head_dim))).astype(np.float32)
    inv_freq = np.broadcast_to(inv_freq, (tile, head_dim // 2))
    ends = np.arange(n_cmp) * cmp_stride + cmp_len - 1
    t = np.arange(tokens)
    seen = (ends[None, :] <= t[:, None]).reshape(n_tiles, tile, n_cmp).transpose(1, 0, 2).reshape(tile, -1)
    consts = np.concatenate([identity, after, before, inv_freq, np.where(seen, 0, np.float32(-1e30)), seen], 1)
    pool = np.zeros((tokens, len(windows), tokens), np.float32)
    for g, w in enumerate(windows):
        lo, hi = np.clip(t - w // 2, 0, tokens), np.clip(t + w // 2, 0, tokens)
        inside = (t[:, None] >= lo[None, :]) & (t[:, None] < hi[None, :])
        pool[:, g, :] = inside / (hi - lo)[None, :].astype(np.float32) - np.eye(tokens, dtype=np.float32)
    pool = pool.reshape(n_tiles, tile, -1).transpose(1, 0, 2)
    return np.ascontiguousarray(consts, np.float32), np.ascontiguousarray(pool, np.float32)


def kernel(**inputs):
    import numpy as _np
    import concourse.bacc as _bacc
    from concourse.bass_utils import run_bass_kernel_spmd as _run

    nc = _bacc.Bacc("TRN2", target_bir_lowering=False, num_devices=1)
    arrays = {name: _np.ascontiguousarray(inputs[name]) for name in _NAMES}
    arrays["consts"], arrays["pool_matrix"] = shape_constants(inputs["x"].shape[1], inputs["diff_lambda"].shape[2])
    io = {name: nc.dram_tensor(f"in_{name}", a.shape, mybir.dt.from_np(a.dtype), kind="ExternalInput").ap()
          for name, a in arrays.items()}
    shape = tuple(inputs["x"].shape)
    out = nc.dram_tensor("out", shape, F32, kind="ExternalOutput").ap()
    build(nc, io, out)
    result = _run(nc, [{f"in_{name}": a for name, a in arrays.items()}], core_ids=[0])
    return result.results[0]["out"]
```
